# Optimizing a Trainium2 kernel written in Bass

```python
import math
import jax
import jax.numpy as jnp
from jax import lax
import numpy as np
import jax, jax.numpy as jnp

D_MODEL = 1024
BATCH = 1
SEQ = 256
DEPTH = 2

N_MIXERS = 2
POOL_WINDOWS = (2, 4, 8, 16)
N_POOL_GROUPS = len(POOL_WINDOWS)
POOL_GROUP_DIM = D_MODEL // N_POOL_GROUPS
HEAD_DIM = 64
N_HEADS = D_MODEL // HEAD_DIM
DIL_CONFIGS = ((128, 1), (512, 4), (2048, 16))
N_DIL_GROUPS = len(DIL_CONFIGS)
ATTN_WIDTH = N_HEADS * HEAD_DIM
QKV_WIDTH = N_DIL_GROUPS * 3 * ATTN_WIDTH
D_FF = 2816
MACARON_WEIGHT = 0.5
ALPHA = (2.0 * DEPTH) ** 0.25
BETA = (8.0 * DEPTH) ** -0.25
LN_EPS = 1e-5
MASK_VALUE = -1e30


def _alibi_slopes():
    n = N_DIL_GROUPS * N_HEADS
    s = 2.0 ** (-8.0 * np.arange(1, n + 1) / n)
    return s.reshape(N_DIL_GROUPS, N_HEADS).astype(np.float32)

def _layer_norm(x, g, b):
    x32 = x.astype(jnp.float32)
    mu = jnp.mean(x32, axis=-1, keepdims=True)
    var = jnp.mean(jnp.square(x32 - mu), axis=-1, keepdims=True)
    y = (x32 - mu) * lax.rsqrt(var + LN_EPS)
    return (y * g.astype(jnp.float32) + b.astype(jnp.float32)).astype(x.dtype)

def _swiglu(x, w_gate, w_up, w_down):
    return (jax.nn.silu(x @ w_gate) * (x @ w_up)) @ w_down

def _pool_mixer(x, w_in, w_group, scale, w_out):
    B, S, _ = x.shape
    u = (x @ w_in).reshape(B, S, N_POOL_GROUPS, POOL_GROUP_DIM).astype(jnp.float32)
    csum = jnp.concatenate([jnp.zeros_like(u[:, :1]), jnp.cumsum(u, axis=1)], axis=1)
    half = jnp.asarray([w // 2 for w in POOL_WINDOWS], dtype=jnp.int32)
    t = jnp.arange(S, dtype=jnp.int32)[:, None]
    lo = jnp.clip(t - half[None, :], 0, S)
    hi = jnp.clip(t + half[None, :], 0, S)
    gidx = jnp.arange(N_POOL_GROUPS)[None, :]
    win_sum = csum[:, hi, gidx] - csum[:, lo, gidx]
    mean = win_sum / (hi - lo).astype(jnp.float32)[None, :, :, None]
    mixed = (mean - u).astype(x.dtype)
    y = jnp.einsum('bsgc,gce->bsge', mixed, w_group).reshape(B, S, D_MODEL) * scale
    return y @ w_out

def _dilated_group(q, k, v, window, dilation, slopes):
    B, S, H, E = q.shape
    d = dilation
    L = S // d
    R = window // (2 * d)
    W = R
    nb = -(-L // W)
    Lp = nb * W

    def to_sub(a):
        return a.reshape(B, L, d, H, E).transpose(0, 2, 3, 1, 4)

    qs = jnp.pad(to_sub(q), ((0, 0),) * 3 + ((0, Lp - L), (0, 0))).reshape(B, d, H, nb, W, E)

    def windows(a):
        ap = jnp.pad(to_sub(a), ((0, 0),) * 3 + ((W, W + Lp - L), (0, 0)))
        ap = ap.reshape(B, d, H, nb + 2, W, E)
        return jnp.concatenate([ap[:, :, :, :-2], ap[:, :, :, 1:-1], ap[:, :, :, 2:]], axis=4)

    kw = windows(k)
    vw = windows(v)
    a_idx = jnp.arange(W)
    c_idx = jnp.arange(3 * W)
    n_idx = jnp.arange(nb)
    rel = c_idx[None, :] - W - a_idx[:, None]
    j = (n_idx[:, None, None] - 1) * W + c_idx[None, None, :]
    valid = (jnp.abs(rel)[None] <= R) & (j >= 0) & (j < L)
    dist = (d * jnp.abs(rel)).astype(jnp.float32)
    bias = -slopes[:, None, None] * dist[None]
    scores = jnp.einsum('bdhnqe,bdhnke->bdhnqk', qs.astype(jnp.float32),
                        kw.astype(jnp.float32)) * (E ** -0.5) + bias[:, None]
    scores = jnp.where(valid, scores, MASK_VALUE)
    lse = jax.nn.logsumexp(scores, axis=-1)
    p = jnp.exp(scores - lse[..., None])
    o = jnp.einsum('bdhnqk,bdhnke->bdhnqe', p, vw.astype(jnp.float32))
    o = o.reshape(B, d, H, Lp, E)[:, :, :, :L].transpose(0, 3, 1, 2, 4).reshape(B, S, H, E)
    lse = lse.reshape(B, d, H, Lp)[..., :L].transpose(0, 3, 1, 2).reshape(B, S, H)
    return o, lse

def _dilated_attention_mixer(x, w_qkv, w_out):
    B, S, _ = x.shape
    qkv = (x @ w_qkv).reshape(B, S, N_DIL_GROUPS, 3, N_HEADS, HEAD_DIM)
    slopes = jnp.asarray(_alibi_slopes())
    outs, lses = [], []
    for g, (window, dil) in enumerate(DIL_CONFIGS):
        o, l = _dilated_group(qkv[:, :, g, 0], qkv[:, :, g, 1], qkv[:, :, g, 2],
                              window, dil, slopes[g])
        outs.append(o)
        lses.append(l)
    wts = jax.nn.softmax(jnp.stack(lses), axis=0)
    o = jnp.sum(wts[..., None] * jnp.stack(outs), axis=0)
    return o.reshape(B, S, ATTN_WIDTH).astype(x.dtype) @ w_out

def first_inputs(seed: int = 0) -> dict:
    key = jax.random.key(seed)
    ks = jax.random.split(key, 16)
    n_pool = (DEPTH + 1) // 2
    n_attn = DEPTH // 2
    f32 = jnp.float32

    def nrm(k, shape, scale):
        return jax.random.normal(k, shape, f32) * scale

    return {
        "x": jax.random.normal(ks[0], (BATCH, SEQ, D_MODEL), f32),
        "ffn1_w_gate": nrm(ks[1], (DEPTH, D_MODEL, D_FF), D_MODEL ** -0.5),
        "ffn1_w_up": nrm(ks[2], (DEPTH, D_MODEL, D_FF), D_MODEL ** -0.5),
        "ffn1_w_down": nrm(ks[3], (DEPTH, D_FF, D_MODEL), BETA * D_FF ** -0.5),
        "ffn2_w_gate": nrm(ks[4], (DEPTH, D_MODEL, D_FF), D_MODEL ** -0.5),
        "ffn2_w_up": nrm(ks[5], (DEPTH, D_MODEL, D_FF), D_MODEL ** -0.5),
        "ffn2_w_down": nrm(ks[6], (DEPTH, D_FF, D_MODEL), BETA * D_FF ** -0.5),
        "ln_gain": 1.0 + nrm(ks[7], (DEPTH, 3, D_MODEL), 0.02),
        "ln_bias": nrm(ks[8], (DEPTH, 3, D_MODEL), 0.02),
        "pool_w_in": nrm(ks[9], (n_pool, D_MODEL, D_MODEL), D_MODEL ** -0.5),
        "pool_w_group": nrm(ks[10], (n_pool, N_POOL_GROUPS, POOL_GROUP_DIM, POOL_GROUP_DIM),
                            POOL_GROUP_DIM ** -0.5),
        "pool_scale": 1.0 + nrm(ks[11], (n_pool, D_MODEL), 0.1),
        "pool_w_out": nrm(ks[12], (n_pool, D_MODEL, D_MODEL), BETA * D_MODEL ** -0.5),
        "attn_w_qkv": nrm(ks[13], (n_attn, D_MODEL, QKV_WIDTH), D_MODEL ** -0.5),
        "attn_w_out": nrm(ks[14], (n_attn, ATTN_WIDTH, D_MODEL), BETA * ATTN_WIDTH ** -0.5),
    }

def first_block(x, ffn1_w_gate, ffn1_w_up, ffn1_w_down, ffn2_w_gate, ffn2_w_up, ffn2_w_down,
              ln_gain, ln_bias, pool_w_in, pool_w_group, pool_scale, pool_w_out,
              attn_w_qkv, attn_w_out):
    for i in range(DEPTH):
        h = _swiglu(x, ffn1_w_gate[i], ffn1_w_up[i], ffn1_w_down[i])
        x = _layer_norm(ALPHA * x + MACARON_WEIGHT * h, ln_gain[i, 0], ln_bias[i, 0])
        if i % N_MIXERS == 0:
            p = i // N_MIXERS
            m = _pool_mixer(x, pool_w_in[p], pool_w_group[p], pool_scale[p], pool_w_out[p])
        else:
            a = i // N_MIXERS
            m = _dilated_attention_mixer(x, attn_w_qkv[a], attn_w_out[a])
        x = _layer_norm(ALPHA * x + m, ln_gain[i, 1], ln_bias[i, 1])
        h = _swiglu(x, ffn2_w_gate[i], ffn2_w_up[i], ffn2_w_down[i])
        x = _layer_norm(ALPHA * x + MACARON_WEIGHT * h, ln_gain[i, 2], ln_bias[i, 2])
    return x


CTX_LEN = 256
GRID_W = 64
EPS = 1e-6
N_MOD = 9

FNET_GROUPS = 4
FNET_GROUP_DIM = 128
FNET_DIM = FNET_GROUPS * FNET_GROUP_DIM
NA_HEADS = 8
NA_HEAD_DIM = 64
NA_DIM = NA_HEADS * NA_HEAD_DIM
NA_KH = 8
NA_KW = 16
AB_IN_DIM = FNET_DIM + 3 * NA_DIM
AB_OUT_DIM = FNET_DIM + NA_DIM
MLA_HEADS = 8
MLA_NOPE = 128
MLA_ROPE = 64
MLA_V = 128
MLA_Q_RANK = 384
MLA_KV_RANK = 128
MLA_IN_DIM = MLA_Q_RANK + MLA_KV_RANK + MLA_ROPE
ROPE_BASE = 10000.0
Q_BLOCK = 128

N_EVEN = (DEPTH + 1) // 2
N_ODD = DEPTH // 2


def rmsnorm(x, g):
    xf = x.astype(jnp.float32)
    y = xf * lax.rsqrt(jnp.mean(xf * xf, axis=-1, keepdims=True) + EPS)
    return (y * g.astype(jnp.float32)).astype(x.dtype)

def swiglu(h, w_gate, w_up, w_down):
    return (jax.nn.silu(h @ w_gate) * (h @ w_up)) @ w_down

def half_ffn(x, shift, scale, gate, g, w_gate, w_up, w_down):
    h = rmsnorm(x, g) * (1 + scale) + shift
    return x + 0.5 * gate * swiglu(h, w_gate, w_up, w_down)

def axial_rope_tables(n_tok, rot_dim):
    pos = jnp.arange(n_tok)
    row = (pos // GRID_W).astype(jnp.float32)
    col = (pos % GRID_W).astype(jnp.float32)
    half = rot_dim // 2
    inv = ROPE_BASE ** (-jnp.arange(0, half, 2, dtype=jnp.float32) / half)
    ang_r = row[:, None] * inv[None]
    ang_c = col[:, None] * inv[None]
    ang = jnp.concatenate([ang_r, ang_r, ang_c, ang_c], axis=-1)
    return jnp.cos(ang), jnp.sin(ang)

def apply_axial_rope(x, cos, sin):
    xf = x.astype(jnp.float32)
    a, b, cc, d = jnp.split(xf, 4, axis=-1)
    rot = jnp.concatenate([-b, a, -d, cc], axis=-1)
    return (xf * cos + rot * sin).astype(x.dtype)

def fourier_mix(u):
    b, n, _ = u.shape
    ug = u.astype(jnp.float32).reshape(b, n, FNET_GROUPS, FNET_GROUP_DIM)
    f = jnp.fft.fft2(ug, axes=(1, 3), norm="ortho").real
    return f.reshape(b, n, FNET_DIM).astype(u.dtype)

def dense_attention(q, k, v):
    s = jnp.einsum('bqhd,bkhd->bhqk', q, k, preferred_element_type=jnp.float32) * (q.shape[-1] ** -0.5)
    p = jax.nn.softmax(s, axis=-1).astype(v.dtype)
    return jnp.einsum('bhqk,bkhd->bqhd', p, v)

def neighbourhood_attention(q, k, v, k_ctx, v_ctx, rpb):
    b, s, h, dh = q.shape
    rows = s // GRID_W
    kh = min(NA_KH, rows)
    kw = NA_KW
    scale = dh ** -0.5
    qg = q.reshape(b, rows, GRID_W, h, dh)
    kg = k.reshape(b, rows, GRID_W, h, dh)
    vg = v.reshape(b, rows, GRID_W, h, dh)
    cols = jnp.arange(GRID_W)
    col_start = jnp.clip(cols - kw // 2, 0, GRID_W - kw)
    col_idx = col_start[:, None] + jnp.arange(kw)[None, :]
    col_off = col_idx - cols[:, None] + (NA_KW - 1)

    def one_row(r):
        r0 = jnp.clip(r - kh // 2, 0, rows - kh)
        row_off = r0 + jnp.arange(kh) - r + (NA_KH - 1)
        k_band = lax.dynamic_slice_in_dim(kg, r0, kh, axis=1)
        v_band = lax.dynamic_slice_in_dim(vg, r0, kh, axis=1)
        k_win = k_band[:, :, col_idx]
        v_win = v_band[:, :, col_idx]
        qr = lax.dynamic_index_in_dim(qg, r, axis=1, keepdims=False)
        bias = rpb[:, row_off[:, None, None], col_off[None, :, :]]
        bias = jnp.transpose(bias, (0, 2, 1, 3)).reshape(h, GRID_W, kh * kw).astype(jnp.float32)
        s_win = jnp.einsum('bqhd,biqjhd->bhqij', qr, k_win, preferred_element_type=jnp.float32)
        s_win = s_win.reshape(b, h, GRID_W, kh * kw) * scale + bias[None]
        s_ctx = jnp.einsum('bqhd,blhd->bhql', qr, k_ctx, preferred_element_type=jnp.float32) * scale
        p = jax.nn.softmax(jnp.concatenate([s_win, s_ctx], axis=-1), axis=-1).astype(v.dtype)
        p_win = p[..., :kh * kw].reshape(b, h, GRID_W, kh, kw)
        p_ctx = p[..., kh * kw:]
        return (jnp.einsum('bhqij,biqjhd->bqhd', p_win, v_win)
                + jnp.einsum('bhql,blhd->bqhd', p_ctx, v_ctx))

    o = lax.map(one_row, jnp.arange(rows))
    return jnp.transpose(o, (1, 0, 2, 3, 4)).reshape(b, s, h * dh)

def fourier_na_mixer(h_lat, h_ctx, w_in, rpb, w_out, need_ctx_out):
    def split(z):
        u = z[..., :FNET_DIM]
        qkv = z[..., FNET_DIM:].reshape(z.shape[0], z.shape[1], 3, NA_HEADS, NA_HEAD_DIM)
        return u, qkv[:, :, 0], qkv[:, :, 1], qkv[:, :, 2]

    u_l, q_l, k_l, v_l = split(h_lat @ w_in)
    u_c, q_c, k_c, v_c = split(h_ctx @ w_in)
    a_l = fourier_mix(u_l)
    b_l = neighbourhood_attention(q_l, k_l, v_l, k_c, v_c, rpb)
    y_lat = jnp.concatenate([a_l, b_l], axis=-1) @ w_out
    if not need_ctx_out:
        return y_lat, None
    a_c = fourier_mix(u_c)
    b_c = dense_attention(q_c, k_c, v_c).reshape(h_ctx.shape[0], h_ctx.shape[1], NA_DIM)
    y_ctx = jnp.concatenate([a_c, b_c], axis=-1) @ w_out
    return y_lat, y_ctx

def mla_block_attention(q_nope, q_rope, k_nope, k_rope, v):
    b, n, h, _ = q_nope.shape
    nb = n // Q_BLOCK
    scale = (MLA_NOPE + MLA_ROPE) ** -0.5
    qn = q_nope.reshape(b, nb, Q_BLOCK, h, MLA_NOPE).swapaxes(0, 1)
    qr = q_rope.reshape(b, nb, Q_BLOCK, h, MLA_ROPE).swapaxes(0, 1)

    def one_block(args):
        qn_b, qr_b = args
        s = (jnp.einsum('bqhd,bkhd->bhqk', qn_b, k_nope, preferred_element_type=jnp.float32)
             + jnp.einsum('bqhr,bkr->bhqk', qr_b, k_rope, preferred_element_type=jnp.float32)) * scale
        p = jax.nn.softmax(s, axis=-1).astype(v.dtype)
        return jnp.einsum('bhqk,bkhd->bqhd', p, v)

    o = lax.map(one_block, (qn, qr))
    return o.swapaxes(0, 1).reshape(b, n, h * MLA_V)

def mla_mixer(h_lat, h_ctx, w_in, g_q, g_kv, w_uq, w_uk, w_uv, w_o, cos, sin, need_ctx_out):
    def project(hh):
        bb, nn = hh.shape[0], hh.shape[1]
        z = hh @ w_in
        c_q = rmsnorm(z[..., :MLA_Q_RANK], g_q)
        c_kv = rmsnorm(z[..., MLA_Q_RANK:MLA_Q_RANK + MLA_KV_RANK], g_kv)
        k_rope = z[..., MLA_Q_RANK + MLA_KV_RANK:]
        q = (c_q @ w_uq).reshape(bb, nn, MLA_HEADS, MLA_NOPE + MLA_ROPE)
        k_nope = (c_kv @ w_uk).reshape(bb, nn, MLA_HEADS, MLA_NOPE)
        v = (c_kv @ w_uv).reshape(bb, nn, MLA_HEADS, MLA_V)
        return q[..., :MLA_NOPE], q[..., MLA_NOPE:], k_nope, k_rope, v

    qn_l, qr_l, kn_l, kr_l, v_l = project(h_lat)
    qn_c, qr_c, kn_c, kr_c, v_c = project(h_ctx)
    qr_l = apply_axial_rope(qr_l, cos[:, None, :], sin[:, None, :])
    kr_l = apply_axial_rope(kr_l, cos, sin)
    kn_all = jnp.concatenate([kn_l, kn_c], axis=1)
    kr_all = jnp.concatenate([kr_l, kr_c], axis=1)
    v_all = jnp.concatenate([v_l, v_c], axis=1)
    y_lat = mla_block_attention(qn_l, qr_l, kn_all, kr_all, v_all) @ w_o
    if not need_ctx_out:
        return y_lat, None
    y_ctx = mla_block_attention(qn_c, qr_c, kn_c, kr_c, v_c) @ w_o
    return y_lat, y_ctx

def second_inputs(seed: int = 0) -> dict:
    key = jax.random.key(seed)
    ks = jax.random.split(key, 24)
    f32 = jnp.float32

    def nrm(k, shape, std):
        return jax.random.normal(k, shape, f32) * std

    return {
        "x": nrm(ks[0], (BATCH, SEQ, D_MODEL), 1.0),
        "c": nrm(ks[1], (BATCH, D_MODEL), 1.0),
        "ctx": nrm(ks[2], (BATCH, CTX_LEN, D_MODEL), 1.0),
        "c_ctx": nrm(ks[3], (D_MODEL,), 1.0),
        "ada_w": nrm(ks[4], (DEPTH, D_MODEL, N_MOD * D_MODEL), 0.5 * D_MODEL ** -0.5),
        "ada_b": nrm(ks[5], (DEPTH, N_MOD * D_MODEL), 0.02),
        "norm_g": 1.0 + nrm(ks[6], (DEPTH, 3, D_MODEL), 0.02),
        "ffn_w_gate": nrm(ks[7], (DEPTH, 2, D_MODEL, D_FF), D_MODEL ** -0.5),
        "ffn_w_up": nrm(ks[8], (DEPTH, 2, D_MODEL, D_FF), D_MODEL ** -0.5),
        "ffn_w_down": nrm(ks[9], (DEPTH, 2, D_FF, D_MODEL), D_FF ** -0.5),
        "ab_w_in": nrm(ks[10], (N_EVEN, D_MODEL, AB_IN_DIM), D_MODEL ** -0.5),
        "ab_rpb": nrm(ks[11], (N_EVEN, NA_HEADS, 2 * NA_KH - 1, 2 * NA_KW - 1), 0.1),
        "ab_w_out": nrm(ks[12], (N_EVEN, AB_OUT_DIM, D_MODEL), AB_OUT_DIM ** -0.5),
        "mla_w_in": nrm(ks[13], (N_ODD, D_MODEL, MLA_IN_DIM), D_MODEL ** -0.5),
        "mla_g_q": 1.0 + nrm(ks[14], (N_ODD, MLA_Q_RANK), 0.02),
        "mla_g_kv": 1.0 + nrm(ks[15], (N_ODD, MLA_KV_RANK), 0.02),
        "mla_w_uq": nrm(ks[16], (N_ODD, MLA_Q_RANK, MLA_HEADS * (MLA_NOPE + MLA_ROPE)), MLA_Q_RANK ** -0.5),
        "mla_w_uk": nrm(ks[17], (N_ODD, MLA_KV_RANK, MLA_HEADS * MLA_NOPE), MLA_KV_RANK ** -0.5),
        "mla_w_uv": nrm(ks[18], (N_ODD, MLA_KV_RANK, MLA_HEADS * MLA_V), MLA_KV_RANK ** -0.5),
        "mla_w_o": nrm(ks[19], (N_ODD, MLA_HEADS * MLA_V, D_MODEL), (MLA_HEADS * MLA_V) ** -0.5),
        "final_g": 1.0 + nrm(ks[20], (D_MODEL,), 0.02),
    }

def second_block(x, c, ctx, c_ctx, ada_w, ada_b, norm_g, ffn_w_gate, ffn_w_up, ffn_w_down,
              ab_w_in, ab_rpb, ab_w_out, mla_w_in, mla_g_q, mla_g_kv, mla_w_uq, mla_w_uk,
              mla_w_uv, mla_w_o, final_g):
    n_lat = x.shape[1]
    cos, sin = axial_rope_tables(n_lat, MLA_ROPE)
    sc = jax.nn.silu(c)
    scc = jax.nn.silu(c_ctx)
    x_l, x_c = x, ctx
    for layer in range(DEPTH):
        last = layer == DEPTH - 1
        mod_l = (sc @ ada_w[layer] + ada_b[layer]).reshape(-1, N_MOD, D_MODEL)[:, :, None, :]
        mod_c = (scc @ ada_w[layer] + ada_b[layer]).reshape(N_MOD, D_MODEL)

        x_l = half_ffn(x_l, mod_l[:, 0], mod_l[:, 1], mod_l[:, 2], norm_g[layer, 0],
                       ffn_w_gate[layer, 0], ffn_w_up[layer, 0], ffn_w_down[layer, 0])
        x_c = half_ffn(x_c, mod_c[0], mod_c[1], mod_c[2], norm_g[layer, 0],
                       ffn_w_gate[layer, 0], ffn_w_up[layer, 0], ffn_w_down[layer, 0])

        h_l = rmsnorm(x_l, norm_g[layer, 1]) * (1 + mod_l[:, 4]) + mod_l[:, 3]
        h_c = rmsnorm(x_c, norm_g[layer, 1]) * (1 + mod_c[4]) + mod_c[3]
        i = layer // 2
        if layer % 2 == 0:
            y_l, y_c = fourier_na_mixer(h_l, h_c, ab_w_in[i], ab_rpb[i], ab_w_out[i], not last)
        else:
            y_l, y_c = mla_mixer(h_l, h_c, mla_w_in[i], mla_g_q[i], mla_g_kv[i], mla_w_uq[i],
                                 mla_w_uk[i], mla_w_uv[i], mla_w_o[i], cos, sin, not last)
        x_l = x_l + mod_l[:, 5] * y_l

        x_l = half_ffn(x_l, mod_l[:, 6], mod_l[:, 7], mod_l[:, 8], norm_g[layer, 2],
                       ffn_w_gate[layer, 1], ffn_w_up[layer, 1], ffn_w_down[layer, 1])
        if not last:
            x_c = x_c + mod_c[5] * y_c
            x_c = half_ffn(x_c, mod_c[6], mod_c[7], mod_c[8], norm_g[layer, 2],
                           ffn_w_gate[layer, 1], ffn_w_up[layer, 1], ffn_w_down[layer, 1])
    return rmsnorm(x_l, final_g)


def setup_inputs(seed=0):
    out = dict(first_inputs(seed))
    for name, value in second_inputs(seed + 1).items():
        if name != "x":
            out[name + "_2"] = value
    return out


def reference(
    x, ffn1_w_gate, ffn1_w_up, ffn1_w_down, ffn2_w_gate, ffn2_w_up, ffn2_w_down, ln_gain,
    ln_bias, pool_w_in, pool_w_group, pool_scale, pool_w_out, attn_w_qkv, attn_w_out, c_2,
    ctx_2, c_ctx_2, ada_w_2, ada_b_2, norm_g_2, ffn_w_gate_2, ffn_w_up_2, ffn_w_down_2,
    ab_w_in_2, ab_rpb_2, ab_w_out_2, mla_w_in_2, mla_g_q_2, mla_g_kv_2, mla_w_uq_2, mla_w_uk_2,
    mla_w_uv_2, mla_w_o_2, final_g_2,
):
    x = first_block(
        x, ffn1_w_gate, ffn1_w_up, ffn1_w_down, ffn2_w_gate, ffn2_w_up, ffn2_w_down, ln_gain,
        ln_bias, pool_w_in, pool_w_group, pool_scale, pool_w_out, attn_w_qkv, attn_w_out,
    )
    return second_block(
        x, c_2, ctx_2, c_ctx_2, ada_w_2, ada_b_2, norm_g_2, ffn_w_gate_2, ffn_w_up_2,
        ffn_w_down_2, ab_w_in_2, ab_rpb_2, ab_w_out_2, mla_w_in_2, mla_g_q_2, mla_g_kv_2,
        mla_w_uq_2, mla_w_uk_2, mla_w_uv_2, mla_w_o_2, final_g_2,
    )


_drawn_inputs = setup_inputs


def setup_inputs(seed=0):
    import zlib

    import numpy as np

    out = dict(_drawn_inputs(seed))
    spreads = {}
    factors = {'norm_g_2': 8.0,
     'ab_rpb_2': 8.0,
     'mla_g_q_2': 8.0,
     'mla_g_kv_2': 24.094,
     'final_g_2': 7.884}
    for name, (base, spread) in spreads.items():
        noise = np.random.default_rng([zlib.crc32(name.encode()), seed]).standard_normal(out[name].shape)
        drawn = base * np.exp(spread * noise) if base else spread * noise
        out[name] = jnp.asarray(drawn.astype(out[name].dtype))
    for name, factor in factors.items():
        out[name] = (out[name] * factor).astype(out[name].dtype)
    return out
```

```python
from contextlib import ExitStack

import numpy as np

import concourse.bass as bass
from concourse import mybir

F32 = mybir.dt.float32
F32R = mybir.dt.float32r
ALU = mybir.AluOpType
ACT = mybir.ActivationFunctionType
AX_X = mybir.AxisListType.X

P = 128
S = 256
D = 1024
DC = D // P
F = 2816
FC = F // P
DEPTH = 2
ALPHA = (2.0 * DEPTH) ** 0.25
LN_EPS = 1e-5
RMS_EPS = 1e-6
HEAD = 64
HEADS = 16
DIL_GROUPS = 3
NA_HEADS = 8
MLA_HEADS = 8
NOPE = 128
ROPE = 64
Q_RANK = 384
N_MOD = 9
MODC = N_MOD * DC
GRID_W = 64
GRID_H = S // GRID_W
RPB_H, RPB_W = 15, 31
UNIT = 2048
RAW_SLOTS = 3
SPLIT_SLOTS = 3
H_CHUNKS = 24
FAR = 1e32


class Engine:

    def __init__(self, sem):
        self.sem, self.count, self.queue, self.seen = sem, 0, [], {}

    def wait(self, *marks):
        for mark in marks:
            if isinstance(mark, list):
                self.wait(*mark)
            elif mark is not None and self.seen.get(mark[0].name, 0) < mark[1]:
                self.seen[mark[0].name] = mark[1]
                self.queue.append(lambda e, m=mark: e.wait_ge(m[0], m[1]))

    def run(self, op, *marks):
        self.wait(*marks)
        self.count += 1
        self.queue.append(lambda e: op(e).then_inc(self.sem, 1))
        return (self.sem, self.count)

    def quiet(self, op, *marks):
        self.wait(*marks)
        self.queue.append(op)

    def dma(self, out, in_, slot, *marks):
        self.wait(*marks)
        slot[1] += 16
        self.queue.append(lambda e: e.dma_start(out, in_).then_inc(slot[0], 16))
        return (slot[0], slot[1])

    def play(self, e):
        for op in self.queue:
            op(e)


def build_program(nc, a, out):
    with ExitStack() as ctx:
        place = [nc.sbuf_base + (-nc.sbuf_base) % 64]

        def at(name, shape, dtype, offset):
            return nc.alloc_sbuf_tensor_at(name, shape, dtype, offset=offset)

        def room(nbytes):
            here = place[0]
            place[0] += nbytes + (-nbytes) % 64
            assert place[0] <= nc.sbuf_usable_end, (place, nc.sbuf_usable_end)
            return here

        def sb(name, shape, dtype=F32):
            return at(name, shape, dtype, room(4 * int(np.prod(shape[1:]))))

        m = {}
        m["x"] = sb("x", [P, DC, 2 * S])
        m["in_hi"] = sb("in_hi", [P, DC, 2 * S], F32R)
        m["in_lo"] = sb("in_lo", [P, DC, 2 * S], F32R)
        base = room(4 * 2 * H_CHUNKS * S)
        m["h_hi"] = at("h_hi", [P, H_CHUNKS * S], F32R, base)
        m["h_lo"] = at("h_lo", [P, H_CHUNKS * S], F32R, base + 4 * H_CHUNKS * S)
        m["work"] = at("work", [P, 2 * H_CHUNKS * S], F32, base)
        m["raw"] = [sb(f"raw{i}", [P, UNIT]) for i in range(RAW_SLOTS)]
        m["hi"] = [sb(f"hi{i}", [P, UNIT], F32R) for i in range(SPLIT_SLOTS)]
        m["lo"] = [sb(f"lo{i}", [P, UNIT], F32R) for i in range(SPLIT_SLOTS)]
        base = room(4 * DC * 2 * S)
        m["tmp"] = at("tmp", [P, DC * 2 * S], F32, base)
        m["latent"] = at("latent", [P, 2560], F32R, base + 4 * 1536)
        m["const"] = sb("const", [P, 2048])
        m["ident"] = sb("ident", [P, P])
        m["mean_w"] = sb("mean_w", [P, P])
        m["stat"] = sb("stat", [P, 4, 2 * S])
        m["cols"] = sb("cols", [P, 512])
        m["mod"] = sb("mod", [P, DEPTH, MODC, 2])
        m["gain"] = sb("gain", [P, DC, 2])
        m["c_split"] = sb("c_split", [P, DC, 4], F32R)
        m["c_silu"] = sb("c_silu", [P, DC, 2])
        m["soft"] = sb("soft", [P, 4, 4])
        m["ada_row"] = sb("ada_row", [4, 512])
        m["banks"] = [ctx.enter_context(nc.psum_tensor(f"bank{i}", [P, 512], F32)) for i in range(8)]

        names = "pe act dve pool sync".split()
        sems = {n: ctx.enter_context(nc.semaphore(f"{n}_done")) for n in names}
        for i in range(RAW_SLOTS):
            sems[f"raw{i}"] = ctx.enter_context(nc.semaphore(f"raw{i}_landed"))
        for n in ("consts", "rows", "tokens", "table", "table2", "rpb", "bias", "out"):
            sems[n] = ctx.enter_context(nc.semaphore(f"{n}_landed"))

        plan = []
        Program(nc, a, out, m, sems, plan, True).emit()
        program = Program(nc, a, out, m, sems, plan, False)
        program.emit()

        block = ctx.enter_context(nc.Block())
        block.sync(program.sync.play)
        block.gpsimd(program.pool.play)
        block.scalar(program.act.play)
        block.vector(program.dve.play)
        block.tensor(program.pe.play)


class Program:
    def __init__(self, nc, a, out, m, sems, plan, dry):
        self.nc, self.a, self.out, self.m, self.plan, self.dry = nc, a, out, m, plan, dry
        self.pe, self.act, self.dve, self.pool, self.sync = (
            Engine(sems[n]) for n in ("pe", "act", "dve", "pool", "sync"))
        self.slot = {n: [sems[n], 0] for n in sems}
        self.loaded = self.split = self.taken = 0
        self.raw_landed, self.hi_done, self.lo_done, self.used = {}, {}, {}, {}
        self.next_bank, self.bank_free = 0, [None] * 8
        self.ada_blocks, self.ada_pending = [], None
        self.x_ready = [None] * (2 * DC)
        self.in_ready = []
        self.in_read = None
        self.h_read = None
        self.tmp_read = []
        self.stat_read = []

    def load_unit(self, i):
        parts, A, B = self.plan[i]
        before = i - RAW_SLOTS
        marks = [self.hi_done[before], self.lo_done[before]] if before >= 0 else []
        for first, src in parts:
            n = src.shape[1] * src.shape[2]
            dst = self.m["raw"][i % RAW_SLOTS][:, first:first + n].rearrange("p (a b) -> p a b", b=src.shape[2])
            self.raw_landed[i] = self.sync.dma(dst, src, self.slot[f"raw{i % RAW_SLOTS}"], *marks)

    def split_unit(self, i):
        _, A, B = self.plan[i]
        n, s = A * B, i % SPLIT_SLOTS
        raw, hi, lo = self.m["raw"][i % RAW_SLOTS], self.m["hi"][s], self.m["lo"][s]
        before = self.used[i - SPLIT_SLOTS] if i >= SPLIT_SLOTS else None
        self.hi_done[i] = self.act.run(
            lambda e: e.activation(hi[:, 0:n], raw[:, 0:n], ACT.Copy), self.raw_landed[i], before)
        self.lo_done[i] = self.dve.run(
            lambda e: e.tensor_tensor(lo[:, 0:n], raw[:, 0:n], hi[:, 0:n].bitcast(F32), ALU.subtract),
            self.raw_landed[i], self.hi_done[i], before)

    def weights(self, src, parts=None):
        A, B = src.shape[1], src.shape[2]
        assert A * B <= UNIT and src.shape[0] == P
        i = self.taken
        self.taken += 1
        if self.dry:
            self.plan.append((parts or [(0, src)], A, B))
        else:
            assert self.plan[i][1:] == (A, B)
            while self.split < min(i + SPLIT_SLOTS, len(self.plan)):
                while self.loaded < min(self.split + RAW_SLOTS, len(self.plan)):
                    self.load_unit(self.loaded)
                    self.loaded += 1
                self.split_unit(self.split)
                self.split += 1
            self.pe.wait(self.hi_done[i], self.lo_done[i])
        s = i % SPLIT_SLOTS
        hi, lo = (self.m[k][s][:, 0:A * B].rearrange("p (a b) -> p a b", a=A) for k in ("hi", "lo"))
        return i, hi, lo

    def bank(self):
        b = self.next_bank
        self.next_bank = (b + 1) % 8
        assert self.bank_free[b] != "held"
        self.pe.wait(self.bank_free[b])
        self.bank_free[b] = "held"
        return b, self.m["banks"][b]

    def mm(self, out, lhs, rhs, start=True, stop=True, mark=False):
        op = lambda e: e.matmul(out, lhs, rhs, start=start, stop=stop)
        return self.pe.run(op) if mark else self.pe.quiet(op)

    def mm3(self, out, w, x, start, stop, mark=False):
        self.mm(out, w[0], x[0], start=start, stop=False)
        self.mm(out, w[0], x[1], start=False, stop=False)
        return self.mm(out, w[1], x[0], start=False, stop=stop, mark=mark)

    def transpose(self, out, in_, mark=False):
        n = in_.shape[0]
        op = lambda e: e.transpose(out, in_, self.m["ident"][0:n, 0:n])
        return self.pe.run(op) if mark else self.pe.quiet(op)

    def project(self, w_dram, n_out, x, N, evacuate):
        K = w_dram.shape[0] // P
        view = w_dram.rearrange("(k p) n -> p k n", p=P)
        width = min(2 * P, n_out)
        for c0 in range(0, n_out, width):
            unit, hi, lo = self.weights(view[:, :, c0:c0 + width])
            taken = self.product(unit, hi, lo, width, K, x, N)
            for i, (b, ps, mark) in enumerate(taken):
                evacuate(c0 // P + i, b, ps, mark)
        return mark

    def product(self, unit, hi, lo, width, K, x, N):
        taken = [(j, min(P, width - j)) + self.bank() for j in range(0, width, P)]
        done = []
        for k in range(K):
            for j, w, b, ps in taken:
                mark = self.mm3(ps[0:w, 0:N], (hi[:, k, j:j + w], lo[:, k, j:j + w]), x(k),
                                k == 0, k == K - 1, mark=k == K - 1)
                if k == K - 1:
                    done.append((b, ps, mark))
        self.used[unit] = mark
        return done

    def stage_in(self, lo_t, n):
        hi, lo, ready = self.m["in_hi"], self.m["in_lo"], self.in_ready

        def chunk(k):
            self.pe.wait(ready[k])
            return hi[:, k, lo_t:lo_t + n], lo[:, k, lo_t:lo_t + n]
        return chunk

    def setup(self):
        m, a, act, dve, pe, sync, pool = self.m, self.a, self.act, self.dve, self.pe, self.sync, self.pool
        consts = pool.dma(m["ident"][:, :], a["k_ident"], self.slot["consts"])
        self.const_tables = pool.dma(m["const"][:, :], a["k_block1"], self.slot["table"])
        mean = dve.run(lambda e: e.memset(m["mean_w"][:, :], 1.0 / D))
        tok = m["tmp"][:, :].rearrange("p (s t d) -> p s t d", s=2, t=2)
        x_in = sync.dma(tok[:, 0, :, :], a["x"].rearrange("b (t p) d -> p (b t) d", p=P), self.slot["tokens"])
        rows = m["work"]
        plan = [
            [(0, "ln_gain", 48), (48, "ln_bias", 48)],
            [(0, "norm_g_2", 48), (48, "pool_scale", 8), (56, "final_g_2", 8), (64, "mla_g_q_2", 3),
             (67, "mla_g_kv_2", 1), (68, "c_2", 8), (76, "c_ctx_2", 8)],
            [(0, "ada_b_2.0", 72)],
            [(0, "ada_b_2.1", 72)],
        ]
        n_rows, landed = [], None
        for g, parts in enumerate(plan):
            for r0, name, n in parts:
                src = a[name]
                landed = pool.dma(rows[r0:r0 + n, g * P:(g + 1) * P], src, self.slot["rows"])
            n_rows.append(r0 + n)
        pe.wait(consts, landed)
        self.col = {}
        offset = 0
        b, ps = self.bank()
        for g, n in enumerate(n_rows):
            mark = self.transpose(ps[:, g * P:g * P + n], rows[0:n, g * P:(g + 1) * P], mark=g == 3)
            for r0, name, k in plan[g]:
                self.col[name] = g * P + r0
        read = act.run(lambda e: e.activation(m["cols"][:, 0:96], ps[:, 0:96], ACT.Copy), mark)
        read = act.run(lambda e: e.activation(m["cols"][:, 128:212], ps[:, 128:212], ACT.Copy))
        for g in (2, 3):
            read = act.run(lambda e, g=g: e.activation(
                m["cols"][:, g * P:g * P + 72], ps[:, g * P:g * P + 72], ACT.Copy))
        self.bank_free[b] = read
        self.cols_ready = read
        c0 = self.col["c_2"]
        c_view = m["cols"][:, c0:c0 + 16].rearrange("p (v d) -> p d v", v=2)
        silu = act.run(lambda e: e.activation(m["c_silu"][:, :, :], c_view, ACT.Silu), read)
        hi = act.run(lambda e: e.activation(m["c_split"][:, :, 0:2], m["c_silu"][:, :, :], ACT.Copy), silu)
        self.c_ready = dve.run(lambda e: e.tensor_tensor(
            m["c_split"][:, :, 2:4], m["c_silu"][:, :, :], m["c_split"][:, :, 0:2].bitcast(F32),
            ALU.subtract), hi)
        self.transpose_in(tok[:, 0], x_in, 0)
        self.mean_ready = mean
        self.h_read = mark
        self.ada_blocks = [(layer, n) for layer in range(DEPTH) for n in range(N_MOD * D // 512)]
        self.ada_bank = None
        self.ada_free = None
        self.mod_ready = [None] * DEPTH

    def transpose_in(self, tok, landed, t0):
        m = self.m
        self.pe.wait(landed)
        for d in range(DC):
            b, ps = self.bank()
            for t in range(2):
                mark = self.transpose(ps[:, t * P:(t + 1) * P], tok[:, t, d * P:(d + 1) * P], mark=t == 1)
            x = m["x"][:, d, t0:t0 + S]
            self.bank_free[b] = self.dve.run(lambda e, x=x, ps=ps: e.tensor_copy(x, ps[:, 0:S]), mark)
            self.x_ready[d] = self.bank_free[b]
            self.in_ready.append(self.split_act(d, t0, x, self.bank_free[b]))
        self.tmp_read = [mark]

    def split_act(self, d, t0, x, mark, n=S):
        hi, lo = (self.m[k][:, d, t0:t0 + n] for k in ("in_hi", "in_lo"))
        h = self.act.run(lambda e: e.activation(hi, x, ACT.Copy), mark, self.in_read)
        return self.dve.run(lambda e: e.tensor_tensor(lo, x, hi.bitcast(F32), ALU.subtract), h)

    def ada_step(self):
        m, pe, act, dve = self.m, self.pe, self.act, self.dve
        if self.ada_bank is None:
            if not self.ada_blocks:
                return
            self.ada_at, self.ada_bank = self.ada_blocks.pop(0), self.bank()
            half = 0
        else:
            half = 1
        (layer, n), (b, ps) = self.ada_at, self.ada_bank
        view = self.a["ada_w_2"][layer].rearrange("(k p) n -> p k n", p=P)
        pe.wait(self.c_ready)
        unit, hi, lo = self.weights(view[:, 4 * half:4 * half + 4, 512 * n:512 * n + 512])
        for k in range(4):
            c = m["c_split"][:, 4 * half + k, :]
            last = half == 1 and k == 3
            self.mm(ps[0:4, :], c, hi[:, k, :], start=half == 0 and k == 0, stop=False)
            mark = self.mm(ps[0:4, :], c, lo[:, k, :], start=False, stop=last, mark=k == 3)
        self.used[unit] = mark
        if half == 0:
            return
        self.ada_bank = None
        self.finish_ada()
        row = m["ada_row"]
        copied = act.run(lambda e: e.activation(row[:, :], ps[0:4, :], ACT.Copy), mark, self.ada_free)
        self.bank_free[b] = copied
        self.ada_pending = (layer, n, row, copied)

    def finish_ada(self):
        if self.ada_pending is None:
            return
        m, dve = self.m, self.dve
        layer, n, row, copied = self.ada_pending
        self.ada_pending = None
        self.pe.wait(copied)
        b, ps = self.bank()
        for j in range(4):
            mark = self.transpose(ps[:, 4 * j:4 * j + 4], row[:, j * P:(j + 1) * P], mark=j == 3)
        self.ada_free = mark
        v = ps[:, 0:16].rearrange("p (j c) -> p j c", c=4)
        mod = m["mod"][:, layer, 4 * n:4 * n + 4, :]
        bias = self.col[f"ada_b_2.{layer}"] + 4 * n
        bias = m["cols"][:, bias:bias + 4][:, :, None].broadcast_to([P, 4, 2])
        one = dve.run(lambda e: e.tensor_tensor(mod, v[:, :, 0:2], bias, ALU.add), mark, self.cols_ready)
        two = dve.run(lambda e: e.tensor_tensor(mod, v[:, :, 2:4], mod, ALU.add), one)
        self.bank_free[b] = two
        self.mod_ready[layer] = two

    def ffn(self, w_gate, w_up, w_down, t0, N, residual, ada=False):
        m, act, dve, pe = self.m, self.act, self.dve, self.pe
        x = self.stage_in(t0, N)
        gate, up = (w.rearrange("(k p) n -> p k n", p=P) for w in (w_gate, w_up))
        down = w_down.rearrange("(f p) n -> p f n", p=P)
        h_hi, h_lo = (m[k][:, :].rearrange("p (f t) -> p f t", t=N) for k in ("h_hi", "h_lo"))
        room = H_CHUNKS * S // N
        groups = [(0, FC)] if FC <= room else [(0, room), (room, FC)]
        gates = m["stat"]
        split_h = []
        for first, last in groups:
            h_ready = {}
            for f0 in range(first, last, 2):
                products = []
                for w in (gate, up):
                    unit, hi, lo = self.weights(w[:, :, f0 * P:f0 * P + 2 * P])
                    products.append(self.product(unit, hi, lo, 2 * P, DC, x, N))
                    if ada and w is gate:
                        self.ada_step()
                mark = products[1][1][2]
                self.in_read = mark
                for f in (f0, f0 + 1):
                    (bg, g, g_mark), (bu, u, u_mark) = products[0][f - f0], products[1][f - f0]
                    s = gates[:, f % 2, 0:N]
                    h32 = gates[:, 2 + f % 2, 0:N]
                    dh, dl = h_hi[:, f - first, :], h_lo[:, f - first, :]
                    slot_read = split_h[-2:-1] if len(split_h) > 1 else self.stat_read
                    silu = act.run(lambda e, s=s, g=g: e.activation(s, g[:, 0:N], ACT.Silu), g_mark,
                                   slot_read)
                    self.bank_free[bg] = silu
                    prod = dve.run(lambda e, s=s, u=u, o=h32: e.scalar_tensor_tensor(
                        o, s, 0.5, u[:, 0:N], ALU.mult, ALU.mult), silu, u_mark, slot_read)
                    self.bank_free[bu] = prod
                    hi_w = act.run(lambda e, o=dh, i=h32: e.activation(o, i, ACT.Copy), prod, self.h_read)
                    lo_w = dve.run(lambda e, o=dl, i=h32, h=dh: e.tensor_tensor(
                        o, i, h.bitcast(F32), ALU.subtract), hi_w, self.h_read)
                    split_h.append(lo_w)
                    h_ready[f] = [hi_w, lo_w]
                if ada:
                    self.ada_step()
            self.stat_read = split_h[-1:]
            if last == FC:
                act.quiet(lambda e: e.preload_act_table_set("natural_log_exp_and_others"))
            parts = [(f, min(f + 8, last)) for f in range(first, last, 8)]
            for d0 in range(0, DC, 2):
                taken = [self.bank(), self.bank()]
                for f0, f1 in parts:
                    unit, hi, lo = self.weights(down[:, f0:f1, d0 * P:d0 * P + 2 * P])
                    for d in range(2):
                        for f in range(f0, f1):
                            pe.wait(*h_ready[f])
                            mark = self.mm3(taken[d][1][:, 0:N],
                                            (hi[:, f - f0, d * P:d * P + P], lo[:, f - f0, d * P:d * P + P]),
                                            (h_hi[:, f - first, :], h_lo[:, f - first, :]),
                                            f == first, f == last - 1, mark=f == f1 - 1)
                        if f1 == last:
                            b, ps = taken[d]
                            self.bank_free[b] = residual(d0 + d, ps, mark)
                    self.used[unit] = mark
            self.h_read = mark

    def add_scaled(self, t0):
        def residual(d, ps, mark):
            x = self.m["x"][:, d, t0:t0 + S]
            done = self.dve.run(lambda e: e.scalar_tensor_tensor(
                x, x, ALPHA, ps[:, 0:S], ALU.mult, ALU.add), mark, self.x_ready[d])
            self.x_ready[d] = done
            return done
        return residual

    def add_gated(self, layer, slot, streams):
        def residual(d, ps, mark):
            for s in streams:
                x = self.m["x"][:, d, s * S:s * S + S]
                gate = self.m["mod"][:, layer, slot * DC + d, s:s + 1]
                p = ps[:, (s - streams[0]) * S:(s - streams[0] + 1) * S]
                done = self.dve.run(lambda e, x=x, g=gate, p=p: e.scalar_tensor_tensor(
                    x, p, g, x, ALU.mult, ALU.add), mark, self.x_ready[s * DC + d], self.mod_ready[layer])
                self.x_ready[s * DC + d] = done
            return done
        return residual

    def inv_root(self, b, ps, N, mark, factor, eps):
        m, act, dve = self.m, self.act, self.dve
        v, y, t = (m["stat"][:, i, 0:N] for i in range(3))
        var = dve.run(lambda e: e.tensor_scalar(v, ps[:, 0:N], factor, eps, ALU.mult, ALU.add),
                      mark, self.stat_read)
        self.bank_free[b] = var
        ln = act.run(lambda e: e.activation(y, v, ACT.Ln), var)
        ex = act.run(lambda e: e.activation(y, y, ACT.Exp, scale=-0.5), ln)
        n1 = dve.run(lambda e: e.scalar_tensor_tensor(t, v, -0.5, y, ALU.mult, ALU.mult), ex)
        n2 = dve.run(lambda e: e.tensor_tensor(t, t, y, ALU.mult), n1)
        return y, dve.run(lambda e: e.scalar_tensor_tensor(y, t, 1.5, y, ALU.add, ALU.mult), n2)

    def layer_norm(self, index, permuted=False):
        m, act, dve, pe = self.m, self.act, self.dve, self.pe
        x = m["x"][:, :, 0:S]
        tmp = m["tmp"][:, :].rearrange("p (d t) -> p d t", d=DC)
        centred, square = tmp[:, :, 0:S], tmp[:, :, S:2 * S]
        pe.wait(self.mean_ready)
        b, ps = self.bank()
        for d in range(DC):
            pe.wait(self.x_ready[d])
            mark = self.mm(ps[:, 0:S], m["mean_w"][:, :], x[:, d, :], d == 0, d == DC - 1, mark=d == DC - 1)
        b2, ps2 = self.bank()
        half = DC // 2
        for g in range(2):
            r = slice(g * half, (g + 1) * half)
            mean = ps[:, 0:S][:, None, :].broadcast_to([P, half, S])
            sub = dve.run(lambda e, r=r, mean=mean: e.tensor_tensor(
                centred[:, r, :], x[:, r, :], mean, ALU.subtract), mark, self.tmp_read)
            sq = act.run(lambda e, r=r: e.activation(square[:, r, :], centred[:, r, :], ACT.Square), sub)
            pe.wait(sq)
            for d in range(g * half, (g + 1) * half):
                var = self.mm(ps2[:, 0:S], m["mean_w"][:, :], square[:, d, :], d == 0, d == DC - 1,
                              mark=d == DC - 1)
        self.bank_free[b] = sub
        y, root = self.inv_root(b2, ps2, S, var, 1.0, LN_EPS)
        self.in_ready = []
        for d in range(DC):
            gain = m["cols"][:, self.col["ln_gain"] + index * DC + d:][:, 0:1]
            bias = m["cols"][:, self.col["ln_bias"] + index * DC + d:][:, 0:1]
            c, o = centred[:, d, :], x[:, d, :]
            hi, lo = m["in_hi"][:, d, 0:S], m["in_lo"][:, d, 0:S]
            if permuted:
                c_, o_ = (v.rearrange("p (c b a) -> p c b a", a=4, b=4) for v in (c, o))
                hi, lo = (v.rearrange("p (a b c) -> p c b a", a=4, b=4) for v in (hi, lo))
            else:
                c_, o_ = c, o
            normed = dve.run(lambda e, c=c: e.tensor_tensor(c, c, y, ALU.mult), root)
            high = act.run(lambda e, hi=hi, c=c_, g=gain, b=bias: e.activation(
                hi, c, ACT.Identity, scale=g, bias=b), normed, self.in_read, self.cols_ready)
            full = act.run(lambda e, o=o, c=c, g=gain, b=bias: e.activation(
                o, c, ACT.Identity, scale=g, bias=b))
            self.x_ready[d] = full
            self.in_ready.append(dve.run(lambda e, lo=lo, o=o_, hi=hi: e.tensor_tensor(
                lo, o, hi.bitcast(F32), ALU.subtract), full, self.in_read))
        self.stat_read = [normed]
        self.tmp_read = [full, normed]

    def sum_squares(self, chunks, N, marks):
        m, act, pe = self.m, self.act, self.pe
        tmp = m["tmp"][:, :].rearrange("p (d t) -> p d t", t=N)
        pe.wait(self.mean_ready)
        b, ps = self.bank()
        for d, c in enumerate(chunks):
            sq = act.run(lambda e, d=d, c=c: e.activation(tmp[:, d, :], c, ACT.Square), marks[d],
                         self.tmp_read)
            pe.wait(sq)
            mark = self.mm(ps[:, 0:N], m["mean_w"][:, :], tmp[:, d, :], d == 0, d == len(chunks) - 1,
                           mark=d == len(chunks) - 1)
        return b, ps, mark

    def rms_mod(self, layer, i, shift, scale, streams):
        m, act, dve = self.m, self.act, self.dve
        t0, N = streams[0] * S, S * len(streams)
        g0 = self.col["norm_g_2"] + (layer * 3 + i) * DC
        norm_g = m["cols"][:, g0:g0 + DC][:, :, None].broadcast_to([P, DC, 2])
        gain, mod = m["gain"], m["mod"]
        gained = dve.run(lambda e: e.scalar_tensor_tensor(
            gain[:, :, :], mod[:, layer, scale * DC:scale * DC + DC, :], 1.0, norm_g, ALU.add, ALU.mult),
            self.mod_ready[layer], self.cols_ready)
        b, ps, mark = self.sum_squares(
            [m["x"][:, d, t0:t0 + N] for d in range(DC)], N,
            [[self.x_ready[s * DC + d] for s in streams] for d in range(DC)])
        y, root = self.inv_root(b, ps, N, mark, 1.0, RMS_EPS)
        tmp = m["tmp"][:, :].rearrange("p (d t) -> p d t", d=DC)
        self.in_ready = [[] for _ in range(DC)]
        for d in range(DC):
            for s in streams:
                x, o = m["x"][:, d, s * S:s * S + S], tmp[:, d, s * S:s * S + S]
                hi, lo = m["in_hi"][:, d, s * S:s * S + S], m["in_lo"][:, d, s * S:s * S + S]
                g, sh = gain[:, d, s:s + 1], mod[:, layer, shift * DC + d, s:s + 1]
                yy = y[:, s * S - t0:s * S - t0 + S]
                n1 = dve.run(lambda e, o=o, x=x, g=g, yy=yy: e.scalar_tensor_tensor(
                    o, x, g, yy, ALU.mult, ALU.mult), root, mark, gained)
                n2 = act.run(lambda e, hi=hi, o=o, sh=sh: e.activation(
                    hi, o, ACT.Identity, bias=sh), n1, self.in_read)
                n3 = dve.run(lambda e, lo=lo, o=o, sh=sh, hi=hi: e.scalar_tensor_tensor(
                    lo, o, sh, hi.bitcast(F32), ALU.add, ALU.subtract), n2, self.in_read)
                self.in_ready[d].append(n3)
        self.stat_read = [n3]
        self.tmp_read = [n3]

    def pool_mixer(self):
        m, act, dve, pe, a = self.m, self.act, self.dve, self.pe, self.a
        PAD, W = 8, S + 16
        padded = m["tmp"][:, 0:DC * W].rearrange("p (d t) -> p d t", d=DC)
        sums = m["tmp"][:, DC * W:DC * W + 4 * W].rearrange("p (i d t) -> p i d t", i=2, d=2)
        mean = m["work"][:, 0:0 + 2 * S]
        zero = dve.run(lambda e: e.memset(padded[:, :, 0:PAD], 0.0), self.tmp_read)
        zero = dve.run(lambda e: e.memset(padded[:, :, PAD + S:], 0.0))
        u_ready = []

        def keep(d, b, ps, mark):
            u_ready.append(act.run(lambda e: e.activation(padded[:, d, PAD:PAD + S], ps[:, 0:S], ACT.Copy),
                                   mark, self.tmp_read))
            self.bank_free[b] = u_ready[-1]

        self.in_read = self.project(a["pool_w_in"][0], D, self.stage_in(0, S), S, keep)
        h_hi, h_lo = (m[k][:, :].rearrange("p (f t) -> p f t", t=S) for k in ("h_hi", "h_lo"))
        stat = m["stat"][:, 0, :].rearrange("p (d t) -> p d t", d=2)
        inverse = m["const"][:, 0:4 * S].rearrange("p (g t) -> p g t", g=4)
        mixed_ready = []
        prev = self.stat_read
        for g in range(4):
            src, half = padded[:, 2 * g:2 * g + 2, :], 1
            n = W
            step = zero
            for i in range(g + 1):
                n -= half
                dst = sums[:, i % 2, :, 0:n]
                step = dve.run(lambda e, d=dst, s=src, n=n, h=half: e.tensor_tensor(
                    d, s[:, :, 0:n], s[:, :, h:h + n], ALU.add), step, u_ready[2 * g + 1])
                src, half = sums[:, i % 2], half * 2
            first = PAD - half // 2
            inv = inverse[:, g, :][:, None, :].broadcast_to([P, 2, S])
            u = padded[:, 2 * g:2 * g + 2, PAD:PAD + S]
            step = dve.run(lambda e, s=src, f=first, inv=inv: e.tensor_tensor(
                stat, s[:, :, f:f + S], inv, ALU.mult), step, self.const_tables, prev)
            step = dve.run(lambda e, u=u: e.tensor_tensor(stat, stat, u, ALU.subtract), step)
            hi, lo = h_hi[:, 2 * g:2 * g + 2, :], h_lo[:, 2 * g:2 * g + 2, :]
            high = act.run(lambda e, hi=hi: e.activation(hi, stat, ACT.Copy), step, self.h_read)
            low = dve.run(lambda e, lo=lo, hi=hi: e.tensor_tensor(lo, stat, hi.bitcast(F32), ALU.subtract),
                          high, self.h_read)
            prev = [high, low]
            mixed_ready += [low]
        self.tmp_read = [step]
        view = a["pool_w_group"][0].rearrange("g (c p) e -> p (g c) e", p=P)
        unit, whi, wlo = self.weights(view)
        pe.wait(*mixed_ready)
        y_ready = []
        for e_ in range(DC):
            g, j = e_ // 2, (e_ % 2) * P
            b, ps = self.bank()
            for c in range(2):
                k = 2 * g + c
                mark = self.mm3(ps[:, 0:S], (whi[:, k, j:j + P], wlo[:, k, j:j + P]),
                                (h_hi[:, k, :], h_lo[:, k, :]), c == 0, c == 1, mark=c == 1)
            t = m["stat"][:, 1 + e_ % 2, 0:S]
            scale = m["cols"][:, self.col["pool_scale"] + e_:][:, 0:1]
            hi, lo = h_hi[:, DC + e_, :], h_lo[:, DC + e_, :]
            scaled = act.run(lambda e, t=t, ps=ps, s=scale: e.activation(t, ps[:, 0:S], ACT.Copy, scale=s),
                             mark, prev, y_ready[e_ - 2] if e_ > 1 else None, self.cols_ready)
            self.bank_free[b] = scaled
            high = act.run(lambda e, hi=hi, t=t: e.activation(hi, t, ACT.Copy), scaled)
            y_ready.append(dve.run(lambda e, lo=lo, t=t, hi=hi: e.tensor_tensor(
                lo, t, hi.bitcast(F32), ALU.subtract), high))
        self.used[unit] = mark
        self.stat_read = [y_ready[-1]]
        residual = self.add_scaled(0)

        def add(d, b, ps, mark):
            self.bank_free[b] = residual(d, ps, mark)

        def y(k):
            pe.wait(y_ready[k])
            return h_hi[:, DC + k, :], h_lo[:, DC + k, :]

        self.h_read = self.project(a["pool_w_out"][0], D, y, S, add)

    def attend(self, items):
        m, act, dve, pe = self.m, self.act, self.dve, self.pe
        buf = m["tmp"][:, 2048:4096].rearrange("p (i n) -> p i n", i=4)
        n_items = len(items)
        st = {}
        for step in range(n_items + 2):
            if step < n_items:
                it = items[step]
                n, s = it["n"], st.setdefault(step, {})
                b, ps = self.bank()
                s["scores"] = it["scores"](ps)
                p = buf[:, step % 2, 0:n]
                peak, neg, total = (m["soft"][:, i, step % 4:step % 4 + 1] for i in range(3))
                slot_free = st[step - 2]["turned"] if step > 1 else self.tmp_read
                if it["bias"]:
                    ready = it["bias"](p, ps, [s["scores"], slot_free])
                    self.bank_free[b] = ready
                    src = p
                else:
                    ready, src = s["scores"], ps[:, 0:n]
                mx = dve.run(lambda e, o=peak, i=src: e.tensor_reduce(o, i, AX_X, ALU.max), ready)
                ng = dve.run(lambda e, o=neg, i=peak, c=-it["scale"]: e.tensor_scalar(
                    o, i, c, None, ALU.mult), mx)
                s["exp"] = act.run(lambda e, o=p, i=src, ng=neg, t=total, c=it["scale"]: e.activation(
                    o, i, ACT.Exp, bias=ng, scale=c, accum_out=t), ng, slot_free)
                if not it["bias"]:
                    self.bank_free[b] = s["exp"]
            if 1 <= step <= n_items:
                it, s = items[step - 1], st[step - 1]
                n = it["n"]
                p = buf[:, (step - 1) % 2, 0:n]
                turned = buf[:, 2 + (step - 1) % 2, 0:n]
                b, ps = self.bank()
                pe.wait(s["exp"])
                for k in range(n // P):
                    s["turned"] = self.transpose(ps[:, k * P:(k + 1) * P], p[:, k * P:(k + 1) * P],
                                                 mark=k == n // P - 1)
                free = st[step - 3]["summed"] if step > 2 else self.tmp_read
                s["back"] = act.run(lambda e, o=turned, i=ps, n=n: e.activation(o, i[:, 0:n], ACT.Copy),
                                    s["turned"], free)
                self.bank_free[b] = s["back"]
            if step >= 2:
                it, s = items[step - 2], st[step - 2]
                n = it["n"]
                turned = buf[:, 2 + (step - 2) % 2, 0:n]
                total, inv = (m["soft"][:, i, (step - 2) % 4:(step - 2) % 4 + 1] for i in (2, 3))
                b, ps = self.bank()
                pe.wait(s["back"], it.get("ready"))
                last = n // P - 1
                for k in range(last + 1):
                    s["summed"] = self.mm(ps[:, 0:it["width"]], turned[:, k * P:(k + 1) * P],
                                          it["values"][k], k == 0, k == last, mark=k == last)
                rec = dve.run(lambda e, o=inv, i=total: e.reciprocal(o, i), s["exp"])
                done = dve.run(lambda e, o=it["o"], ps=ps, w=it["width"], inv=inv: e.tensor_scalar(
                    o, ps[:, 0:w], inv, None, ALU.mult), s["summed"], rec, self.tmp_read)
                self.bank_free[b] = done
        return done, s["summed"]

    def turn_rows(self, rows, n_tiles, chunk0, n_chunks, ready):
        m, act, dve, pe = self.m, self.act, self.dve, self.pe
        N = n_tiles * P
        pe.wait(ready)
        marks = []
        for c in range(n_chunks):
            b, ps = self.bank()
            for t in range(n_tiles):
                mark = self.transpose(ps[:, t * P:(t + 1) * P], rows(t)[:, c * P:(c + 1) * P],
                                      mark=t == n_tiles - 1)
            hi, lo = (m[k][:, chunk0 + c, 0:N] for k in ("in_hi", "in_lo"))
            high = act.run(lambda e, hi=hi, ps=ps: e.activation(hi, ps[:, 0:N], ACT.Copy), mark,
                           self.in_read)
            low = dve.run(lambda e, lo=lo, ps=ps, hi=hi: e.tensor_tensor(
                lo, ps[:, 0:N], hi.bitcast(F32), ALU.subtract), high, self.in_read)
            self.bank_free[b] = low
            marks.append(low)
        self.tmp_read = [mark]
        return marks

    def value_rows(self, w_dram, x, n_tiles, dst):
        m, act = self.m, self.act
        K, n = w_dram.shape[0] // P, w_dram.shape[1]
        view = w_dram.rearrange("(k p) n -> p k n", p=P)
        width = min(UNIT // K, 512, n)
        done = []
        for c0 in range(0, n, width):
            unit, hi, lo = self.weights(view[:, :, c0:c0 + width])
            for t in range(n_tiles):
                b, ps = self.bank()
                for k in range(K):
                    xh, xl = x(k)
                    tok = slice(t * P, (t + 1) * P)
                    self.mm(ps[:, 0:width], xh[:, tok], hi[:, k, :], k == 0, False)
                    self.mm(ps[:, 0:width], xh[:, tok], lo[:, k, :], False, False)
                    mark = self.mm(ps[:, 0:width], xl[:, tok], hi[:, k, :], False, k == K - 1,
                                   mark=k == K - 1)
                o = dst(t)[:, c0:c0 + width]
                copied = act.run(lambda e, o=o, ps=ps: e.activation(o, ps[:, 0:width], ACT.Copy), mark,
                                 self.h_read)
                self.bank_free[b] = copied
            self.used[unit] = mark
        return copied, mark

    def dilated_mixer(self):
        m, act, dve, pe, a = self.m, self.act, self.dve, self.pe, self.a
        w_qkv = a["attn_w_qkv"][0]
        quad = 4 * HEAD
        size = DIL_GROUPS * 2 * S
        slopes = (2.0 ** (-8.0 * np.arange(1, 49) / 48)).reshape(3, 16).astype(np.float32)
        dist = m["const"][:, 4 * S:].rearrange("p (t n) -> p t n", t=2)
        rows = m["tmp"][:, 0:2048].rearrange("p (t n) -> p t n", t=2)
        x = self.stage_in(0, S)
        summed = [self.h_read, self.h_read]
        start_free = self.h_read
        for hq in range(HEADS // 4):
            buf = m["work"][:, (hq % 2) * 3 * size:(hq % 2 + 1) * 3 * size]
            qT, kT = (buf[:, i * size:(i + 1) * size].rearrange("p (g c t) -> p g c t", g=3, c=2)
                      for i in range(2))
            v = buf[:, 2 * size:3 * size].rearrange("p (t g n) -> p t g n", t=2, g=3)
            self.h_read = summed[hq % 2]
            ready = []
            for g in range(DIL_GROUPS):
                for which, dst, factor in ((0, qT, HEAD ** -0.5), (1, kT, 1.0)):
                    def keep(c, b, ps, mark, g=g, dst=dst, factor=factor):
                        done = act.run(lambda e: e.activation(dst[:, g, c, :], ps[:, 0:S], ACT.Copy,
                                                              scale=factor), mark, self.h_read)
                        self.bank_free[b] = done
                        ready.append(done)
                    c0 = (g * 3 + which) * D + hq * quad
                    self.project(w_qkv[:, c0:c0 + quad], quad, x, S, keep)
                c0 = (g * 3 + 2) * D + hq * quad
                copied, self.in_read = self.value_rows(
                    w_qkv[:, c0:c0 + quad], x, 2, lambda t, g=g: v[:, t, g, :])
                ready.append(copied)
            items = []
            pe.wait(*ready)
            for h in range(4):
                for t in range(2):
                    c, r = h // 2, (h % 2) * HEAD
                    q0 = t * P

                    def scores(ps, c=c, r=r, q0=q0):
                        for g, k0, n, col in ((0, 0, S, 0), (1, q0, P, S), (2, q0, P, S + P)):
                            mark = self.mm(ps[:, col:col + n], qT[r:r + HEAD, g, c, q0:q0 + P],
                                           kT[r:r + HEAD, g, c, k0:k0 + n], mark=g == 2)
                        return mark

                    def bias(o, ps, marks, head=hq * 4 + h, t=t):
                        for g, col, n in ((0, 0, S), (1, S, P), (2, S + P, P)):
                            mark = dve.run(lambda e, s=-float(slopes[g, head]), col=col, n=n:
                                           e.scalar_tensor_tensor(o[:, col:col + n], dist[:, t, col:col + n],
                                                                  s, ps[:, col:col + n], ALU.mult, ALU.add),
                                           *marks, self.const_tables)
                        return mark

                    e0 = h * HEAD
                    items.append(dict(
                        n=512, scores=scores, bias=bias, scale=1.0, width=HEAD,
                        values=[v[:, 0, 0, e0:e0 + HEAD], v[:, 1, 0, e0:e0 + HEAD],
                                v[:, t, 1, e0:e0 + HEAD], v[:, t, 2, e0:e0 + HEAD]],
                        o=rows[:, t, (hq * 4 + h) * HEAD:(hq * 4 + h + 1) * HEAD]))
            done, summed[hq % 2] = self.attend(items)
            self.tmp_read = [summed[hq % 2]]
        self.h_read = summed[(HEADS // 4 - 1) % 2]
        turned = self.turn_rows(lambda t: rows[:, t, :], 2, 0, DC, done)
        residual = self.add_scaled(0)
        tmp = m["stat"]

        def add(d, b, ps, mark):
            t = tmp[:, d % 2, 0:S]
            natural = ps[:, 0:S].rearrange("p (a b c) -> p c b a", a=4, b=4)
            copied = act.run(lambda e: e.activation(t.rearrange("p (c b a) -> p c b a", a=4, b=4), natural,
                                                    ACT.Copy), mark, self.x_ready[max(d - 2, 0)],
                             self.stat_read)
            self.bank_free[b] = copied
            residual(d, t, copied)

        self.in_ready = turned
        self.in_read = self.project(a["attn_w_out"][0], D, self.stage_in(0, S), S, add)
        self.stat_read = [self.x_ready[DC - 1]]

    def load_rpb(self):
        pad = self.m["tmp"][0:NA_HEADS * RPB_H, 0:P]
        zero = self.pool.run(lambda e: e.memset(pad, 0.0), self.tmp_read)
        src = self.a["ab_rpb_2"][0].rearrange("h r c -> (h r) c")
        first = GRID_W - 1 - (RPB_W // 2)
        got = self.pool.dma(pad[:, first:first + RPB_W], src, self.slot["rpb"], zero)
        copies = pad[:, None, :].broadcast_to([NA_HEADS * RPB_H, GRID_W, P])
        self.rpb_stored = self.pool.dma(self.a["scratch"], copies, self.slot["rpb"], got)
        self.tmp_read = [self.rpb_stored]

    def load_na_tables(self):
        m, pool = self.m, self.pool
        self.const_tables = pool.dma(m["const"][:, 0:1792], self.a["k_mixer"], self.slot["table"],
                                     self.const_read)
        bias = m["work"][:, 8192:8192 + 4096].rearrange("p (h t n) -> p h t n", h=NA_HEADS, t=2)
        scratch = self.a["scratch"]
        pool.wait(self.rpb_stored)
        for h in range(NA_HEADS):
            for qr in range(GRID_H):
                row = h * RPB_H + RPB_H // 2 - qr
                src = bass.AP(scratch.tensor, row * GRID_W * P + GRID_W - 1,
                              [[P - 1, GRID_W], [GRID_W * P, GRID_H], [1, GRID_W]])
                p0 = (qr % 2) * GRID_W
                dst = bias[p0:p0 + GRID_W, h, qr // 2, :].rearrange("p (r c) -> p r c", r=GRID_H)
                got = pool.dma(dst, src, self.slot["bias"], self.h_read)
        mask = m["const"][:, 1280:1792].rearrange("p (t n) -> p t n", t=2)
        self.na_bias = bias
        for h in range(NA_HEADS):
            self.na_bias_ready = pool.run(lambda e, h=h: e.tensor_tensor(
                bias[:, h, :, :], bias[:, h, :, :], mask, ALU.add), got, self.const_tables)

    def fourier_na_mixer(self, layer):
        m, act, dve, pe, a = self.m, self.act, self.dve, self.pe, self.a
        w_in = a["ab_w_in_2"][0]
        N = 2 * S
        x = self.stage_in(0, N)
        self.load_na_tables()
        uT, qT, kT, v = (m["work"][:, i * 2048:(i + 1) * 2048].rearrange("p (c t) -> p c t", c=4)
                         for i in range(4))
        ready = {}

        def keeper(name, dst, factor=1.0):
            def keep(c, b, ps, mark):
                ready[name] = act.run(lambda e: e.activation(dst[:, c, :], ps[:, 0:N], ACT.Copy,
                                                             scale=factor), mark, self.h_read)
                self.bank_free[b] = ready[name]
            return keep

        self.project(w_in[:, 0:512], 512, x, N, keeper("u", uT))
        dft_d = m["const"][:, 0:256]
        dft_n = m["const"][:, 256:1280].rearrange("p (k f n) -> p k f n", k=2, f=2)
        spec = m["tmp"][:, :].rearrange("p (t g n) -> p t g n", t=4, g=4)
        pe.wait(ready["u"], self.const_tables)
        for g in range(4):
            for t in range(4):
                b, ps = self.bank()
                mark = self.mm(ps[:, 0:256], uT[:, g, t * P:(t + 1) * P], dft_d, mark=True)
                spec_ready = dve.run(lambda e, ps=ps, t=t, g=g: e.tensor_copy(spec[:, t, g, :], ps[:, 0:256]),
                                     mark, self.tmp_read)
                self.bank_free[b] = spec_ready
        self.project(w_in[:, 512:1024], 512, x, N, keeper("q", qT, HEAD ** -0.5))
        self.project(w_in[:, 1024:1536], 512, x, N, keeper("k", kT))
        v_done, self.in_read = self.value_rows(w_in[:, 1536:2048], x, 4, lambda t: v[:, t, :])
        turned = []
        pe.wait(spec_ready)
        for g in range(4):
            b, ps = self.bank()
            for s in range(2):
                for i, (k, f) in enumerate(((0, 0), (1, 0), (0, 1), (1, 1))):
                    mark = self.mm(ps[:, s * S:(s + 1) * S], spec[:, 2 * s + k, g, f * P:(f + 1) * P],
                                   dft_n[:, k, f, :], i == 0, i == 3, mark=s == 1 and i == 3)
            hi, lo = (m[k][:, g, 0:N] for k in ("in_hi", "in_lo"))
            high = act.run(lambda e, hi=hi, ps=ps: e.activation(hi, ps[:, 0:N], ACT.Copy), mark, self.in_read)
            low = dve.run(lambda e, lo=lo, ps=ps, hi=hi: e.tensor_tensor(
                lo, ps[:, 0:N], hi.bitcast(F32), ALU.subtract), high)
            self.bank_free[b] = low
            turned.append(low)
        self.tmp_read = [mark]
        rows = m["tmp"][:, 0:2048].rearrange("p (t n) -> p t n", t=4)
        pe.wait(ready["q"], ready["k"], v_done)
        items = []
        for t in range(4):
            for h in range(NA_HEADS):
                c, r = h // 2, (h % 2) * HEAD
                k0, n = (0, N) if t < 2 else (S, S)

                def scores(ps, c=c, r=r, t=t, k0=k0, n=n):
                    return self.mm(ps[:, 0:n], qT[r:r + HEAD, c, t * P:(t + 1) * P],
                                   kT[r:r + HEAD, c, k0:k0 + n], mark=True)

                def bias(o, ps, marks, h=h, t=t):
                    dve.run(lambda e: e.tensor_tensor(o[:, 0:S], self.na_bias[:, h, t, :], ps[:, 0:S],
                                                      ALU.add), *marks, self.na_bias_ready)
                    return dve.run(lambda e: e.tensor_copy(o[:, S:N], ps[:, S:N]))

                items.append(dict(
                    n=n, scores=scores, bias=bias if t < 2 else None, scale=1.0, width=HEAD,
                    values=[v[:, k, h * HEAD:(h + 1) * HEAD] for k in range(k0 // P, (k0 + n) // P)],
                    o=rows[:, t, h * HEAD:(h + 1) * HEAD]))
        done, summed = self.attend(items)
        self.h_read = summed
        turned += self.turn_rows(lambda t: rows[:, t, :], 4, 4, 4, done)
        residual = self.add_gated(layer, 5, (0, 1))

        def add(d, b, ps, mark):
            self.bank_free[b] = residual(d, ps, mark)

        self.in_ready = turned
        self.in_read = self.project(a["ab_w_out_2"][0], D, self.stage_in(0, N), N, add)

    def mla_mixer(self, layer):
        m, act, dve, pe, a = self.m, self.act, self.dve, self.pe, self.a
        N = 2 * S
        tables = self.pool.dma(m["const"][:, 0:896], a["k_rope"], self.slot["table"], self.const_read)
        cos, sin = m["const"][:, 0:S], m["const"][:, S:2 * S]
        rotate = m["const"][:, 512:640]
        dup, dup_rotate = m["const"][0:ROPE, 640:768], m["const"][0:ROPE, 768:896]
        tmp, work = m["tmp"], m["work"]
        cq = tmp[:, 0:768].rearrange("p (c t) -> p c t", c=3)
        ckv = tmp[:, 768:1280]
        lat = m["latent"]
        cq_hi, cq_lo = (lat[:, i * 768:(i + 1) * 768].rearrange("p (c t) -> p c t", c=3) for i in range(2))
        ckv_hi, ckv_lo = lat[:, 1536:2048], lat[:, 2048:2560]
        qn = work[:, 0:2048].rearrange("p (h t) -> p h t", h=8)
        qr = work[:, 2048:3072].rearrange("p (j t) -> p j t", j=4)
        kn = work[:, 3072:7168].rearrange("p (h t) -> p h t", h=8)
        kr = work[:, 7168:7680]
        v = work[:, 7680:11776].rearrange("p (t n) -> p t n", t=4)
        spare = work[:, 11776:12288]
        w_in = a["mla_w_in_2"][0]
        xq, xk = self.stage_in(0, S), self.stage_in(0, N)
        h_free, t_free = self.h_read, self.tmp_read
        ready = {}

        def keep_q(c, b, ps, mark):
            ready[c] = act.run(lambda e: e.activation(cq[:, c, :], ps[:, 0:S], ACT.Copy), mark, t_free)
            self.bank_free[b] = ready[c]

        def keep_kv(c, b, ps, mark):
            ready["kv"] = act.run(lambda e: e.activation(ckv, ps[:, 0:N], ACT.Copy), mark, t_free)
            self.bank_free[b] = ready["kv"]

        def keep_kr(c, b, ps, mark):
            ready["kr"] = act.run(lambda e: e.activation(kr[0:ROPE, :], ps[0:ROPE, 0:N], ACT.Copy), mark,
                                  h_free)
            self.bank_free[b] = ready["kr"]

        self.project(w_in[:, 0:256], 256, xq, S, keep_q)
        self.project(w_in[:, 256:384], 128, xq, S, lambda c, b, ps, mark: keep_q(2, b, ps, mark))
        self.project(w_in[:, 384:512], 128, xk, N, keep_kv)
        self.in_read = self.project(w_in[:, 512:576], 64, xk, N, keep_kr)

        pe.wait(ready["kr"], tables)
        b1, both = self.bank()
        m1 = self.mm(both[:, 0:N], dup, kr[0:ROPE, :], mark=True)
        b2, other = self.bank()
        m2 = self.mm(other[:, 0:S], dup_rotate, kr[0:ROPE, 0:S], mark=True)
        r0 = dve.run(lambda e: e.tensor_tensor(spare[:, 0:S], other[:, 0:S], sin, ALU.mult), m2, h_free, tables)
        self.bank_free[b2] = r0
        r1 = dve.run(lambda e: e.tensor_copy(kr[:, S:N], both[:, S:N]), m1, m2)
        r2 = dve.run(lambda e: e.tensor_tensor(kr[:, 0:S], both[:, 0:S], cos, ALU.mult))
        self.bank_free[b1] = r2
        kr_done = dve.run(lambda e: e.tensor_tensor(kr[:, 0:S], kr[:, 0:S], spare[:, 0:S], ALU.add), r0, r2)

        sq = m["tmp"][:, 1536:2560]
        def latent_norm(chunks, n, width, gain, his, los, marks):
            b, ps = self.bank()
            for d, c in enumerate(chunks):
                q = work[:, 7680 + d * n:7680 + (d + 1) * n]
                s = act.run(lambda e, q=q, c=c: e.activation(q, c, ACT.Square), marks[d], h_free)
                pe.wait(s)
                mark = self.mm(ps[:, 0:n], m["mean_w"][:, :], q, d == 0, d == len(chunks) - 1,
                               mark=d == len(chunks) - 1)
            y, root = self.inv_root(b, ps, n, mark, D / width, RMS_EPS)
            for d, c in enumerate(chunks):
                g = m["cols"][:, gain + d:gain + d + 1]
                n1 = dve.run(lambda e, c=c, g=g: e.scalar_tensor_tensor(c, c, g, y, ALU.mult, ALU.mult),
                             root, mark)
                n2 = act.run(lambda e, c=c, hi=his[d]: e.activation(hi, c, ACT.Copy), n1, t_free)
                n3 = dve.run(lambda e, c=c, hi=his[d], lo=los[d]: e.tensor_tensor(
                    lo, c, hi.bitcast(F32), ALU.subtract), n2, t_free)
            self.stat_read = [n3]
            return n3, mark

        kv_ready, mark = latent_norm([ckv], N, P, self.col["mla_g_kv_2"], [ckv_hi], [ckv_lo], [ready["kv"]])
        h_free = [h_free, mark]
        q_ready, mark = latent_norm([cq[:, c, :] for c in range(3)], S, Q_RANK, self.col["mla_g_q_2"],
                                    [cq_hi[:, c, :] for c in range(3)], [cq_lo[:, c, :] for c in range(3)],
                                    [ready[c] for c in range(3)])
        self.h_read = [h_free, mark]

        w_uq = a["mla_w_uq_2"][0].rearrange("(k p) n -> p k n", p=P)
        pe.wait(q_ready)
        for j in range(MLA_HEADS // 2):
            cols = w_uq[:, :, j * 384:(j + 1) * 384]
            heads = [cols[:, k, :].rearrange("p (h c) -> p h c", h=2) for k in range(3)]
            unit, hi, lo = self.weights(cols, [(k * 384 + first, heads[k][:, :, c0:c1]) for k in range(3)
                                               for first, c0, c1 in ((0, 0, NOPE), (2 * NOPE, NOPE, 192))])
            for part in range(3):
                b, ps = self.bank()
                for k in range(3):
                    w = [t[:, k, part * P:(part + 1) * P] for t in (hi, lo)]
                    mark = self.mm3(ps[:, 0:S], w, (cq_hi[:, k, :], cq_lo[:, k, :]), k == 0, k == 2,
                                    mark=k == 2)
                if part < 2:
                    q_done = act.run(lambda e, o=qn[:, 2 * j + part, :], ps=ps: e.activation(
                        o, ps[:, 0:S], ACT.Copy), mark, h_free)
                    self.bank_free[b] = q_done
                else:
                    raw = spare[:, 0:S]
                    c1 = act.run(lambda e, ps=ps: e.activation(raw, ps[:, 0:S], ACT.Copy), mark, kr_done)
                    self.bank_free[b] = c1
                    pe.wait(c1)
                    b2, ps2 = self.bank()
                    rot = self.mm(ps2[:, 0:S], rotate, raw, mark=True)
                    o, t = qr[:, j, :], spare[:, S:2 * S]
                    d1 = dve.run(lambda e, t=t, ps2=ps2: e.tensor_tensor(t, ps2[:, 0:S], sin, ALU.mult), rot)
                    self.bank_free[b2] = d1
                    d2 = dve.run(lambda e, o=o: e.tensor_tensor(o, raw, cos, ALU.mult), c1)
                    kr_done = dve.run(lambda e, o=o, t=t: e.tensor_tensor(o, o, t, ALU.add), d1, d2)
            self.used[unit] = mark
        unit, hi, lo = self.weights(a["mla_w_uk_2"][0].rearrange("(k p) n -> p k n", p=P))
        pe.wait(kv_ready)
        for h in range(MLA_HEADS):
            b, ps = self.bank()
            w = [t[:, 0, h * P:(h + 1) * P] for t in (hi, lo)]
            mark = self.mm3(ps[:, 0:N], w, (ckv_hi, ckv_lo), True, True, mark=True)
            kn_done = act.run(lambda e, ps=ps, h=h: e.activation(kn[:, h, :], ps[:, 0:N], ACT.Copy), mark)
            self.bank_free[b] = kn_done
        self.used[unit] = mark
        v_done, mark = self.value_rows(a["mla_w_uv_2"][0], lambda k: (ckv_hi, ckv_lo), 4,
                                       lambda t: v[:, t, :])
        self.tmp_read = [mark, kv_ready, q_ready]
        rows = m["tmp"][:, 0:2048].rearrange("p (t n) -> p t n", t=2)
        pe.wait(q_done, kn_done, v_done, kr_done)
        items = []
        for t in range(2):
            for h in range(MLA_HEADS):
                r = (h % 2) * ROPE

                def scores(ps, h=h, r=r, t=t):
                    self.mm(ps[:, 0:N], qn[:, h, t * P:(t + 1) * P], kn[:, h, :], True, False)
                    return self.mm(ps[:, 0:N], qr[r:r + ROPE, h // 2, t * P:(t + 1) * P],
                                   kr[r:r + ROPE, :], False, True, mark=True)

                items.append(dict(
                    n=N, scores=scores, bias=None, scale=float((NOPE + ROPE) ** -0.5), width=P,
                    values=[v[:, k, h * P:(h + 1) * P] for k in range(4)],
                    o=rows[:, t, h * P:(h + 1) * P]))
        done, summed = self.attend(items)
        self.h_read = summed
        turned = self.turn_rows(lambda t: rows[:, t, :], 2, 0, DC, done)
        residual = self.add_gated(layer, 5, (0,))

        def add(d, b, ps, mark):
            self.bank_free[b] = residual(d, ps, mark)

        self.in_ready = turned
        self.in_read = self.project(a["mla_w_o_2"][0], D, self.stage_in(0, S), S, add)

    def finish(self):
        m, dve, act, pe = self.m, self.dve, self.act, self.pe
        b, ps, mark = self.sum_squares([m["x"][:, d, 0:S] for d in range(DC)], S, self.x_ready[:DC])
        y, root = self.inv_root(b, ps, S, mark, 1.0, RMS_EPS)
        g0 = self.col["final_g_2"]
        rows = m["work"][:, 0:2048].rearrange("p (t n) -> p t n", t=2)
        out = self.out.rearrange("b (t p) d -> p (b t) d", p=P)
        for d in range(DC):
            x, g = m["x"][:, d, 0:S], m["cols"][:, g0 + d:g0 + d + 1]
            n = dve.run(lambda e, x=x, g=g: e.scalar_tensor_tensor(x, x, g, y, ALU.mult, ALU.mult), root)
            pe.wait(n)
            b, ps = self.bank()
            for t in range(2):
                mark = self.transpose(ps[:, t * P:(t + 1) * P], x[:, t * P:(t + 1) * P], mark=t == 1)
            o = rows[:, :, d * P:(d + 1) * P]
            done = act.run(lambda e, o=o, ps=ps: e.activation(
                o, ps[:, 0:S].rearrange("p (t n) -> p t n", t=2), ACT.Copy), mark, self.h_read)
            self.bank_free[b] = done
        self.sync.wait(self.sync.dma(out, rows, self.slot["out"], done))

    def emit(self):
        a = self.a
        self.setup()
        for i in range(2):
            w = [a[f"ffn1_w_{k}"][i] for k in ("gate", "up", "down")]
            self.ffn(*w, 0, S, self.add_scaled(0), ada=True)
            self.layer_norm(i * 3, permuted=i == 1)
            if i == 0:
                self.pool_mixer()
            else:
                self.dilated_mixer()
                self.const_read = self.dve_mark()
            self.layer_norm(i * 3 + 1)
            w = [a[f"ffn2_w_{k}"][i] for k in ("gate", "up", "down")]
            self.ffn(*w, 0, S, self.add_scaled(0), ada=True)
            self.layer_norm(i * 3 + 2)
        while self.ada_blocks or self.ada_bank:
            self.ada_step()
        self.finish_ada()
        self.load_rpb()
        ctx = self.m["tmp"][:, 2048:4096].rearrange("p (t d) -> p t d", t=2)
        landed = self.sync.dma(ctx, a["ctx_2"].rearrange("b (t p) d -> p (b t) d", p=P),
                               self.slot["tokens"], self.tmp_read)
        self.context_in(ctx, landed)
        for layer in range(DEPTH):
            last = layer == DEPTH - 1
            self.rms_mod(layer, 0, 0, 1, (0, 1))
            w = [a[f"ffn_w_{k}_2"][layer, 0] for k in ("gate", "up", "down")]
            self.ffn(*w, 0, 2 * S, self.add_gated(layer, 2, (0, 1)))
            self.rms_mod(layer, 1, 3, 4, (0, 1))
            if layer == 0:
                self.fourier_na_mixer(layer)
                self.const_read = [self.h_read, self.dve_mark()]
            else:
                self.mla_mixer(layer)
            streams = (0,) if last else (0, 1)
            self.rms_mod(layer, 2, 6, 7, streams)
            w = [a[f"ffn_w_{k}_2"][layer, 1] for k in ("gate", "up", "down")]
            self.ffn(*w, 0, S * len(streams), self.add_gated(layer, 8, streams))
        self.finish()

    def dve_mark(self):
        return (self.dve.sem, self.dve.count)

    def context_in(self, tok, landed):
        self.pe.wait(landed)
        for d in range(DC):
            b, ps = self.bank()
            for t in range(2):
                mark = self.transpose(ps[:, t * P:(t + 1) * P], tok[:, t, d * P:(d + 1) * P], mark=t == 1)
            x = self.m["x"][:, d, S:2 * S]
            done = self.dve.run(lambda e, x=x, ps=ps: e.tensor_copy(x, ps[:, 0:S]), mark)
            self.bank_free[b] = done
            self.x_ready[DC + d] = done
        self.tmp_read = [mark, self.rpb_stored]


def tables():
    f32 = np.float32
    t = np.arange(S)
    inverse = []
    for w in (2, 4, 8, 16):
        lo, hi = np.clip(t - w // 2, 0, S), np.clip(t + w // 2, 0, S)
        inverse.append(1.0 / (hi - lo))
    inverse = np.broadcast_to(np.concatenate(inverse)[None], (P, 4 * S))
    order = np.array([c * 16 + b * 4 + a for a in range(4) for b in range(4) for c in range(16)])
    dist = np.abs(order[:, None] - order[None, :]).astype(np.float64)
    same = lambda n: order[:, None] % n == order[None, :] % n
    d0 = np.where(dist <= 64, dist, FAR)
    d1, d2 = (np.where(same(n), dist, FAR) for n in (4, 16))
    tiles = []
    for i in range(2):
        r = slice(i * P, (i + 1) * P)
        tiles.append(np.concatenate([d0[r], d1[r, r], d2[r, r]], axis=1))
    block1 = np.concatenate([inverse] + tiles, axis=1).astype(f32)
    ang = 2 * np.pi * np.outer(np.arange(P), np.arange(P)) / P
    dft_d = np.concatenate([np.cos(ang), np.sin(ang)], axis=1) / np.sqrt(P)
    ang = 2 * np.pi * (np.outer(np.arange(S), np.arange(S)) % S) / S
    dft_n = np.stack([np.cos(ang), -np.sin(ang)], axis=1) / np.sqrt(S)
    dft_n = dft_n.reshape(2, P, 2, S).transpose(1, 0, 2, 3).reshape(P, 4 * S)
    col = t % GRID_W
    start = np.clip(col - 8, 0, GRID_W - 16)
    seen = (col[None, :] >= start[:, None]) & (col[None, :] < start[:, None] + 16)
    mask = np.where(seen, 0.0, -1e30).reshape(2, P, S).transpose(1, 0, 2).reshape(P, 2 * S)
    mixer = np.concatenate([dft_d, dft_n, mask], axis=1).astype(f32)
    inv = (10000.0 ** (-np.arange(0, 32, 2, dtype=f32) / f32(32))).astype(f32)
    row, colf = (t // GRID_W).astype(f32), (t % GRID_W).astype(f32)
    ar, ac = row[:, None] * inv[None], colf[:, None] * inv[None]
    angle = np.concatenate([ar, ar, ac, ac], axis=1)
    cos, sin = (np.concatenate([f(angle).T] * 2, axis=0) for f in (np.cos, np.sin))
    rot = np.zeros((ROPE, ROPE))
    for i in range(16):
        rot[16 + i, i] = rot[48 + i, 32 + i] = -1.0
        rot[i, 16 + i] = rot[32 + i, 48 + i] = 1.0
    rot2 = np.zeros((P, P))
    rot2[:ROPE, :ROPE] = rot2[ROPE:, ROPE:] = rot
    dup = np.zeros((P, 2 * P))
    dup[:ROPE] = np.concatenate([np.eye(ROPE), np.eye(ROPE), rot, rot], axis=1)
    rope = np.concatenate([cos, sin, rot2, dup], axis=1).astype(f32)
    return {"k_ident": np.eye(P, dtype=f32), "k_block1": block1, "k_mixer": mixer, "k_rope": rope}


NAMES = ["x", "ffn1_w_gate", "ffn1_w_up", "ffn1_w_down", "ffn2_w_gate", "ffn2_w_up", "ffn2_w_down",
         "ln_gain", "ln_bias", "pool_w_in", "pool_w_group", "pool_scale", "pool_w_out", "attn_w_qkv",
         "attn_w_out", "c_2", "ctx_2", "c_ctx_2", "ada_w_2", "ada_b_2", "norm_g_2", "ffn_w_gate_2",
         "ffn_w_up_2", "ffn_w_down_2", "ab_w_in_2", "ab_rpb_2", "ab_w_out_2", "mla_w_in_2", "mla_g_q_2",
         "mla_g_kv_2", "mla_w_uq_2", "mla_w_uk_2", "mla_w_uv_2", "mla_w_o_2", "final_g_2"]
IN_ROWS = ["ln_gain", "ln_bias", "norm_g_2", "pool_scale", "final_g_2", "mla_g_q_2", "mla_g_kv_2", "c_2",
           "c_ctx_2"]


def as_rows(ap):
    n = int(np.prod(ap.shape))
    return bass.AP(ap.tensor, 0, [[P, n // P], [1, P]])


def build(nc, shapes):
    a = {name: nc.dram_tensor(f"in_{name}", shape, F32, kind="ExternalInput").ap()
         for name, shape in shapes.items()}
    out = nc.dram_tensor("out_0", (1, S, D), F32, kind="ExternalOutput").ap()
    a["scratch"] = nc.dram_tensor("rpb_rows", (NA_HEADS * RPB_H, GRID_W, P), F32, kind="Internal").ap()
    for name in IN_ROWS:
        a[name] = as_rows(a[name])
    ada_b = as_rows(a["ada_b_2"])
    for layer in range(DEPTH):
        a[f"ada_b_2.{layer}"] = ada_b[layer * MODC:(layer + 1) * MODC, :]
    build_program(nc, a, out)
    return "out_0"


def kernel(**inputs):
    import concourse.bacc as bacc
    from concourse.bass_utils import run_bass_kernel_spmd

    nc = bacc.Bacc("TRN2", target_bir_lowering=False, num_devices=1)
    arrays = {name: np.ascontiguousarray(inputs[name]) for name in NAMES}
    arrays.update(tables())
    result = build(nc, {name: v.shape for name, v in arrays.items()})
    r = run_bass_kernel_spmd(nc, [{f"in_{n}": v for n, v in arrays.items()}], core_ids=[0])
    return r.results[0][result]
```

```python
from contextlib import ExitStack

import numpy as np

import concourse.bass as bass
from concourse import mybir

F32 = mybir.dt.float32
F32R = mybir.dt.float32r
ALU = mybir.AluOpType
ACT = mybir.ActivationFunctionType
AX_X = mybir.AxisListType.X

P = 128
S = 256
D = 1024
DC = D // P
F = 2816
FC = F // P
DEPTH = 2
ALPHA = (2.0 * DEPTH) ** 0.25
LN_EPS = 1e-5
RMS_EPS = 1e-6
HEAD = 64
HEADS = 16
DIL_GROUPS = 3
NA_HEADS = 8
MLA_HEADS = 8
NOPE = 128
ROPE = 64
Q_RANK = 384
N_MOD = 9
MODC = N_MOD * DC
GRID_W = 64
GRID_H = S // GRID_W
RPB_H, RPB_W = 15, 31
UNIT = 2048
RAW_SLOTS = 4
SPLIT_SLOTS = 3
H_CHUNKS = 24
FAR = 1e32


class Engine:

    def __init__(self, sem):
        self.sem, self.count, self.queue, self.seen = sem, 0, [], {}

    def wait(self, *marks):
        for mark in marks:
            if isinstance(mark, list):
                self.wait(*mark)
            elif mark is not None and self.seen.get(mark[0].name, 0) < mark[1]:
                self.seen[mark[0].name] = mark[1]
                self.queue.append(lambda e, m=mark: e.wait_ge(m[0], m[1]))

    def run(self, op, *marks):
        self.wait(*marks)
        self.count += 1
        self.queue.append(lambda e: op(e).then_inc(self.sem, 1))
        return (self.sem, self.count)

    def quiet(self, op, *marks):
        self.wait(*marks)
        self.queue.append(op)

    def dma(self, out, in_, slot, *marks):
        self.wait(*marks)
        slot[1] += 16
        self.queue.append(lambda e: e.dma_start(out, in_).then_inc(slot[0], 16))
        return (slot[0], slot[1])

    def play(self, e):
        for op in self.queue:
            op(e)


def build_program(nc, a, out):
    with ExitStack() as ctx:
        place = [nc.sbuf_base + (-nc.sbuf_base) % 64]

        def at(name, shape, dtype, offset):
            return nc.alloc_sbuf_tensor_at(name, shape, dtype, offset=offset)

        def room(nbytes):
            here = place[0]
            place[0] += nbytes + (-nbytes) % 64
            assert place[0] <= nc.sbuf_usable_end, (place, nc.sbuf_usable_end)
            return here

        def sb(name, shape, dtype=F32):
            return at(name, shape, dtype, room(4 * int(np.prod(shape[1:]))))

        m = {}
        m["x"] = sb("x", [P, DC, 2 * S])
        m["in_hi"] = sb("in_hi", [P, DC, 2 * S], F32R)
        m["in_lo"] = sb("in_lo", [P, DC, 2 * S], F32R)
        base = room(4 * 2 * H_CHUNKS * S)
        m["h_hi"] = at("h_hi", [P, H_CHUNKS * S], F32R, base)
        m["h_lo"] = at("h_lo", [P, H_CHUNKS * S], F32R, base + 4 * H_CHUNKS * S)
        m["work"] = at("work", [P, 2 * H_CHUNKS * S], F32, base)
        m["raw"] = [sb(f"raw{i}", [P, UNIT]) for i in range(RAW_SLOTS)]
        m["hi"] = [sb(f"hi{i}", [P, UNIT], F32R) for i in range(SPLIT_SLOTS)]
        m["lo"] = [sb(f"lo{i}", [P, UNIT], F32R) for i in range(SPLIT_SLOTS)]
        base = room(4 * DC * 2 * S)
        m["tmp"] = at("tmp", [P, DC * 2 * S], F32, base)
        m["latent"] = at("latent", [P, 2560], F32R, base + 4 * 1536)
        m["const"] = sb("const", [P, 2048])
        m["ident"] = sb("ident", [P, P])
        m["mean_w"] = sb("mean_w", [P, P])
        m["stat"] = sb("stat", [P, 4, 2 * S])
        m["cols"] = sb("cols", [P, 512])
        m["mod"] = sb("mod", [P, DEPTH, MODC, 2])
        m["gain"] = sb("gain", [P, DC, 2])
        m["c_split"] = sb("c_split", [P, DC, 4], F32R)
        m["c_silu"] = sb("c_silu", [P, DC, 2])
        m["soft"] = sb("soft", [P, 4, 4])
        m["rpb"] = sb("rpb", [NA_HEADS * RPB_H, P])
        m["ada_row"] = sb("ada_row", [4, 512])
        m["banks"] = [ctx.enter_context(nc.psum_tensor(f"bank{i}", [P, 512], F32)) for i in range(8)]

        names = "pe act dve pool sync".split()
        sems = {n: ctx.enter_context(nc.semaphore(f"{n}_done")) for n in names}
        for i in range(RAW_SLOTS):
            sems[f"raw{i}"] = ctx.enter_context(nc.semaphore(f"raw{i}_landed"))
        for n in ("consts", "rows", "tokens", "context", "table", "rpb", "bias", "out"):
            sems[n] = ctx.enter_context(nc.semaphore(f"{n}_landed"))

        plan = []
        Program(nc, a, out, m, sems, plan, True).emit()
        program = Program(nc, a, out, m, sems, plan, False)
        program.emit()

        block = ctx.enter_context(nc.Block())
        block.sync(program.sync.play)
        block.gpsimd(program.pool.play)
        block.scalar(program.act.play)
        block.vector(program.dve.play)
        block.tensor(program.pe.play)


class Program:
    def __init__(self, nc, a, out, m, sems, plan, dry):
        self.nc, self.a, self.out, self.m, self.plan, self.dry = nc, a, out, m, plan, dry
        self.pe, self.act, self.dve, self.pool, self.sync = (
            Engine(sems[n]) for n in ("pe", "act", "dve", "pool", "sync"))
        self.slot = {n: [sems[n], 0] for n in sems}
        self.loaded = self.split = self.taken = 0
        self.raw_landed, self.hi_done, self.lo_done, self.used = {}, {}, {}, {}
        self.next_bank, self.bank_free = 0, [None] * 8
        self.ada_blocks, self.ada_pending = [], None
        self.x_ready = [None] * (2 * DC)
        self.in_ready = []
        self.norm, self.norm_chunk_read = None, {}
        self.norm_added, self.norm_sum = {}, {}
        self.norming = None
        self.in_read = None
        self.h_read = None
        self.tmp_read = []
        self.stat_read = []

    def load_unit(self, i):
        parts, A, B = self.plan[i]
        before = i - RAW_SLOTS
        marks = [self.hi_done[before], self.lo_done[before]] if before >= 0 else []
        for first, src in parts:
            n = src.shape[1] * src.shape[2]
            dst = self.m["raw"][i % RAW_SLOTS][:, first:first + n].rearrange("p (a b) -> p a b", b=src.shape[2])
            self.raw_landed[i] = self.sync.dma(dst, src, self.slot[f"raw{i % RAW_SLOTS}"], *marks)

    def split_unit(self, i):
        _, A, B = self.plan[i]
        n, s = A * B, i % SPLIT_SLOTS
        raw, hi, lo = self.m["raw"][i % RAW_SLOTS], self.m["hi"][s], self.m["lo"][s]
        before = self.used[i - SPLIT_SLOTS] if i >= SPLIT_SLOTS else None
        self.hi_done[i] = self.act.run(
            lambda e: e.activation(hi[:, 0:n], raw[:, 0:n], ACT.Copy), self.raw_landed[i], before)
        self.lo_done[i] = self.dve.run(
            lambda e: e.tensor_tensor(lo[:, 0:n], raw[:, 0:n], hi[:, 0:n].bitcast(F32), ALU.subtract),
            self.raw_landed[i], self.hi_done[i], before)

    def weights(self, src, parts=None, ahead=SPLIT_SLOTS):
        A, B = src.shape[1], src.shape[2]
        assert A * B <= UNIT and src.shape[0] == P
        i = self.taken
        self.taken += 1
        if self.dry:
            self.plan.append((parts or [(0, src)], A, B))
        else:
            assert self.plan[i][1:] == (A, B)
            self.split_until(i + ahead)
            self.pe.wait(self.hi_done[i], self.lo_done[i])
        s = i % SPLIT_SLOTS
        hi, lo = (self.m[k][s][:, 0:A * B].rearrange("p (a b) -> p a b", a=A) for k in ("hi", "lo"))
        return i, hi, lo

    def split_until(self, end):
        while not self.dry and self.split < min(end, len(self.plan)):
            while self.loaded < min(self.split + RAW_SLOTS, len(self.plan)):
                self.load_unit(self.loaded)
                self.loaded += 1
            self.split_unit(self.split)
            self.split += 1

    def bank(self):
        b = self.next_bank
        self.next_bank = (b + 1) % 8
        assert self.bank_free[b] != "held"
        self.pe.wait(self.bank_free[b])
        self.bank_free[b] = "held"
        return b, self.m["banks"][b]

    def mm(self, out, lhs, rhs, start=True, stop=True, mark=False):
        op = lambda e: e.matmul(out, lhs, rhs, start=start, stop=stop)
        return self.pe.run(op) if mark else self.pe.quiet(op)

    def mm3(self, out, w, x, start, stop, mark=False):
        self.mm(out, w[0], x[0], start=start, stop=False)
        self.mm(out, w[0], x[1], start=False, stop=False)
        return self.mm(out, w[1], x[0], start=False, stop=stop, mark=mark)

    def transpose(self, out, in_, mark=False):
        n = in_.shape[0]
        op = lambda e: e.transpose(out, in_, self.m["ident"][0:n, 0:n])
        return self.pe.run(op) if mark else self.pe.quiet(op)

    def project(self, w_dram, n_out, x, N, evacuate, backwards=False):
        K = w_dram.shape[0] // P
        view = w_dram.rearrange("(k p) n -> p k n", p=P)
        width = min(2 * P, n_out)
        for c0 in sorted(range(0, n_out, width), reverse=backwards):
            if self.norming and N == 2 * S:
                unit, hi, lo = self.weights(view[:, :, c0:c0 + width], ahead=SPLIT_SLOTS - 1)
                taken = self.start_product(unit, hi, lo)
            else:
                unit, hi, lo = self.weights(view[:, :, c0:c0 + width])
                taken = self.product(unit, hi, lo, width, K, x, N, self.advance if self.norming else None)
            for i, (b, ps, mark) in enumerate(taken):
                evacuate(c0 // P + i, b, ps, mark)
        return mark

    def project_gated(self, w_dram, layer, slot):
        x, x0, x1 = (self.stage_in(t0, n) for t0, n in ((0, 2 * S), (0, S), (S, S)))
        view = w_dram.rearrange("(k p) n -> p k n", p=P)
        residual = self.add_gated(layer, slot, (0, 1))

        def add(d, b, ps, mark):
            self.bank_free[b] = residual(d, ps, mark)

        self.project(w_dram[:, 0:D - 2 * P], D - 2 * P, x, 2 * S, add)
        unit, hi, lo = self.weights(view[:, :, D - 2 * P:])
        for s in (0, 1):
            residual = self.add_gated(layer, slot, (s,))
            taken = self.open_banks(2 * P)
            marks = self.accumulate(hi, lo, taken, DC, (x0, x1)[s], 0, S,
                                    self.start_norm if s else None)
            self.in_read = marks[1]
            for j in (0, 1):
                self.bank_free[taken[j][2]] = residual(DC - 2 + j, taken[j][3], marks[j])
        self.used[unit] = marks[1]
        self.advance()

    def open_banks(self, width):
        return [(j, min(P, width - j)) + self.bank() for j in range(0, width, P)]

    def accumulate(self, hi, lo, taken, K, x, t0, n, midway=None):
        marks = []
        for k in range(K):
            if k == K // 2 and midway:
                midway()
            x_k = x(k)
            for j, w, b, ps in taken:
                mark = self.mm3(ps[0:w, t0:t0 + n], (hi[:, k, j:j + w], lo[:, k, j:j + w]), x_k,
                                k == 0, k == K - 1, mark=k == K - 1)
                if k == K - 1:
                    marks.append(mark)
        return marks

    def product(self, unit, hi, lo, width, K, x, N, midway=None):
        taken = self.open_banks(width)
        marks = self.accumulate(hi, lo, taken, K, x, 0, N, midway)
        self.used[unit] = marks[-1]
        return [(t[2], t[3], mark) for t, mark in zip(taken, marks)]

    def start_product(self, unit, hi, lo):
        taken = self.open_banks(2 * P)
        self.accumulate(hi, lo, taken, DC, self.stage_in(0, S), 0, S, self.advance)
        marks = self.accumulate(hi, lo, taken, DC, self.stage_in(S, S), S, S)
        self.used[unit] = marks[-1]
        return [(t[2], t[3], mark) for t, mark in zip(taken, marks)]

    def start_norm(self):
        self.norming = self.norm[2]
        self.advance()

    def advance(self):
        if next(self.norming, "over") == "over":
            self.norming = None

    def stage_in(self, lo_t, n):
        hi, lo = self.m["in_hi"], self.m["in_lo"]
        streams = range(lo_t // S, (lo_t + n) // S)

        def chunk(k):
            ready = self.in_ready[k]
            self.pe.wait([ready[s] for s in streams] if isinstance(ready, dict) else ready)
            return hi[:, k, lo_t:lo_t + n], lo[:, k, lo_t:lo_t + n]
        return chunk

    def setup(self):
        m, a, act, dve, pe, sync, pool = self.m, self.a, self.act, self.dve, self.pe, self.sync, self.pool
        tok = m["tmp"][:, :].rearrange("p (s t d) -> p s t d", s=2, t=2)
        consts = sync.dma(m["ident"][:, :], a["k_ident"], self.slot["consts"])
        x_in = sync.dma(tok[:, 0, :, :], a["x"].rearrange("b (t p) d -> p (b t) d", p=P), self.slot["tokens"])
        mean = dve.run(lambda e: e.memset(m["mean_w"][:, :], 1.0 / D))
        rows = m["work"]
        plan = [
            [(0, "ln_gain", 48), (48, "ln_bias", 48)],
            [(0, "norm_g_2", 48), (48, "pool_scale", 8), (56, "final_g_2", 8), (64, "mla_g_q_2", 3),
             (67, "mla_g_kv_2", 1), (68, "c_2", 8), (76, "c_ctx_2", 8)],
            [(0, "ada_b_2.0", 72)],
            [(0, "ada_b_2.1", 72)],
        ]
        n_rows, landed = [], None
        for g, parts in enumerate(plan):
            for r0, name, n in parts:
                src = a[name]
                landed = act.dma(rows[r0:r0 + n, g * P:(g + 1) * P], src, self.slot["rows"])
            n_rows.append(r0 + n)
        self.context_landed = act.dma(tok[:, 1, :, :], a["ctx_2"].rearrange("b (t p) d -> p (b t) d", p=P),
                                      self.slot["context"])
        self.const_tables = act.dma(m["const"][:, :], a["k_block1"], self.slot["table"])
        pe.wait(consts)
        self.transpose_in(tok[:, 0], x_in, 0)
        pe.wait(landed)
        self.col = {}
        b, ps = self.bank()
        for g, n in enumerate(n_rows):
            mark = self.transpose(ps[:, g * P:g * P + n], rows[0:n, g * P:(g + 1) * P], mark=g == 3)
            for r0, name, k in plan[g]:
                self.col[name] = g * P + r0
        read = act.run(lambda e: e.activation(m["cols"][:, 0:96], ps[:, 0:96], ACT.Copy), mark)
        read = act.run(lambda e: e.activation(m["cols"][:, 128:212], ps[:, 128:212], ACT.Copy))
        for g in (2, 3):
            read = act.run(lambda e, g=g: e.activation(
                m["cols"][:, g * P:g * P + 72], ps[:, g * P:g * P + 72], ACT.Copy))
        self.bank_free[b] = read
        self.cols_ready = read
        c0 = self.col["c_2"]
        c_view = m["cols"][:, c0:c0 + 16].rearrange("p (v d) -> p d v", v=2)
        silu = act.run(lambda e: e.activation(m["c_silu"][:, :, :], c_view, ACT.Silu), read)
        hi = act.run(lambda e: e.activation(m["c_split"][:, :, 0:2], m["c_silu"][:, :, :], ACT.Copy), silu)
        self.c_ready = dve.run(lambda e: e.tensor_tensor(
            m["c_split"][:, :, 2:4], m["c_silu"][:, :, :], m["c_split"][:, :, 0:2].bitcast(F32),
            ALU.subtract), hi)
        self.load_rpb()
        self.mean_ready = mean
        self.h_read = mark
        self.ada_blocks = [(layer, n) for layer in range(DEPTH) for n in range(N_MOD * D // 512)]
        self.ada_bank = None
        self.ada_free = None
        self.mod_ready = [None] * DEPTH

    def transpose_in(self, tok, landed, stream):
        m, t0 = self.m, stream * S
        self.pe.wait(landed)
        for d in range(DC):
            b, ps = self.bank()
            for t in range(2):
                mark = self.transpose(ps[:, t * P:(t + 1) * P], tok[:, t, d * P:(d + 1) * P], mark=t == 1)
            x = m["x"][:, d, t0:t0 + S]
            done = self.dve.run(lambda e, x=x, ps=ps: e.tensor_copy(x, ps[:, 0:S]), mark)
            self.bank_free[b] = self.x_ready[stream * DC + d] = done
            if stream == 0:
                self.in_ready.append(self.split_act(d, t0, x, done))
        self.tmp_read = self.tmp_read + [mark]

    def split_act(self, d, t0, x, mark, n=S):
        hi, lo = (self.m[k][:, d, t0:t0 + n] for k in ("in_hi", "in_lo"))
        h = self.act.run(lambda e: e.activation(hi, x, ACT.Copy), mark, self.in_read)
        return self.dve.run(lambda e: e.tensor_tensor(lo, x, hi.bitcast(F32), ALU.subtract), h)

    def ada_step(self):
        m, pe, act, dve = self.m, self.pe, self.act, self.dve
        if self.ada_bank is None:
            if not self.ada_blocks:
                return
            self.ada_at, self.ada_bank = self.ada_blocks.pop(0), self.bank()
            half = 0
        else:
            half = 1
        (layer, n), (b, ps) = self.ada_at, self.ada_bank
        view = self.a["ada_w_2"][layer].rearrange("(k p) n -> p k n", p=P)
        pe.wait(self.c_ready)
        unit, hi, lo = self.weights(view[:, 4 * half:4 * half + 4, 512 * n:512 * n + 512])
        for k in range(4):
            c = m["c_split"][:, 4 * half + k, :]
            last = half == 1 and k == 3
            self.mm(ps[0:4, :], c, hi[:, k, :], start=half == 0 and k == 0, stop=False)
            mark = self.mm(ps[0:4, :], c, lo[:, k, :], start=False, stop=last, mark=k == 3)
        self.used[unit] = mark
        if half == 0:
            return
        self.ada_bank = None
        self.finish_ada()
        row = m["ada_row"]
        copied = act.run(lambda e: e.activation(row[:, :], ps[0:4, :], ACT.Copy), mark, self.ada_free)
        self.bank_free[b] = copied
        self.ada_pending = (layer, n, row, copied)

    def finish_ada(self):
        if self.ada_pending is None:
            return
        m, dve = self.m, self.dve
        layer, n, row, copied = self.ada_pending
        self.ada_pending = None
        self.pe.wait(copied)
        b, ps = self.bank()
        for j in range(4):
            mark = self.transpose(ps[:, 4 * j:4 * j + 4], row[:, j * P:(j + 1) * P], mark=j == 3)
        self.ada_free = mark
        v = ps[:, 0:16].rearrange("p (j c) -> p j c", c=4)
        mod = m["mod"][:, layer, 4 * n:4 * n + 4, :]
        bias = self.col[f"ada_b_2.{layer}"] + 4 * n
        bias = m["cols"][:, bias:bias + 4][:, :, None].broadcast_to([P, 4, 2])
        one = dve.run(lambda e: e.tensor_tensor(mod, v[:, :, 0:2], bias, ALU.add), mark, self.cols_ready)
        two = dve.run(lambda e: e.tensor_tensor(mod, v[:, :, 2:4], mod, ALU.add), one)
        self.bank_free[b] = two
        self.mod_ready[layer] = two

    def ffn(self, w_gate, w_up, w_down, N, residual, ada=False, extra=None, before_down=None,
            start=None):
        m, act, dve, pe = self.m, self.act, self.dve, self.pe
        x = self.stage_in(0, N)
        gate, up = (w.rearrange("(k p) n -> p k n", p=P) for w in (w_gate, w_up))
        down = w_down.rearrange("(f p) n -> p f n", p=P)
        h_hi, h_lo = (m[k][:, :].rearrange("p (f t) -> p f t", t=N) for k in ("h_hi", "h_lo"))
        room = H_CHUNKS * S // N
        groups = [(0, FC)] if FC <= room else [(0, room), (room, FC)]
        gates = m["stat"]
        split_h = []
        for first, last in groups:
            h_ready = {}
            for f0 in range(first, last, 2):
                products = start(gate[:, :, 0:2 * P], up[:, :, 0:2 * P]) if start and f0 == 0 else []
                for w in (gate, up)[len(products):]:
                    if self.norming:
                        unit, hi, lo = self.weights(w[:, :, 0:2 * P], ahead=SPLIT_SLOTS - 1)
                        products.append(self.start_product(unit, hi, lo))
                        continue
                    unit, hi, lo = self.weights(w[:, :, f0 * P:f0 * P + 2 * P])
                    products.append(self.product(unit, hi, lo, 2 * P, DC, x, N))
                    if ada and w is gate:
                        self.ada_step()
                mark = products[1][1][2]
                self.in_read = mark
                for f in (f0, f0 + 1):
                    (bg, g, g_mark), (bu, u, u_mark) = products[0][f - f0], products[1][f - f0]
                    s = gates[:, f % 2, 0:N]
                    h32 = gates[:, 2 + f % 2, 0:N]
                    dh, dl = h_hi[:, f - first, :], h_lo[:, f - first, :]
                    slot_read = split_h[-2:-1] if len(split_h) > 1 else self.stat_read
                    silu = act.run(lambda e, s=s, g=g: e.activation(s, g[:, 0:N], ACT.Silu), g_mark,
                                   slot_read)
                    self.bank_free[bg] = silu
                    prod = dve.run(lambda e, s=s, u=u, o=h32: e.scalar_tensor_tensor(
                        o, s, 0.5, u[:, 0:N], ALU.mult, ALU.mult), silu, u_mark, slot_read)
                    self.bank_free[bu] = prod
                    hi_w = act.run(lambda e, o=dh, i=h32: e.activation(o, i, ACT.Copy), prod, self.h_read)
                    lo_w = dve.run(lambda e, o=dl, i=h32, h=dh: e.tensor_tensor(
                        o, i, h.bitcast(F32), ALU.subtract), hi_w, self.h_read)
                    split_h.append(lo_w)
                    h_ready[f] = [hi_w, lo_w]
                if ada:
                    self.ada_step()
                if extra and f0 == 4:
                    extra()
            self.stat_read = split_h[-1:]
            if last == FC:
                act.quiet(lambda e: e.preload_act_table_set("natural_log_exp_and_others"))
            if before_down:
                before_down()
            parts = [(f, min(f + 8, last)) for f in range(first, last, 8)]
            by_stream = DC - 2 if N == 2 * S and last == FC else DC
            for d0 in range(0, by_stream, 2):
                taken = [self.bank(), self.bank()]
                for f0, f1 in parts:
                    unit, hi, lo = self.weights(down[:, f0:f1, d0 * P:d0 * P + 2 * P])
                    for d in range(2):
                        for f in range(f0, f1):
                            pe.wait(*h_ready[f])
                            mark = self.mm3(taken[d][1][:, 0:N],
                                            (hi[:, f - f0, d * P:d * P + P], lo[:, f - f0, d * P:d * P + P]),
                                            (h_hi[:, f - first, :], h_lo[:, f - first, :]),
                                            f == first, f == last - 1, mark=f == f1 - 1)
                        if f1 == last:
                            b, ps = taken[d]
                            self.bank_free[b] = residual(d0 + d, ps, mark, last == FC)
                    self.used[unit] = mark
            if by_stream < DC:
                parts = [(first, last - 7), (last - 7, last)]
                units = [self.weights(down[:, f0:f1, by_stream * P:], ahead=SPLIT_SLOTS - i)
                         for i, (f0, f1) in enumerate(parts)]
                for s in (0, 1):
                    taken = [self.bank(), self.bank()]
                    for (f0, f1), (unit, hi, lo) in zip(parts, units):
                        for d in range(2):
                            for f in range(f0, f1):
                                mark = self.mm3(
                                    taken[d][1][:, 0:S],
                                    (hi[:, f - f0, d * P:d * P + P], lo[:, f - f0, d * P:d * P + P]),
                                    [h[:, f - first, s * S:s * S + S] for h in (h_hi, h_lo)],
                                    f == first, f == last - 1, mark=f == f1 - 1)
                            if f1 == last:
                                b, ps = taken[d]
                                self.bank_free[b] = residual(by_stream + d, ps, mark, True, (s,))
                        if s == 1:
                            self.used[unit] = mark
                            if f0 == parts[0][0]:
                                self.start_norm()
                self.advance()
            self.h_read = mark

    def add_scaled(self, t0):
        def residual(d, ps, mark, last=True):
            x = self.m["x"][:, d, t0:t0 + S]
            done = self.dve.run(lambda e: e.scalar_tensor_tensor(
                x, x, ALPHA, ps[:, 0:S], ALU.mult, ALU.add), mark, self.x_ready[d])
            self.x_ready[d] = done
            self.feed_norm(d)
            return done
        return residual

    def add_gated(self, layer, slot, streams):
        def residual(d, ps, mark, last=True, part=streams):
            for s in part:
                x = self.m["x"][:, d, s * S:s * S + S]
                gate = self.m["mod"][:, layer, slot * DC + d, s:s + 1]
                p = ps[:, (s - part[0]) * S:(s - part[0] + 1) * S]
                done = self.dve.run(lambda e, x=x, g=gate, p=p: e.scalar_tensor_tensor(
                    x, p, g, x, ALU.mult, ALU.add), mark, self.x_ready[s * DC + d], self.mod_ready[layer])
                self.x_ready[s * DC + d] = done
            if last:
                self.feed_norm(d, part)
            return done
        return residual

    def norm_of(self, kind, streams=(0,), norming=None):
        self.norm = (kind, streams, norming)

    def feed_norm(self, d, streams=(0,)):
        m, act, dve = self.m, self.act, self.dve
        kind, all_streams, _ = self.norm
        t0, N = streams[0] * S, S * len(streams)
        tmp = m["tmp"][:, :].rearrange("p (d t) -> p d t", d=DC)
        ready = [self.x_ready[s * DC + d] for s in streams]
        x = m["x"][:, :, t0:t0 + N]
        added_before = [self.norm_added.get(s) for s in streams]
        if kind == "rms":
            total = tmp[:, 0, t0:t0 + N]
            free = [self.tmp_read, self.norm_chunk_read.get(d)]
            added = act.run(lambda e: e.activation(tmp[:, d, t0:t0 + N], x[:, d, :], ACT.Square), ready, free)
            if d:
                added = dve.run(lambda e: e.tensor_tensor(total, total, tmp[:, d, t0:t0 + N], ALU.add), added,
                                added_before)
        elif d:
            total = tmp[:, 0, S:2 * S]
            first = x[:, 0, :] if d == 1 else total
            added = dve.run(lambda e: e.tensor_tensor(total, first, x[:, d, :], ALU.add), ready,
                            self.tmp_read, added_before if d > 1 else self.x_ready[0])
        else:
            return
        for s in streams:
            self.norm_added[s] = added
        if d == DC - 1 and len(all_streams) == 1:
            self.mean_of(all_streams[0], total)

    def mean_of(self, stream, total):
        b, ps = self.bank()
        self.pe.wait(self.norm_added[stream], self.mean_ready)
        mark = self.mm(ps[:, 0:S], self.m["mean_w"][:, :], total, mark=True)
        self.norm_sum[stream] = (b, ps, mark)
        self.norm_chunk_read = {}

    def inv_root(self, b, ps, N, mark, factor, eps, silu_next=False, t0=0, meanwhile=None):
        m, act, dve = self.m, self.act, self.dve
        v, y, t = (m["stat"][:, i, t0:t0 + N] for i in range(3))
        var = dve.run(lambda e: e.tensor_scalar(v, ps[:, 0:N], factor, eps, ALU.mult, ALU.add),
                      mark, self.stat_read)
        self.bank_free[b] = var
        ln = act.run(lambda e: e.activation(y, v, ACT.Ln), var)
        ex = act.run(lambda e: e.activation(y, y, ACT.Exp, scale=-0.5), ln)
        if silu_next:
            act.quiet(lambda e: e.preload_act_table_set("silu_and_others"))
        if meanwhile:
            meanwhile()
        n1 = dve.run(lambda e: e.scalar_tensor_tensor(t, v, -0.5, y, ALU.mult, ALU.mult), ex)
        n2 = dve.run(lambda e: e.tensor_tensor(t, t, y, ALU.mult), n1)
        return y, dve.run(lambda e: e.scalar_tensor_tensor(y, t, 1.5, y, ALU.add, ALU.mult), n2)

    def layer_norm(self, index, permuted=False, split=True, meanwhile=None):
        m, act, dve, pe = self.m, self.act, self.dve, self.pe
        x = m["x"][:, :, 0:S]
        tmp = m["tmp"][:, :].rearrange("p (d t) -> p d t", d=DC)
        centred, square = tmp[:, :, 0:S], tmp[:, :, S:2 * S]
        b, ps, mark = self.norm_sum[0]
        b2, ps2 = self.bank()
        step = 2
        for r0 in range(0, DC, step):
            r = slice(r0, r0 + step)
            mean = ps[:, 0:S][:, None, :].broadcast_to([P, step, S])
            sub = dve.run(lambda e, r=r, mean=mean: e.tensor_tensor(
                centred[:, r, :], x[:, r, :], mean, ALU.subtract), mark, self.tmp_read)
            sq = act.run(lambda e, r=r: e.activation(square[:, r, :], centred[:, r, :], ACT.Square), sub)
            pe.wait(sq)
            for d in range(r0, r0 + step):
                var = self.mm(ps2[:, 0:S], m["mean_w"][:, :], square[:, d, :], d == 0, d == DC - 1,
                              mark=d == DC - 1)
        self.bank_free[b] = sub
        if meanwhile:
            meanwhile()
        y, root = self.inv_root(b2, ps2, S, var, 1.0, LN_EPS, silu_next=split and index % 3 != 0)
        if split:
            self.in_ready = []
        low_parts = []
        for d in range(DC):
            gain = m["cols"][:, self.col["ln_gain"] + index * DC + d:][:, 0:1]
            bias = m["cols"][:, self.col["ln_bias"] + index * DC + d:][:, 0:1]
            c, o = centred[:, d, :], x[:, d, :]
            hi, lo = m["in_hi"][:, d, 0:S], m["in_lo"][:, d, 0:S]
            if permuted:
                c_, o_ = (v.rearrange("p (c b a) -> p c b a", a=4, b=4) for v in (c, o))
                hi, lo = (v.rearrange("p (a b c) -> p c b a", a=4, b=4) for v in (hi, lo))
            else:
                c_, o_ = c, o
            normed = dve.run(lambda e, c=c: e.tensor_tensor(c, c, y, ALU.mult), root)
            high = None
            if split:
                high = act.run(lambda e, hi=hi, c=c_, g=gain, b=bias: e.activation(
                    hi, c, ACT.Identity, scale=g, bias=b), normed, self.in_read, self.cols_ready)
            if d % 2 == 0:
                full = dve.run(lambda e, o=o, c=c, g=gain, b=bias: e.tensor_scalar(
                    o, c, g, b, ALU.mult, ALU.add), normed, self.cols_ready)
            else:
                full = act.run(lambda e, o=o, c=c, g=gain, b=bias: e.activation(
                    o, c, ACT.Identity, scale=g, bias=b), normed, self.cols_ready)
            self.x_ready[d] = full
            self.norm_chunk_read[d] = [full, high, var]
            low_parts.append(lambda lo=lo, o=o_, hi=hi, full=full, high=high: self.in_ready.append(
                dve.run(lambda e: e.tensor_tensor(lo, o, hi.bitcast(F32), ALU.subtract),
                        full, high, self.in_read)))
            if split and d:
                low_parts[d - 1]()
            if not split and d > 1:
                self.feed_norm(d - 2)
        self.stat_read = [normed]
        self.tmp_read = [full, high, normed]
        if split:
            low_parts[d]()
        else:
            self.feed_norm(d - 1)
            self.feed_norm(d)

    def rms_gain(self, layer, i, scale):
        g0 = self.col["norm_g_2"] + (layer * 3 + i) * DC
        norm_g = self.m["cols"][:, g0:g0 + DC][:, :, None].broadcast_to([P, DC, 2])
        gain, scales = self.m["gain"], self.m["mod"][:, layer, scale * DC:scale * DC + DC, :]
        return self.dve.run(lambda e: e.scalar_tensor_tensor(
            gain[:, :, :], scales, 1.0, norm_g, ALU.add, ALU.mult),
            self.mod_ready[layer], self.cols_ready)

    def rms_chunks(self, layer, shift, s, chunks, ready, *marks):
        m, act, dve = self.m, self.act, self.dve
        tmp = m["tmp"][:, :].rearrange("p (d t) -> p d t", d=DC)
        tok = slice(s * S, s * S + S)
        y = m["stat"][:, 1, tok]
        high = {}

        def low_part(d):
            o, hi, lo = (v[:, d, tok] for v in (tmp, m["in_hi"], m["in_lo"]))
            sh = m["mod"][:, layer, shift * DC + d, s:s + 1]
            ready[d][s] = dve.run(lambda e: e.scalar_tensor_tensor(
                lo, o, sh, hi.bitcast(F32), ALU.add, ALU.subtract), high[d], self.in_read)

        for d in chunks:
            x, o, hi = (v[:, d, tok] for v in (m["x"], tmp, m["in_hi"]))
            g, sh = m["gain"][:, d, s:s + 1], m["mod"][:, layer, shift * DC + d, s:s + 1]
            scaled = dve.run(lambda e, o=o, x=x, g=g: e.scalar_tensor_tensor(
                o, x, g, y, ALU.mult, ALU.mult), *marks)
            high[d] = act.run(lambda e, hi=hi, o=o, sh=sh: e.activation(
                hi, o, ACT.Identity, bias=sh), scaled, self.in_read)
            if d - 1 in high:
                low_part(d - 1)
        low_part(d)
        return ready[d][s]

    def rms_both(self, layer, i, shift, scale):
        total = self.m["tmp"][:, 0:2 * S]
        silu_next = i != 1
        gained = self.rms_gain(layer, i, scale)
        ready = [{} for _ in range(DC)]
        self.mean_of(0, total[:, 0:S])
        b, ps, mark0 = self.norm_sum[0]
        y, root0 = self.inv_root(b, ps, S, mark0, 1.0, RMS_EPS)
        self.rms_chunks(layer, shift, 0, (0, 1), ready, root0, mark0, gained)
        yield
        self.in_ready = ready
        self.rms_chunks(layer, shift, 0, (2, 3), ready, root0, mark0, gained)
        yield
        self.mean_of(1, total[:, S:])
        b, ps, mark1 = self.norm_sum[1]
        y, root1 = self.inv_root(b, ps, S, mark1, 1.0, RMS_EPS, silu_next=silu_next, t0=S,
                                 meanwhile=lambda: self.rms_chunks(layer, shift, 0, (4, 5), ready, root0))
        self.rms_chunks(layer, shift, 0, (6, 7), ready, root0)
        done = self.rms_chunks(layer, shift, 1, range(DC), ready, root1, mark1)
        self.stat_read = self.tmp_read = [done]

    def rms_mod(self, layer, i, shift, scale, s=0, silu_next=True):
        gained = self.rms_gain(layer, i, scale)
        b, ps, mark = self.norm_sum[s]
        y, root = self.inv_root(b, ps, S, mark, 1.0, RMS_EPS, silu_next=silu_next, t0=s * S)
        if not isinstance(self.in_ready[0], dict):
            self.in_ready = [{} for _ in range(DC)]
        done = self.rms_chunks(layer, shift, s, range(DC), self.in_ready, root, mark, gained)
        self.stat_read = self.tmp_read = [done]

    def pool_mixer(self):
        m, act, dve, pe, a = self.m, self.act, self.dve, self.pe, self.a
        PAD, W = 8, S + 16
        padded = m["tmp"][:, 0:DC * W].rearrange("p (d t) -> p d t", d=DC)
        sums = m["tmp"][:, DC * W:DC * W + 4 * W].rearrange("p (i d t) -> p i d t", i=2, d=2)
        mean = m["work"][:, 0:0 + 2 * S]
        zero = dve.run(lambda e: e.memset(padded[:, :, 0:PAD], 0.0), self.tmp_read)
        zero = dve.run(lambda e: e.memset(padded[:, :, PAD + S:], 0.0))
        u_ready = {}

        def keep(d, b, ps, mark):
            u_ready[d] = act.run(lambda e: e.activation(padded[:, d, PAD:PAD + S], ps[:, 0:S], ACT.Copy),
                                 mark, self.tmp_read)
            self.bank_free[b] = u_ready[d]

        self.in_read = self.project(a["pool_w_in"][0], D, self.stage_in(0, S), S, keep, True)
        h_hi, h_lo = (m[k][:, :].rearrange("p (f t) -> p f t", t=S) for k in ("h_hi", "h_lo"))
        inverse = m["const"][:, 0:4 * S].rearrange("p (g t) -> p g t", g=4)
        mixed_ready = {}
        prev = [self.stat_read, self.stat_read]
        for g in reversed(range(4)):
            stat = m["stat"][:, g % 2, :].rearrange("p (d t) -> p d t", d=2)
            src, half = padded[:, 2 * g:2 * g + 2, :], 1
            n = W
            step = zero
            for i in range(g + 1):
                n -= half
                dst = sums[:, i % 2, :, 0:n]
                step = dve.run(lambda e, d=dst, s=src, n=n, h=half: e.tensor_tensor(
                    d, s[:, :, 0:n], s[:, :, h:h + n], ALU.add), step, u_ready[2 * g + 1])
                src, half = sums[:, i % 2], half * 2
            first = PAD - half // 2
            inv = inverse[:, g, :][:, None, :].broadcast_to([P, 2, S])
            u = padded[:, 2 * g:2 * g + 2, PAD:PAD + S]
            step = dve.run(lambda e, s=src, f=first, inv=inv, o=stat: e.tensor_tensor(
                o, s[:, :, f:f + S], inv, ALU.mult), step, self.const_tables, prev[g % 2])
            step = dve.run(lambda e, u=u, o=stat: e.tensor_tensor(o, o, u, ALU.subtract), step)
            hi, lo = h_hi[:, 2 * g:2 * g + 2, :], h_lo[:, 2 * g:2 * g + 2, :]
            high = act.run(lambda e, hi=hi, i=stat: e.activation(hi, i, ACT.Copy), step, self.h_read)
            low = dve.run(lambda e, lo=lo, hi=hi, i=stat: e.tensor_tensor(
                lo, i, hi.bitcast(F32), ALU.subtract), high, self.h_read)
            prev[g % 2] = [high, low]
            mixed_ready[g] = low
        self.tmp_read = [step]
        view = a["pool_w_group"][0].rearrange("g (c p) e -> p (g c) e", p=P)
        unit, whi, wlo = self.weights(view)
        y_ready = {}
        for e_ in reversed(range(DC)):
            g, j = e_ // 2, (e_ % 2) * P
            pe.wait(mixed_ready[g])
            b, ps = self.bank()
            for c in range(2):
                k = 2 * g + c
                mark = self.mm3(ps[:, 0:S], (whi[:, k, j:j + P], wlo[:, k, j:j + P]),
                                (h_hi[:, k, :], h_lo[:, k, :]), c == 0, c == 1, mark=c == 1)
            t = m["stat"][:, 2 + e_ % 2, 0:S]
            scale = m["cols"][:, self.col["pool_scale"] + e_:][:, 0:1]
            hi, lo = h_hi[:, DC + e_, :], h_lo[:, DC + e_, :]
            scaled = act.run(lambda e, t=t, ps=ps, s=scale: e.activation(t, ps[:, 0:S], ACT.Copy, scale=s),
                             mark, prev[0], y_ready.get(e_ + 2), self.cols_ready)
            self.bank_free[b] = scaled
            high = act.run(lambda e, hi=hi, t=t: e.activation(hi, t, ACT.Copy), scaled)
            y_ready[e_] = dve.run(lambda e, lo=lo, t=t, hi=hi: e.tensor_tensor(
                lo, t, hi.bitcast(F32), ALU.subtract), high)
        self.used[unit] = mark
        self.stat_read = [y_ready[0]]
        residual = self.add_scaled(0)

        def add(d, b, ps, mark):
            self.bank_free[b] = residual(d, ps, mark)

        def y(k):
            pe.wait(y_ready[k])
            return h_hi[:, DC + k, :], h_lo[:, DC + k, :]

        self.h_read = self.project(a["pool_w_out"][0], D, y, S, add)

    def attend(self, items):
        m, act, dve, pe = self.m, self.act, self.dve, self.pe
        buf = m["tmp"][:, 2048:4096].rearrange("p (i n) -> p i n", i=4)
        n_items = len(items)
        st = {}
        for step in range(n_items + 2):
            if step < n_items:
                it = items[step]
                n, s = it["n"], st.setdefault(step, {})
                b, ps = self.bank()
                s["scores"] = it["scores"](ps)
                p = buf[:, step % 2, 0:n]
                peak, neg, total = (m["soft"][:, i, step % 4:step % 4 + 1] for i in range(3))
                slot_free = st[step - 2]["turned"] if step > 1 else self.tmp_read
                if it["bias"]:
                    ready = it["bias"](p, ps, [s["scores"], slot_free])
                    self.bank_free[b] = ready
                    src = p
                else:
                    ready, src = s["scores"], ps[:, 0:n]
                mx = dve.run(lambda e, o=peak, i=src: e.tensor_reduce(o, i, AX_X, ALU.max), ready)
                ng = dve.run(lambda e, o=neg, i=peak, c=-it["scale"]: e.tensor_scalar(
                    o, i, c, None, ALU.mult), mx)
                s["exp"] = act.run(lambda e, o=p, i=src, ng=neg, t=total, c=it["scale"]: e.activation(
                    o, i, ACT.Exp, bias=ng, scale=c, accum_out=t), ng, slot_free)
                if not it["bias"]:
                    self.bank_free[b] = s["exp"]
            if 1 <= step <= n_items:
                it, s = items[step - 1], st[step - 1]
                n = it["n"]
                p = buf[:, (step - 1) % 2, 0:n]
                turned = buf[:, 2 + (step - 1) % 2, 0:n]
                b, ps = self.bank()
                pe.wait(s["exp"])
                for k in range(n // P):
                    s["turned"] = self.transpose(ps[:, k * P:(k + 1) * P], p[:, k * P:(k + 1) * P],
                                                 mark=k == n // P - 1)
                free = st[step - 3]["summed"] if step > 2 else self.tmp_read
                s["back"] = act.run(lambda e, o=turned, i=ps, n=n: e.activation(o, i[:, 0:n], ACT.Copy),
                                    s["turned"], free)
                self.bank_free[b] = s["back"]
            if step >= 2:
                it, s = items[step - 2], st[step - 2]
                n = it["n"]
                turned = buf[:, 2 + (step - 2) % 2, 0:n]
                total, inv = (m["soft"][:, i, (step - 2) % 4:(step - 2) % 4 + 1] for i in (2, 3))
                b, ps = self.bank()
                pe.wait(s["back"], it.get("ready"))
                last = n // P - 1
                for k in range(last + 1):
                    s["summed"] = self.mm(ps[:, 0:it["width"]], turned[:, k * P:(k + 1) * P],
                                          it["values"][k], k == 0, k == last, mark=k == last)
                rec = dve.run(lambda e, o=inv, i=total: e.reciprocal(o, i), s["exp"])
                done = dve.run(lambda e, o=it["o"], ps=ps, w=it["width"], inv=inv: e.tensor_scalar(
                    o, ps[:, 0:w], inv, None, ALU.mult), s["summed"], rec, self.tmp_read)
                self.bank_free[b] = done
        return done, s["summed"]

    def turn_rows(self, rows, n_tiles, chunk0, n_chunks, ready):
        m, act, dve, pe = self.m, self.act, self.dve, self.pe
        N = n_tiles * P
        pe.wait(ready)
        marks = []
        for c in range(n_chunks):
            b, ps = self.bank()
            for t in range(n_tiles):
                mark = self.transpose(ps[:, t * P:(t + 1) * P], rows(t)[:, c * P:(c + 1) * P],
                                      mark=t == n_tiles - 1)
            hi, lo = (m[k][:, chunk0 + c, 0:N] for k in ("in_hi", "in_lo"))
            high = act.run(lambda e, hi=hi, ps=ps: e.activation(hi, ps[:, 0:N], ACT.Copy), mark,
                           self.in_read)
            low = dve.run(lambda e, lo=lo, ps=ps, hi=hi: e.tensor_tensor(
                lo, ps[:, 0:N], hi.bitcast(F32), ALU.subtract), high, self.in_read)
            self.bank_free[b] = low
            marks.append(low)
        self.tmp_read = [mark]
        return marks

    def value_rows(self, w_dram, x, n_tiles, dst):
        m, act = self.m, self.act
        K, n = w_dram.shape[0] // P, w_dram.shape[1]
        view = w_dram.rearrange("(k p) n -> p k n", p=P)
        width = min(UNIT // K, 512, n)
        done = []
        for c0 in range(0, n, width):
            unit, hi, lo = self.weights(view[:, :, c0:c0 + width])
            for t in range(n_tiles):
                b, ps = self.bank()
                for k in range(K):
                    xh, xl = x(k)
                    tok = slice(t * P, (t + 1) * P)
                    self.mm(ps[:, 0:width], xh[:, tok], hi[:, k, :], k == 0, False)
                    self.mm(ps[:, 0:width], xh[:, tok], lo[:, k, :], False, False)
                    mark = self.mm(ps[:, 0:width], xl[:, tok], hi[:, k, :], False, k == K - 1,
                                   mark=k == K - 1)
                o = dst(t)[:, c0:c0 + width]
                copied = act.run(lambda e, o=o, ps=ps: e.activation(o, ps[:, 0:width], ACT.Copy), mark,
                                 self.h_read)
                self.bank_free[b] = copied
            self.used[unit] = mark
        return copied, mark

    def dilated_mixer(self):
        m, act, dve, pe, a = self.m, self.act, self.dve, self.pe, self.a
        w_qkv = a["attn_w_qkv"][0]
        quad = 4 * HEAD
        size = DIL_GROUPS * 2 * S
        slopes = (2.0 ** (-8.0 * np.arange(1, 49) / 48)).reshape(3, 16).astype(np.float32)
        dist = m["const"][:, 4 * S:].rearrange("p (t n) -> p t n", t=2)
        rows = m["tmp"][:, 0:2048].rearrange("p (t n) -> p t n", t=2)
        x = self.stage_in(0, S)
        summed = [self.h_read, self.h_read]
        start_free = self.h_read
        for hq in range(HEADS // 4):
            buf = m["work"][:, (hq % 2) * 3 * size:(hq % 2 + 1) * 3 * size]
            qT, kT = (buf[:, i * size:(i + 1) * size].rearrange("p (g c t) -> p g c t", g=3, c=2)
                      for i in range(2))
            v = buf[:, 2 * size:3 * size].rearrange("p (t g n) -> p t g n", t=2, g=3)
            self.h_read = summed[hq % 2]
            ready = []
            for g in range(DIL_GROUPS):
                for which, dst, factor in ((0, qT, HEAD ** -0.5), (1, kT, 1.0)):
                    def keep(c, b, ps, mark, g=g, dst=dst, factor=factor):
                        done = act.run(lambda e: e.activation(dst[:, g, c, :], ps[:, 0:S], ACT.Copy,
                                                              scale=factor), mark, self.h_read)
                        self.bank_free[b] = done
                        ready.append(done)
                    c0 = (g * 3 + which) * D + hq * quad
                    self.project(w_qkv[:, c0:c0 + quad], quad, x, S, keep)
                c0 = (g * 3 + 2) * D + hq * quad
                copied, self.in_read = self.value_rows(
                    w_qkv[:, c0:c0 + quad], x, 2, lambda t, g=g: v[:, t, g, :])
                ready.append(copied)
            items = []
            pe.wait(*ready)
            for h in range(4):
                for t in range(2):
                    c, r = h // 2, (h % 2) * HEAD
                    q0 = t * P

                    def scores(ps, c=c, r=r, q0=q0):
                        for g, k0, n, col in ((0, 0, S, 0), (1, q0, P, S), (2, q0, P, S + P)):
                            mark = self.mm(ps[:, col:col + n], qT[r:r + HEAD, g, c, q0:q0 + P],
                                           kT[r:r + HEAD, g, c, k0:k0 + n], mark=g == 2)
                        return mark

                    def bias(o, ps, marks, head=hq * 4 + h, t=t):
                        for g, col, n in ((0, 0, S), (1, S, P), (2, S + P, P)):
                            mark = dve.run(lambda e, s=-float(slopes[g, head]), col=col, n=n:
                                           e.scalar_tensor_tensor(o[:, col:col + n], dist[:, t, col:col + n],
                                                                  s, ps[:, col:col + n], ALU.mult, ALU.add),
                                           *marks, self.const_tables)
                        return mark

                    e0 = h * HEAD
                    items.append(dict(
                        n=512, scores=scores, bias=bias, scale=1.0, width=HEAD,
                        values=[v[:, 0, 0, e0:e0 + HEAD], v[:, 1, 0, e0:e0 + HEAD],
                                v[:, t, 1, e0:e0 + HEAD], v[:, t, 2, e0:e0 + HEAD]],
                        o=rows[:, t, (hq * 4 + h) * HEAD:(hq * 4 + h + 1) * HEAD]))
            done, summed[hq % 2] = self.attend(items)
            self.tmp_read = [summed[hq % 2]]
        self.h_read = summed[(HEADS // 4 - 1) % 2]
        turned = self.turn_rows(lambda t: rows[:, t, :], 2, 0, DC, done)
        residual = self.add_scaled(0)
        tmp = m["stat"]

        def add(d, b, ps, mark):
            t = tmp[:, d % 2, 0:S]
            natural = ps[:, 0:S].rearrange("p (a b c) -> p c b a", a=4, b=4)
            copied = act.run(lambda e: e.activation(t.rearrange("p (c b a) -> p c b a", a=4, b=4), natural,
                                                    ACT.Copy), mark, self.x_ready[max(d - 2, 0)],
                             self.stat_read)
            self.bank_free[b] = copied
            residual(d, t, copied)

        self.in_ready = turned
        self.in_read = self.project(a["attn_w_out"][0], D, self.stage_in(0, S), S, add)
        self.stat_read = [self.x_ready[DC - 1]]

    def load_rpb(self):
        pad = self.m["rpb"]
        zero = self.dve.run(lambda e: e.memset(pad[:, :], 0.0))
        src = self.a["ab_rpb_2"][0].rearrange("h r c -> (h r) c")
        first = GRID_W - 1 - (RPB_W // 2)
        got = self.act.dma(pad[:, first:first + RPB_W], src, self.slot["rpb"], zero)
        copies = pad[:, None, :].broadcast_to([NA_HEADS * RPB_H, GRID_W, P])
        self.rpb_stored = self.act.dma(self.a["scratch"], copies, self.slot["rpb"], got)

    def load_mixer_tables(self):
        self.const_tables = self.sync.dma(self.m["const"][:, 0:1792], self.a["k_mixer"],
                                          self.slot["table"], self.const_read)

    def na_bias_loads(self):
        bias = self.m["work"][:, 8192:8192 + 4096].rearrange("p (h t n) -> p h t n", h=NA_HEADS, t=2)
        self.na_bias, scratch, free = bias, self.a["scratch"], self.h_read
        self.sync.wait(self.rpb_stored)
        for h in range(NA_HEADS):
            for qr in range(GRID_H):
                row = h * RPB_H + RPB_H // 2 - qr
                src = bass.AP(scratch.tensor, row * GRID_W * P + GRID_W - 1,
                              [[P - 1, GRID_W], [GRID_W * P, GRID_H], [1, GRID_W]])
                p0 = (qr % 2) * GRID_W
                dst = bias[p0:p0 + GRID_W, h, qr // 2, :].rearrange("p (r c) -> p r c", r=GRID_H)
                self.na_bias_landed = self.sync.dma(dst, src, self.slot["bias"], free)
            if h % 2:
                yield

    def mask_na_bias(self):
        m, bias = self.m, self.na_bias
        mask = m["const"][:, 1280:1792].rearrange("p (t n) -> p t n", t=2)
        for h in range(NA_HEADS):
            self.na_bias_ready = self.dve.run(lambda e, h=h: e.tensor_tensor(
                bias[:, h, :, :], bias[:, h, :, :], mask, ALU.add), self.na_bias_landed, self.const_tables)

    def fourier_na_mixer(self, layer):
        m, act, dve, pe, a = self.m, self.act, self.dve, self.pe, self.a
        w_in = a["ab_w_in_2"][0]
        N = 2 * S
        x = self.stage_in(0, N)
        bias_loads = self.na_bias_loads()
        uT, qT, kT, v = (m["work"][:, i * 2048:(i + 1) * 2048].rearrange("p (c t) -> p c t", c=4)
                         for i in range(4))
        ready = {}

        def keeper(name, dst, factor=1.0):
            def keep(c, b, ps, mark):
                ready[name] = act.run(lambda e: e.activation(dst[:, c, :], ps[:, 0:N], ACT.Copy,
                                                             scale=factor), mark, self.h_read)
                self.bank_free[b] = ready[name]
            return keep

        self.project(w_in[:, 0:512], 512, x, N, keeper("u", uT))
        dft_d = m["const"][:, 0:256]
        dft_n = m["const"][:, 256:1280].rearrange("p (k f n) -> p k f n", k=2, f=2)
        spec = m["tmp"][:, :].rearrange("p (t g n) -> p t g n", t=4, g=4)
        pe.wait(ready["u"], self.const_tables)
        for g in range(4):
            for t in range(4):
                b, ps = self.bank()
                mark = self.mm(ps[:, 0:256], uT[:, g, t * P:(t + 1) * P], dft_d, mark=True)
                spec_ready = dve.run(lambda e, ps=ps, t=t, g=g: e.tensor_copy(spec[:, t, g, :], ps[:, 0:256]),
                                     mark, self.tmp_read)
                self.bank_free[b] = spec_ready
        next(bias_loads)
        for c0, name, dst, factor in ((512, "q", qT, HEAD ** -0.5), (1024, "k", kT, 1.0)):
            self.project(w_in[:, c0:c0 + 512], 512, x, N, keeper(name, dst, factor))
            next(bias_loads)
        v_done, self.in_read = self.value_rows(w_in[:, 1536:2048], x, 4, lambda t: v[:, t, :])
        next(bias_loads)
        turned = []
        pe.wait(spec_ready)
        for g in range(4):
            b, ps = self.bank()
            for s in range(2):
                for i, (k, f) in enumerate(((0, 0), (1, 0), (0, 1), (1, 1))):
                    mark = self.mm(ps[:, s * S:(s + 1) * S], spec[:, 2 * s + k, g, f * P:(f + 1) * P],
                                   dft_n[:, k, f, :], i == 0, i == 3, mark=s == 1 and i == 3)
            hi, lo = (m[k][:, g, 0:N] for k in ("in_hi", "in_lo"))
            high = act.run(lambda e, hi=hi, ps=ps: e.activation(hi, ps[:, 0:N], ACT.Copy), mark, self.in_read)
            low = dve.run(lambda e, lo=lo, ps=ps, hi=hi: e.tensor_tensor(
                lo, ps[:, 0:N], hi.bitcast(F32), ALU.subtract), high)
            self.bank_free[b] = low
            turned.append(low)
        self.tmp_read = [mark]
        self.mask_na_bias()
        rows = m["tmp"][:, 0:2048].rearrange("p (t n) -> p t n", t=4)
        pe.wait(ready["q"], ready["k"], v_done)
        items = []
        for t in range(4):
            for h in range(NA_HEADS):
                c, r = h // 2, (h % 2) * HEAD
                k0, n = (0, N) if t < 2 else (S, S)

                def scores(ps, c=c, r=r, t=t, k0=k0, n=n):
                    return self.mm(ps[:, 0:n], qT[r:r + HEAD, c, t * P:(t + 1) * P],
                                   kT[r:r + HEAD, c, k0:k0 + n], mark=True)

                def bias(o, ps, marks, h=h, t=t):
                    dve.run(lambda e: e.tensor_tensor(o[:, 0:S], self.na_bias[:, h, t, :], ps[:, 0:S],
                                                      ALU.add), *marks, self.na_bias_ready)
                    return dve.run(lambda e: e.tensor_copy(o[:, S:N], ps[:, S:N]))

                items.append(dict(
                    n=n, scores=scores, bias=bias if t < 2 else None, scale=1.0, width=HEAD,
                    values=[v[:, k, h * HEAD:(h + 1) * HEAD] for k in range(k0 // P, (k0 + n) // P)],
                    o=rows[:, t, h * HEAD:(h + 1) * HEAD]))
        done, summed = self.attend(items)
        self.h_read = summed
        turned += self.turn_rows(lambda t: rows[:, t, :], 4, 4, 4, done)
        self.in_ready = turned
        self.project_gated(a["ab_w_out_2"][0], layer, 5)

    def mla_mixer(self, layer):
        m, act, dve, pe, a = self.m, self.act, self.dve, self.pe, self.a
        N = 2 * S
        tables = act.dma(m["const"][:, 0:896], a["k_rope"], self.slot["table"], self.const_read)
        cos, sin = m["const"][:, 0:S], m["const"][:, S:2 * S]
        rotate = m["const"][:, 512:640]
        dup, dup_rotate = m["const"][0:ROPE, 640:768], m["const"][0:ROPE, 768:896]
        tmp, work = m["tmp"], m["work"]
        cq = tmp[:, 0:768].rearrange("p (c t) -> p c t", c=3)
        ckv = tmp[:, 768:1280]
        lat = m["latent"]
        cq_hi, cq_lo = (lat[:, i * 768:(i + 1) * 768].rearrange("p (c t) -> p c t", c=3) for i in range(2))
        ckv_hi, ckv_lo = lat[:, 1536:2048], lat[:, 2048:2560]
        qn = work[:, 0:2048].rearrange("p (h t) -> p h t", h=8)
        qr = work[:, 2048:3072].rearrange("p (j t) -> p j t", j=4)
        kn = work[:, 3072:7168].rearrange("p (h t) -> p h t", h=8)
        kr = work[:, 7168:7680]
        v = work[:, 7680:11776].rearrange("p (t n) -> p t n", t=4)
        spare = work[:, 11776:12288]
        w_in = a["mla_w_in_2"][0]
        xq, xk = self.stage_in(0, S), self.stage_in(0, N)
        h_free, t_free = self.h_read, self.tmp_read
        ready = {}

        def keep_q(c, b, ps, mark):
            ready[c] = act.run(lambda e: e.activation(cq[:, c, :], ps[:, 0:S], ACT.Copy), mark, t_free)
            self.bank_free[b] = ready[c]

        def keep_kv(c, b, ps, mark):
            ready["kv"] = act.run(lambda e: e.activation(ckv, ps[:, 0:N], ACT.Copy), mark, t_free)
            self.bank_free[b] = ready["kv"]

        def keep_kr(c, b, ps, mark):
            ready["kr"] = act.run(lambda e: e.activation(kr[0:ROPE, :], ps[0:ROPE, 0:N], ACT.Copy), mark,
                                  h_free)
            self.bank_free[b] = ready["kr"]

        self.project(w_in[:, 0:256], 256, xq, S, keep_q)
        self.project(w_in[:, 256:384], 128, xq, S, lambda c, b, ps, mark: keep_q(2, b, ps, mark))
        self.project(w_in[:, 384:512], 128, xk, N, keep_kv)
        self.in_read = self.project(w_in[:, 512:576], 64, xk, N, keep_kr)

        pe.wait(ready["kr"], tables)
        b1, both = self.bank()
        m1 = self.mm(both[:, 0:N], dup, kr[0:ROPE, :], mark=True)
        b2, other = self.bank()
        m2 = self.mm(other[:, 0:S], dup_rotate, kr[0:ROPE, 0:S], mark=True)
        r0 = dve.run(lambda e: e.tensor_tensor(spare[:, 0:S], other[:, 0:S], sin, ALU.mult), m2, h_free, tables)
        self.bank_free[b2] = r0
        r1 = dve.run(lambda e: e.tensor_copy(kr[:, S:N], both[:, S:N]), m1, m2)
        r2 = dve.run(lambda e: e.tensor_tensor(kr[:, 0:S], both[:, 0:S], cos, ALU.mult))
        self.bank_free[b1] = r2
        kr_done = dve.run(lambda e: e.tensor_tensor(kr[:, 0:S], kr[:, 0:S], spare[:, 0:S], ALU.add), r0, r2)

        sq = m["tmp"][:, 1536:2560]
        def latent_norm(chunks, n, width, gain, his, los, marks):
            b, ps = self.bank()
            for d, c in enumerate(chunks):
                q = work[:, 7680 + d * n:7680 + (d + 1) * n]
                s = act.run(lambda e, q=q, c=c: e.activation(q, c, ACT.Square), marks[d], h_free)
                pe.wait(s)
                mark = self.mm(ps[:, 0:n], m["mean_w"][:, :], q, d == 0, d == len(chunks) - 1,
                               mark=d == len(chunks) - 1)
            y, root = self.inv_root(b, ps, n, mark, D / width, RMS_EPS)
            for d, c in enumerate(chunks):
                g = m["cols"][:, gain + d:gain + d + 1]
                n1 = dve.run(lambda e, c=c, g=g: e.scalar_tensor_tensor(c, c, g, y, ALU.mult, ALU.mult),
                             root, mark)
                n2 = act.run(lambda e, c=c, hi=his[d]: e.activation(hi, c, ACT.Copy), n1, t_free)
                n3 = dve.run(lambda e, c=c, hi=his[d], lo=los[d]: e.tensor_tensor(
                    lo, c, hi.bitcast(F32), ALU.subtract), n2, t_free)
            self.stat_read = [n3]
            return n3, mark

        kv_ready, mark = latent_norm([ckv], N, P, self.col["mla_g_kv_2"], [ckv_hi], [ckv_lo], [ready["kv"]])
        h_free = [h_free, mark]
        q_ready, mark = latent_norm([cq[:, c, :] for c in range(3)], S, Q_RANK, self.col["mla_g_q_2"],
                                    [cq_hi[:, c, :] for c in range(3)], [cq_lo[:, c, :] for c in range(3)],
                                    [ready[c] for c in range(3)])
        self.h_read = [h_free, mark]

        w_uq = a["mla_w_uq_2"][0].rearrange("(k p) n -> p k n", p=P)
        pe.wait(q_ready)
        for j in range(MLA_HEADS // 2):
            cols = w_uq[:, :, j * 384:(j + 1) * 384]
            heads = [cols[:, k, :].rearrange("p (h c) -> p h c", h=2) for k in range(3)]
            unit, hi, lo = self.weights(cols, [(k * 384 + first, heads[k][:, :, c0:c1]) for k in range(3)
                                               for first, c0, c1 in ((0, 0, NOPE), (2 * NOPE, NOPE, 192))])
            for part in range(3):
                b, ps = self.bank()
                for k in range(3):
                    w = [t[:, k, part * P:(part + 1) * P] for t in (hi, lo)]
                    mark = self.mm3(ps[:, 0:S], w, (cq_hi[:, k, :], cq_lo[:, k, :]), k == 0, k == 2,
                                    mark=k == 2)
                if part < 2:
                    q_done = act.run(lambda e, o=qn[:, 2 * j + part, :], ps=ps: e.activation(
                        o, ps[:, 0:S], ACT.Copy), mark, h_free)
                    self.bank_free[b] = q_done
                else:
                    raw = spare[:, 0:S]
                    c1 = act.run(lambda e, ps=ps: e.activation(raw, ps[:, 0:S], ACT.Copy), mark, kr_done)
                    self.bank_free[b] = c1
                    pe.wait(c1)
                    b2, ps2 = self.bank()
                    rot = self.mm(ps2[:, 0:S], rotate, raw, mark=True)
                    o, t = qr[:, j, :], spare[:, S:2 * S]
                    d1 = dve.run(lambda e, t=t, ps2=ps2: e.tensor_tensor(t, ps2[:, 0:S], sin, ALU.mult), rot)
                    self.bank_free[b2] = d1
                    d2 = dve.run(lambda e, o=o: e.tensor_tensor(o, raw, cos, ALU.mult), c1)
                    kr_done = dve.run(lambda e, o=o, t=t: e.tensor_tensor(o, o, t, ALU.add), d1, d2)
            self.used[unit] = mark
        unit, hi, lo = self.weights(a["mla_w_uk_2"][0].rearrange("(k p) n -> p k n", p=P))
        pe.wait(kv_ready)
        for h in range(MLA_HEADS):
            b, ps = self.bank()
            w = [t[:, 0, h * P:(h + 1) * P] for t in (hi, lo)]
            mark = self.mm3(ps[:, 0:N], w, (ckv_hi, ckv_lo), True, True, mark=True)
            kn_done = act.run(lambda e, ps=ps, h=h: e.activation(kn[:, h, :], ps[:, 0:N], ACT.Copy), mark)
            self.bank_free[b] = kn_done
        self.used[unit] = mark
        v_done, mark = self.value_rows(a["mla_w_uv_2"][0], lambda k: (ckv_hi, ckv_lo), 4,
                                       lambda t: v[:, t, :])
        self.tmp_read = [mark, kv_ready, q_ready]
        rows = m["tmp"][:, 0:2048].rearrange("p (t n) -> p t n", t=2)
        pe.wait(q_done, kn_done, v_done, kr_done)
        items = []
        for t in range(2):
            for h in range(MLA_HEADS):
                r = (h % 2) * ROPE

                def scores(ps, h=h, r=r, t=t):
                    self.mm(ps[:, 0:N], qn[:, h, t * P:(t + 1) * P], kn[:, h, :], True, False)
                    return self.mm(ps[:, 0:N], qr[r:r + ROPE, h // 2, t * P:(t + 1) * P],
                                   kr[r:r + ROPE, :], False, True, mark=True)

                items.append(dict(
                    n=N, scores=scores, bias=None, scale=float((NOPE + ROPE) ** -0.5), width=P,
                    values=[v[:, k, h * P:(h + 1) * P] for k in range(4)],
                    o=rows[:, t, h * P:(h + 1) * P]))
        done, summed = self.attend(items)
        self.h_read = summed
        turned = self.turn_rows(lambda t: rows[:, t, :], 2, 0, DC, done)
        residual = self.add_gated(layer, 5, (0,))

        def add(d, b, ps, mark):
            self.bank_free[b] = residual(d, ps, mark)

        self.in_ready = turned
        self.in_read = self.project(a["mla_w_o_2"][0], D, self.stage_in(0, S), S, add)

    def finish(self):
        m, dve, act, pe = self.m, self.dve, self.act, self.pe
        b, ps, mark = self.norm_sum[0]
        y, root = self.inv_root(b, ps, S, mark, 1.0, RMS_EPS)
        g0 = self.col["final_g_2"]
        rows = m["work"][:, 0:2048].rearrange("p (t n) -> p t n", t=2)
        out = self.out.rearrange("b (t p) d -> p (b t) d", p=P)
        for d in range(DC):
            x, g = m["x"][:, d, 0:S], m["cols"][:, g0 + d:g0 + d + 1]
            n = dve.run(lambda e, x=x, g=g: e.scalar_tensor_tensor(x, x, g, y, ALU.mult, ALU.mult), root)
            pe.wait(n)
            b, ps = self.bank()
            for t in range(2):
                mark = self.transpose(ps[:, t * P:(t + 1) * P], x[:, t * P:(t + 1) * P], mark=t == 1)
            o = rows[:, :, d * P:(d + 1) * P]
            done = act.run(lambda e, o=o, ps=ps: e.activation(
                o, ps[:, 0:S].rearrange("p (t n) -> p t n", t=2), ACT.Copy), mark, self.h_read)
            self.bank_free[b] = done
        self.sync.wait(self.sync.dma(out, rows, self.slot["out"], done))

    def emit(self):
        a = self.a
        self.setup()
        both = (0, 1)
        for i in range(DEPTH):
            w = [a[f"ffn1_w_{k}"][i] for k in ("gate", "up", "down")]
            extra = None
            if i == 0:
                tok = self.m["tmp"][:, 2048:4096].rearrange("p (t d) -> p t d", t=2)
                extra = lambda: self.transpose_in(tok, self.context_landed, 1)
            self.norm_of("ln")
            self.ffn(*w, S, self.add_scaled(0), ada=True, extra=extra)
            self.layer_norm(i * 3, permuted=i == 1)
            if i == 0:
                self.pool_mixer()
            else:
                self.dilated_mixer()
                self.const_read = self.dve_mark()
            self.layer_norm(i * 3 + 1)
            w = [a[f"ffn2_w_{k}"][i] for k in ("gate", "up", "down")]
            self.ffn(*w, S, self.add_scaled(0), ada=True,
                     before_down=self.first_context_norm if i == DEPTH - 1 else None)
            if i < DEPTH - 1:
                self.layer_norm(i * 3 + 2)
        for layer in range(DEPTH):
            last = layer == DEPTH - 1
            w = [a[f"ffn_w_{k}_2"][layer, 0] for k in ("gate", "up", "down")]
            self.norm_of("rms", both, self.rms_both(layer, 1, 3, 4))
            self.ffn(*w, 2 * S, self.add_gated(layer, 2, both),
                     start=self.first_products if layer == 0 else None)
            if last:
                self.norm_of("rms")
                self.mla_mixer(layer)
                self.rms_mod(layer, 2, 6, 7)
                self.norm_of("rms")
            else:
                self.norm_of("rms", both, self.rms_both(layer, 2, 6, 7))
                self.fourier_na_mixer(layer)
                self.const_read = [self.h_read, self.dve_mark()]
                self.norm_of("rms", both, self.rms_both(layer + 1, 0, 0, 1))
            streams = (0,) if last else both
            w = [a[f"ffn_w_{k}_2"][layer, 1] for k in ("gate", "up", "down")]
            self.ffn(*w, S * len(streams), self.add_gated(layer, 8, streams))
        self.finish()

    def first_context_norm(self):
        while self.ada_blocks or self.ada_bank:
            self.ada_step()
        self.finish_ada()
        norm, self.norm = self.norm, ("rms", (1,), None)
        for d in range(DC):
            self.feed_norm(d, (1,))
        self.rms_mod(0, 0, 0, 1, s=1, silu_next=False)
        self.norm = norm

    def first_products(self, gate, up):
        norm = self.norm
        latents, context = self.stage_in(0, S), self.stage_in(S, S)
        units, banks, products = [], [], []

        def context_product(w, ahead):
            units.append(self.weights(w, ahead=ahead))
            banks.append(self.open_banks(2 * P))
            self.accumulate(*units[-1][1:], banks[-1], DC, context, S, S)

        context_product(gate, 2)
        self.load_mixer_tables()
        self.norm_of("rms")
        self.layer_norm(DEPTH * 3 - 1, split=False, meanwhile=lambda: context_product(up, 1))
        self.rms_mod(0, 0, 0, 1)
        self.split_until(self.taken + 1)
        for (unit, hi, lo), taken in zip(units, banks):
            marks = self.accumulate(hi, lo, taken, DC, latents, 0, S)
            self.used[unit] = marks[-1]
            self.split_until(self.taken + 1 + len(products))
            products.append([(t[2], t[3], mark) for t, mark in zip(taken, marks)])
        self.norm = norm
        return products

    def dve_mark(self):
        return (self.dve.sem, self.dve.count)


def tables():
    f32 = np.float32
    t = np.arange(S)
    inverse = []
    for w in (2, 4, 8, 16):
        lo, hi = np.clip(t - w // 2, 0, S), np.clip(t + w // 2, 0, S)
        inverse.append(1.0 / (hi - lo))
    inverse = np.broadcast_to(np.concatenate(inverse)[None], (P, 4 * S))
    order = np.array([c * 16 + b * 4 + a for a in range(4) for b in range(4) for c in range(16)])
    dist = np.abs(order[:, None] - order[None, :]).astype(np.float64)
    same = lambda n: order[:, None] % n == order[None, :] % n
    d0 = np.where(dist <= 64, dist, FAR)
    d1, d2 = (np.where(same(n), dist, FAR) for n in (4, 16))
    tiles = []
    for i in range(2):
        r = slice(i * P, (i + 1) * P)
        tiles.append(np.concatenate([d0[r], d1[r, r], d2[r, r]], axis=1))
    block1 = np.concatenate([inverse] + tiles, axis=1).astype(f32)
    ang = 2 * np.pi * np.outer(np.arange(P), np.arange(P)) / P
    dft_d = np.concatenate([np.cos(ang), np.sin(ang)], axis=1) / np.sqrt(P)
    ang = 2 * np.pi * (np.outer(np.arange(S), np.arange(S)) % S) / S
    dft_n = np.stack([np.cos(ang), -np.sin(ang)], axis=1) / np.sqrt(S)
    dft_n = dft_n.reshape(2, P, 2, S).transpose(1, 0, 2, 3).reshape(P, 4 * S)
    col = t % GRID_W
    start = np.clip(col - 8, 0, GRID_W - 16)
    seen = (col[None, :] >= start[:, None]) & (col[None, :] < start[:, None] + 16)
    mask = np.where(seen, 0.0, -1e30).reshape(2, P, S).transpose(1, 0, 2).reshape(P, 2 * S)
    mixer = np.concatenate([dft_d, dft_n, mask], axis=1).astype(f32)
    inv = (10000.0 ** (-np.arange(0, 32, 2, dtype=f32) / f32(32))).astype(f32)
    row, colf = (t // GRID_W).astype(f32), (t % GRID_W).astype(f32)
    ar, ac = row[:, None] * inv[None], colf[:, None] * inv[None]
    angle = np.concatenate([ar, ar, ac, ac], axis=1)
    cos, sin = (np.concatenate([f(angle).T] * 2, axis=0) for f in (np.cos, np.sin))
    rot = np.zeros((ROPE, ROPE))
    for i in range(16):
        rot[16 + i, i] = rot[48 + i, 32 + i] = -1.0
        rot[i, 16 + i] = rot[32 + i, 48 + i] = 1.0
    rot2 = np.zeros((P, P))
    rot2[:ROPE, :ROPE] = rot2[ROPE:, ROPE:] = rot
    dup = np.zeros((P, 2 * P))
    dup[:ROPE] = np.concatenate([np.eye(ROPE), np.eye(ROPE), rot, rot], axis=1)
    rope = np.concatenate([cos, sin, rot2, dup], axis=1).astype(f32)
    return {"k_ident": np.eye(P, dtype=f32), "k_block1": block1, "k_mixer": mixer, "k_rope": rope}


NAMES = ["x", "ffn1_w_gate", "ffn1_w_up", "ffn1_w_down", "ffn2_w_gate", "ffn2_w_up", "ffn2_w_down",
         "ln_gain", "ln_bias", "pool_w_in", "pool_w_group", "pool_scale", "pool_w_out", "attn_w_qkv",
         "attn_w_out", "c_2", "ctx_2", "c_ctx_2", "ada_w_2", "ada_b_2", "norm_g_2", "ffn_w_gate_2",
         "ffn_w_up_2", "ffn_w_down_2", "ab_w_in_2", "ab_rpb_2", "ab_w_out_2", "mla_w_in_2", "mla_g_q_2",
         "mla_g_kv_2", "mla_w_uq_2", "mla_w_uk_2", "mla_w_uv_2", "mla_w_o_2", "final_g_2"]
IN_ROWS = ["ln_gain", "ln_bias", "norm_g_2", "pool_scale", "final_g_2", "mla_g_q_2", "mla_g_kv_2", "c_2",
           "c_ctx_2"]


def as_rows(ap):
    n = int(np.prod(ap.shape))
    return bass.AP(ap.tensor, 0, [[P, n // P], [1, P]])


def build(nc, shapes):
    a = {name: nc.dram_tensor(f"in_{name}", shape, F32, kind="ExternalInput").ap()
         for name, shape in shapes.items()}
    out = nc.dram_tensor("out_0", (1, S, D), F32, kind="ExternalOutput").ap()
    a["scratch"] = nc.dram_tensor("rpb_rows", (NA_HEADS * RPB_H, GRID_W, P), F32, kind="Internal").ap()
    for name in IN_ROWS:
        a[name] = as_rows(a[name])
    ada_b = as_rows(a["ada_b_2"])
    for layer in range(DEPTH):
        a[f"ada_b_2.{layer}"] = ada_b[layer * MODC:(layer + 1) * MODC, :]
    build_program(nc, a, out)
    return "out_0"


def kernel(**inputs):
    import concourse.bacc as bacc
    from concourse.bass_utils import run_bass_kernel_spmd

    nc = bacc.Bacc("TRN2", target_bir_lowering=False, num_devices=1,
                   dynamic_dma_scratch_size=1024)
    arrays = {name: np.ascontiguousarray(inputs[name]) for name in NAMES}
    arrays.update(tables())
    result = build(nc, {name: v.shape for name, v in arrays.items()})
    r = run_bass_kernel_spmd(nc, [{f"in_{n}": v for n, v in arrays.items()}], core_ids=[0])
    return r.results[0][result]
```

```python
from contextlib import ExitStack

import numpy as np

import concourse.bass as bass
from concourse import mybir

F32 = mybir.dt.float32
F32R = mybir.dt.float32r
ALU = mybir.AluOpType
ACT = mybir.ActivationFunctionType
AX_X = mybir.AxisListType.X

P = 128
S = 256
D = 1024
DC = D // P
F = 2816
FC = F // P
DEPTH = 2
ALPHA = (2.0 * DEPTH) ** 0.25
LN_EPS = 1e-5
RMS_EPS = 1e-6
HEAD = 64
HEADS = 16
DIL_GROUPS = 3
NA_HEADS = 8
MLA_HEADS = 8
NOPE = 128
ROPE = 64
Q_RANK = 384
N_MOD = 9
MODC = N_MOD * DC
GRID_W = 64
GRID_H = S // GRID_W
RPB_H, RPB_W = 15, 31
UNIT = 2048
RAW_SLOTS = 4
SPLIT_SLOTS = 3
H_CHUNKS = 24
FAR = 1e32


class Engine:

    def __init__(self, sem):
        self.sem, self.count, self.queue, self.seen = sem, 0, [], {}

    def wait(self, *marks):
        for mark in marks:
            if isinstance(mark, list):
                self.wait(*mark)
            elif mark is not None and self.seen.get(mark[0].name, 0) < mark[1]:
                self.seen[mark[0].name] = mark[1]
                self.queue.append(lambda e, m=mark: e.wait_ge(m[0], m[1]))

    def run(self, op, *marks):
        self.wait(*marks)
        self.count += 1
        self.queue.append(lambda e: op(e).then_inc(self.sem, 1))
        return (self.sem, self.count)

    def quiet(self, op, *marks):
        self.wait(*marks)
        self.queue.append(op)

    def dma(self, out, in_, slot, *marks):
        self.wait(*marks)
        slot[1] += 16
        self.queue.append(lambda e: e.dma_start(out, in_).then_inc(slot[0], 16))
        return (slot[0], slot[1])

    def play(self, e):
        for op in self.queue:
            op(e)


def build_program(nc, a, out):
    with ExitStack() as ctx:
        place = [nc.sbuf_base + (-nc.sbuf_base) % 64]

        def at(name, shape, dtype, offset):
            return nc.alloc_sbuf_tensor_at(name, shape, dtype, offset=offset)

        def room(nbytes):
            here = place[0]
            place[0] += nbytes + (-nbytes) % 64
            assert place[0] <= nc.sbuf_usable_end, (place, nc.sbuf_usable_end)
            return here

        def sb(name, shape, dtype=F32):
            return at(name, shape, dtype, room(4 * int(np.prod(shape[1:]))))

        m = {}
        m["x"] = sb("x", [P, DC, 2 * S])
        m["in_hi"] = sb("in_hi", [P, DC, 2 * S], F32R)
        m["in_lo"] = sb("in_lo", [P, DC, 2 * S], F32R)
        base = room(4 * 2 * H_CHUNKS * S)
        m["h_hi"] = at("h_hi", [P, H_CHUNKS * S], F32R, base)
        m["h_lo"] = at("h_lo", [P, H_CHUNKS * S], F32R, base + 4 * H_CHUNKS * S)
        m["work"] = at("work", [P, 2 * H_CHUNKS * S], F32, base)
        m["raw"] = [sb(f"raw{i}", [P, UNIT]) for i in range(RAW_SLOTS)]
        m["hi"] = [sb(f"hi{i}", [P, UNIT], F32R) for i in range(SPLIT_SLOTS)]
        m["lo"] = [sb(f"lo{i}", [P, UNIT], F32R) for i in range(SPLIT_SLOTS)]
        base = room(4 * DC * 2 * S)
        m["tmp"] = at("tmp", [P, DC * 2 * S], F32, base)
        m["latent"] = at("latent", [P, 2560], F32R, base + 4 * 1536)
        m["const"] = sb("const", [P, 2048])
        m["ident"] = sb("ident", [P, P])
        m["mean_w"] = sb("mean_w", [P, P])
        m["stat"] = sb("stat", [P, 4, 2 * S])
        m["cols"] = sb("cols", [P, 512])
        m["mod"] = sb("mod", [P, DEPTH, MODC, 2])
        m["gain"] = sb("gain", [P, DC, 2])
        m["c_silu"] = sb("c_silu", [P, DC, 2])
        m["soft"] = sb("soft", [P, 4, 4])
        m["exp"] = sb("exp", [P, 512])
        m["rpb"] = sb("rpb", [NA_HEADS * RPB_H, P])
        m["ada_acc"] = sb("ada_acc", [P, 2, 512])
        m["ones"] = sb("ones", [P, 1])
        m["banks"] = [ctx.enter_context(nc.psum_tensor(f"bank{i}", [P, 512], F32)) for i in range(8)]

        names = "pe act dve sync".split()
        sems = {n: ctx.enter_context(nc.semaphore(f"{n}_done")) for n in names}
        for i in range(RAW_SLOTS):
            sems[f"raw{i}"] = ctx.enter_context(nc.semaphore(f"raw{i}_landed"))
        for n in ("consts", "rows", "tokens", "context", "table", "rpb", "bias0", "bias1", "bias2", "bias3",
                  "out"):
            sems[n] = ctx.enter_context(nc.semaphore(f"{n}_landed"))

        plan = []
        Program(nc, a, out, m, sems, plan, True).emit()
        program = Program(nc, a, out, m, sems, plan, False)
        program.emit()

        block = ctx.enter_context(nc.Block())
        block.sync(program.sync.play)
        block.scalar(program.act.play)
        block.vector(program.dve.play)
        block.tensor(program.pe.play)


class Program:
    def __init__(self, nc, a, out, m, sems, plan, dry):
        self.nc, self.a, self.out, self.m, self.plan, self.dry = nc, a, out, m, plan, dry
        self.pe, self.act, self.dve, self.sync = (Engine(sems[n]) for n in ("pe", "act", "dve", "sync"))
        self.slot = {n: [sems[n], 0] for n in sems}
        self.loaded = self.at = self.split = self.taken = 0
        self.raw_landed, self.raw_read, self.hi_done, self.lo_done, self.used = {}, {}, {}, {}, {}
        self.next_bank, self.bank_free = 0, [None] * 8
        self.ada_halves = [(layer, n, half) for layer in range(DEPTH) for n in range(N_MOD * D // 512)
                           for half in range(2)]
        self.ada_period, self.ada_ticks = 5, 0
        self.ada_done, self.ada_summed, self.mod_ready = {}, None, [None] * DEPTH
        self.x_ready = [None] * (2 * DC)
        self.in_ready = []
        self.norm, self.norm_chunk_read = None, {}
        self.norm_added, self.norm_sum = {}, {}
        self.norming = None
        self.in_read = None
        self.h_read = None
        self.tmp_read = []
        self.stat_read = []

    def load_unit(self, i):
        parts = self.plan[i][0]
        for first, src in parts:
            n = src.shape[1] * src.shape[2]
            dst = self.m["raw"][i % RAW_SLOTS][:, first:first + n].rearrange("p (a b) -> p a b", b=src.shape[2])
            self.raw_landed[i] = self.sync.dma(dst, src, self.slot[f"raw{i % RAW_SLOTS}"],
                                               self.raw_read.get(i - RAW_SLOTS))

    def load_until(self, end):
        while self.loaded < min(end, len(self.plan)):
            self.load_unit(self.loaded)
            self.loaded += 1

    def split_unit(self, i, j):
        n, s = self.plan[i][1] * self.plan[i][2], j % SPLIT_SLOTS
        raw, hi, lo = self.m["raw"][i % RAW_SLOTS], self.m["hi"][s], self.m["lo"][s]
        before = self.used[j - SPLIT_SLOTS] if j >= SPLIT_SLOTS else None
        self.hi_done[j] = self.act.run(
            lambda e: e.activation(hi[:, 0:n], raw[:, 0:n], ACT.Copy), self.raw_landed[i], before)
        self.lo_done[j] = self.dve.run(
            lambda e: e.tensor_tensor(lo[:, 0:n], raw[:, 0:n], hi[:, 0:n].bitcast(F32), ALU.subtract),
            self.raw_landed[i], self.hi_done[j], before)
        self.raw_read[i] = [self.hi_done[j], self.lo_done[j]]

    def split_until(self, end):
        while not self.dry and self.split < end and self.at < len(self.plan):
            self.load_until(self.at + RAW_SLOTS)
            if self.plan[self.at][3]:
                self.ada_products(self.at, *self.plan[self.at][3])
            else:
                self.split_unit(self.at, self.split)
                self.split += 1
            self.at += 1

    def weights(self, src, parts=None, ahead=SPLIT_SLOTS):
        A, B = src.shape[1], src.shape[2]
        assert A * B <= UNIT and src.shape[0] == P
        j = self.taken
        self.taken += 1
        if self.dry:
            self.plan.append((parts or [(0, src)], A, B, None))
        else:
            self.split_until(j + ahead)
            self.pe.wait(self.hi_done[j], self.lo_done[j])
        s = j % SPLIT_SLOTS
        hi, lo = (self.m[k][s][:, 0:A * B].rearrange("p (a b) -> p a b", a=A) for k in ("hi", "lo"))
        return j, hi, lo

    def bank(self):
        b = self.next_bank
        self.next_bank = (b + 1) % 8
        assert self.bank_free[b] != "held"
        self.pe.wait(self.bank_free[b])
        self.bank_free[b] = "held"
        return b, self.m["banks"][b]

    def mm(self, out, lhs, rhs, start=True, stop=True, mark=False):
        op = lambda e: e.matmul(out, lhs, rhs, start=start, stop=stop)
        return self.pe.run(op) if mark else self.pe.quiet(op)

    def mm3(self, out, w, x, start, stop, mark=False):
        self.mm(out, w[0], x[0], start=start, stop=False)
        self.mm(out, w[0], x[1], start=False, stop=False)
        return self.mm(out, w[1], x[0], start=False, stop=stop, mark=mark)

    def transpose(self, out, in_, mark=False):
        n = in_.shape[0]
        op = lambda e: e.transpose(out, in_, self.m["ident"][0:n, 0:n])
        return self.pe.run(op) if mark else self.pe.quiet(op)

    def project(self, w_dram, n_out, x, N, evacuate, backwards=False, order=None):
        K = w_dram.shape[0] // P
        view = w_dram.rearrange("(k p) n -> p k n", p=P)
        width = min(2 * P, n_out)
        for c0 in sorted(range(0, n_out, width), reverse=backwards):
            if self.norming and N == 2 * S:
                unit, hi, lo = self.weights(view[:, :, c0:c0 + width], ahead=SPLIT_SLOTS - 1)
                taken = self.start_product(unit, hi, lo)
            else:
                unit, hi, lo = self.weights(view[:, :, c0:c0 + width])
                taken = self.product(unit, hi, lo, width, K, x, N, self.advance if self.norming else None,
                                     order)
            for i, (b, ps, mark) in enumerate(taken):
                evacuate(c0 // P + i, b, ps, mark)
        return mark

    def project_gated(self, w_dram, layer, slot):
        x, x0, x1 = (self.stage_in(t0, n) for t0, n in ((0, 2 * S), (0, S), (S, S)))
        view = w_dram.rearrange("(k p) n -> p k n", p=P)
        residual = self.add_gated(layer, slot, (0, 1))

        def add(d, b, ps, mark):
            self.bank_free[b] = residual(d, ps, mark)

        self.project(w_dram[:, 0:D - 2 * P], D - 2 * P, x, 2 * S, add)
        unit, hi, lo = self.weights(view[:, :, D - 2 * P:])
        for s in (0, 1):
            residual = self.add_gated(layer, slot, (s,))
            taken = self.open_banks(2 * P)
            marks = self.accumulate(hi, lo, taken, DC, (x0, x1)[s], 0, S,
                                    self.start_norm if s else None)
            self.in_read = marks[1]
            for j in (0, 1):
                self.bank_free[taken[j][2]] = residual(DC - 2 + j, taken[j][3], marks[j])
        self.used[unit] = marks[1]
        self.advance()

    def open_banks(self, width):
        return [(j, min(P, width - j)) + self.bank() for j in range(0, width, P)]

    def accumulate(self, hi, lo, taken, K, x, t0, n, midway=None, order=None):
        marks = []
        for i, k in enumerate(order or range(K)):
            if i == K // 2 and midway:
                midway()
            x_k = x(k)
            for j, w, b, ps in taken:
                mark = self.mm3(ps[0:w, t0:t0 + n], (hi[:, k, j:j + w], lo[:, k, j:j + w]), x_k,
                                i == 0, i == K - 1, mark=i == K - 1)
                if i == K - 1:
                    marks.append(mark)
        return marks

    def product(self, unit, hi, lo, width, K, x, N, midway=None, order=None):
        taken = self.open_banks(width)
        marks = self.accumulate(hi, lo, taken, K, x, 0, N, midway, order)
        self.used[unit] = marks[-1]
        return [(t[2], t[3], mark) for t, mark in zip(taken, marks)]

    def start_product(self, unit, hi, lo):
        taken = self.open_banks(2 * P)
        self.accumulate(hi, lo, taken, DC, self.stage_in(0, S), 0, S, self.advance)
        marks = self.accumulate(hi, lo, taken, DC, self.stage_in(S, S), S, S)
        self.used[unit] = marks[-1]
        return [(t[2], t[3], mark) for t, mark in zip(taken, marks)]

    def start_norm(self):
        self.norming = self.norm[2]
        self.advance()

    def advance(self):
        if next(self.norming, "over") == "over":
            self.norming = None

    def stage_in(self, lo_t, n):
        hi, lo = self.m["in_hi"], self.m["in_lo"]
        streams = range(lo_t // S, (lo_t + n) // S)

        def chunk(k):
            ready = self.in_ready[k]
            self.pe.wait([ready[s] for s in streams] if isinstance(ready, dict) else ready)
            return hi[:, k, lo_t:lo_t + n], lo[:, k, lo_t:lo_t + n]
        return chunk

    def setup(self):
        m, a, dve, pe, sync = self.m, self.a, self.dve, self.pe, self.sync
        tok = m["tmp"][:, :].rearrange("p (s t d) -> p s t d", s=2, t=2)
        x_in = sync.dma(tok[:, 0, :, :], a["x"].rearrange("b (t p) d -> p (b t) d", p=P), self.slot["tokens"])
        consts = sync.dma(m["ident"][:, :], a["k_ident"], self.slot["consts"])
        self.load_until(RAW_SLOTS)
        self.row_plan = [
            [(0, "ln_gain", 48), (48, "ln_bias", 48)],
            [(0, "norm_g_2", 48), (48, "pool_scale", 8), (56, "final_g_2", 8), (64, "mla_g_q_2", 3),
             (67, "mla_g_kv_2", 1), (68, "c_2", 8), (76, "c_ctx_2", 8)],
            [(0, "ada_b_2.0", 72)],
            [(0, "ada_b_2.1", 72)],
        ]
        self.col = {}
        for g, parts in enumerate(self.row_plan):
            for r0, name, n in parts:
                self.rows_landed = sync.dma(m["stat"][r0:r0 + n, 3, g * P:(g + 1) * P], a[name],
                                            self.slot["rows"])
                self.col[name] = g * P + r0
        self.context_landed = sync.dma(tok[:, 1, :, :], a["ctx_2"].rearrange("b (t p) d -> p (b t) d", p=P),
                                       self.slot["context"])
        self.const_tables = sync.dma(m["const"][:, :], a["k_block1"], self.slot["table"])
        dve.run(lambda e: e.memset(m["ones"][:, :], 1.0))
        self.mean_ready = dve.run(lambda e: e.memset(m["mean_w"][:, :], 1.0 / D))
        self.rpb_zero = dve.run(lambda e: e.memset(m["rpb"][:, :], 0.0))
        pe.wait(consts)
        self.transpose_in(tok[:, 0], x_in, 0)

    def columns(self):
        m, act, pe = self.m, self.act, self.pe
        pe.wait(self.rows_landed)
        b, ps = self.bank()
        sizes = [parts[-1][0] + parts[-1][2] for parts in self.row_plan]
        for g, n in enumerate(sizes):
            mark = self.transpose(ps[:, g * P:g * P + n], m["stat"][0:n, 3, g * P:(g + 1) * P], mark=g == 3)
        for g, n in enumerate(sizes):
            read = act.run(lambda e, g=g, n=n: e.activation(
                m["cols"][:, g * P:g * P + n], ps[:, g * P:g * P + n], ACT.Copy), mark)
        self.bank_free[b] = self.cols_ready = read
        self.stat_read = [mark]
        c0 = self.col["c_2"]
        c_view = m["cols"][:, c0:c0 + 16].rearrange("p (v d) -> p d v", v=2)
        self.c_ready = act.run(lambda e: e.activation(m["c_silu"][:, :, :], c_view, ACT.Silu), read)

    def first_gate(self, gate, up):
        products = [self.product(*self.weights(gate), 2 * P, DC, self.stage_in(0, S), S)]
        self.columns()
        return products

    def transpose_in(self, tok, landed, stream):
        m, t0, low_parts = self.m, stream * S, []
        self.pe.wait(landed)
        for d in range(DC):
            b, ps = self.bank()
            for t in range(2):
                mark = self.transpose(ps[:, t * P:(t + 1) * P], tok[:, t, d * P:(d + 1) * P], mark=t == 1)
            x, hi, lo = (m[k][:, d, t0:t0 + S] for k in ("x", "in_hi", "in_lo"))
            done = self.dve.run(lambda e, x=x, ps=ps: e.tensor_copy(x, ps[:, 0:S]), mark)
            self.bank_free[b] = self.x_ready[stream * DC + d] = done
            if stream == 0:
                high = self.act.run(lambda e, hi=hi, x=x: e.activation(hi, x, ACT.Copy), done)
                low_parts.append(lambda lo=lo, x=x, hi=hi, high=high: self.in_ready.append(
                    self.dve.run(lambda e: e.tensor_tensor(lo, x, hi.bitcast(F32), ALU.subtract), high)))
                if d:
                    low_parts[d - 1]()
        if low_parts:
            low_parts[-1]()
        self.tmp_read = self.tmp_read + [mark]

    def ada_tick(self):
        self.ada_ticks += 1
        if not self.ada_halves or self.ada_ticks % self.ada_period:
            return
        layer, n, half = self.ada_halves.pop(0)
        if self.dry:
            view = self.a["ada_w_2"][layer].rearrange("(k p) n -> p k n", p=P)
            src = view[:, 4 * half:4 * half + 4, 512 * n:512 * n + 512]
            self.plan.append(([(0, src)], 4, 512, (layer, n, half)))
        if half:
            self.ada_sum(layer, n)

    def ada_products(self, i, layer, n, half):
        m, acc = self.m, self.m["ada_acc"]
        raw = m["raw"][i % RAW_SLOTS][:, :].rearrange("p (k n) -> p k n", k=4)
        added = {c: self.ada_done.get((layer, n, 0)) for c in range(2)}
        for k in range(4):
            for c in range(2):
                o, w, factor = acc[:, c, :], raw[:, k, :], m["c_silu"][:, 4 * half + k, c:c + 1]
                if half == k == 0:
                    op = lambda e, o=o, w=w, f=factor: e.tensor_scalar(o, w, f, None, ALU.mult)
                else:
                    op = lambda e, o=o, w=w, f=factor: e.scalar_tensor_tensor(o, w, f, o, ALU.mult, ALU.add)
                mark = added[c] = self.dve.run(op, self.raw_landed[i], self.c_ready, self.ada_summed,
                                               added.get(c))
        self.raw_read[i] = self.ada_done[layer, n, half] = mark

    def ada_sum(self, layer, n):
        m, acc = self.m, self.m["ada_acc"]
        self.pe.wait(self.ada_done.get((layer, n, 1)), self.mean_ready)
        b, ps = self.bank()
        for j in range(4):
            for c in range(2):
                mark = self.mm(ps[:, 2 * j + c:2 * j + c + 1], acc[:, c, j * P:(j + 1) * P],
                               m["ones"][:, 0:1], mark=j == 3 and c == 1)
        self.ada_summed = mark
        bias = self.col[f"ada_b_2.{layer}"] + 4 * n
        bias = m["cols"][:, bias:bias + 4][:, :, None].broadcast_to([P, 4, 2])
        done = self.dve.run(lambda e: e.tensor_tensor(
            m["mod"][:, layer, 4 * n:4 * n + 4, :], ps[:, 0:8].rearrange("p (j c) -> p j c", c=2), bias,
            ALU.add), mark, self.cols_ready)
        self.bank_free[b] = self.mod_ready[layer] = done

    def ffn(self, w_gate, w_up, w_down, N, residual, extra=None, in_down=None,
            start=None):
        m, act, dve, pe = self.m, self.act, self.dve, self.pe
        x = self.stage_in(0, N)
        gate, up = (w.rearrange("(k p) n -> p k n", p=P) for w in (w_gate, w_up))
        down = w_down.rearrange("(f p) n -> p f n", p=P)
        h_hi, h_lo = (m[k][:, :].rearrange("p (f t) -> p f t", t=N) for k in ("h_hi", "h_lo"))
        room = H_CHUNKS * S // N
        groups = [(0, FC)] if FC <= room else [(0, room), (room, FC)]
        gates = m["stat"]
        split_h = []
        for first, last in groups:
            h_ready = {}
            for f0 in range(first, last, 2):
                products = start(gate[:, :, 0:2 * P], up[:, :, 0:2 * P]) if start and f0 == 0 else []
                for w in (gate, up)[len(products):]:
                    if self.norming:
                        unit, hi, lo = self.weights(w[:, :, 0:2 * P], ahead=SPLIT_SLOTS - 1)
                        products.append(self.start_product(unit, hi, lo))
                        continue
                    unit, hi, lo = self.weights(w[:, :, f0 * P:f0 * P + 2 * P])
                    products.append(self.product(unit, hi, lo, 2 * P, DC, x, N))
                    self.ada_tick()
                mark = products[1][1][2]
                self.in_read = mark
                for f in (f0, f0 + 1):
                    (bg, g, g_mark), (bu, u, u_mark) = products[0][f - f0], products[1][f - f0]
                    s = gates[:, f % 2, 0:N]
                    h32 = gates[:, 2 + f % 2, 0:N]
                    dh, dl = h_hi[:, f - first, :], h_lo[:, f - first, :]
                    slot_read = split_h[-2:-1] if len(split_h) > 1 else self.stat_read
                    silu = act.run(lambda e, s=s, g=g: e.activation(s, g[:, 0:N], ACT.Silu), g_mark,
                                   slot_read)
                    self.bank_free[bg] = silu
                    prod = dve.run(lambda e, s=s, u=u, o=h32: e.scalar_tensor_tensor(
                        o, s, 0.5, u[:, 0:N], ALU.mult, ALU.mult), silu, u_mark, slot_read)
                    self.bank_free[bu] = prod
                    hi_w = act.run(lambda e, o=dh, i=h32: e.activation(o, i, ACT.Copy), prod, self.h_read)
                    lo_w = dve.run(lambda e, o=dl, i=h32, h=dh: e.tensor_tensor(
                        o, i, h.bitcast(F32), ALU.subtract), hi_w, self.h_read)
                    split_h.append(lo_w)
                    h_ready[f] = [hi_w, lo_w]
                if extra and f0 == 4:
                    extra()
            self.stat_read = split_h[-1:]
            if last == FC:
                act.quiet(lambda e: e.preload_act_table_set("natural_log_exp_and_others"))
            parts = [(f, min(f + 8, last)) for f in range(first, last, 8)]
            by_stream = DC - 2 if N == 2 * S and last == FC else DC
            for d0 in range(0, by_stream, 2):
                taken = [self.bank(), self.bank()]
                for f0, f1 in parts:
                    unit, hi, lo = self.weights(down[:, f0:f1, d0 * P:d0 * P + 2 * P])
                    if in_down:
                        next(in_down, None)
                    for d in range(2):
                        for f in range(f0, f1):
                            pe.wait(*h_ready[f])
                            mark = self.mm3(taken[d][1][:, 0:N],
                                            (hi[:, f - f0, d * P:d * P + P], lo[:, f - f0, d * P:d * P + P]),
                                            (h_hi[:, f - first, :], h_lo[:, f - first, :]),
                                            f == first, f == last - 1, mark=f == f1 - 1)
                        if f1 == last:
                            b, ps = taken[d]
                            self.bank_free[b] = residual(d0 + d, ps, mark, last == FC)
                    self.used[unit] = mark
                    if d0 < DC - 2:
                        self.ada_tick()
            if by_stream < DC:
                parts = [(first, last - 7), (last - 7, last)]
                units = [self.weights(down[:, f0:f1, by_stream * P:], ahead=SPLIT_SLOTS - i)
                         for i, (f0, f1) in enumerate(parts)]
                for s in (0, 1):
                    taken = [self.bank(), self.bank()]
                    for (f0, f1), (unit, hi, lo) in zip(parts, units):
                        for d in range(2):
                            for f in range(f0, f1):
                                mark = self.mm3(
                                    taken[d][1][:, 0:S],
                                    (hi[:, f - f0, d * P:d * P + P], lo[:, f - f0, d * P:d * P + P]),
                                    [h[:, f - first, s * S:s * S + S] for h in (h_hi, h_lo)],
                                    f == first, f == last - 1, mark=f == f1 - 1)
                            if f1 == last:
                                b, ps = taken[d]
                                self.bank_free[b] = residual(by_stream + d, ps, mark, True, (s,))
                        if s == 1:
                            self.used[unit] = mark
                            if f0 == parts[0][0]:
                                self.start_norm()
                self.advance()
            self.h_read = mark

    def add_scaled(self, t0):
        def residual(d, ps, mark, last=True):
            x = self.m["x"][:, d, t0:t0 + S]
            done = self.dve.run(lambda e: e.scalar_tensor_tensor(
                x, x, ALPHA, ps[:, 0:S], ALU.mult, ALU.add), mark, self.x_ready[d])
            self.x_ready[d] = done
            self.feed_norm(d)
            return done
        return residual

    def add_gated(self, layer, slot, streams):
        def residual(d, ps, mark, last=True, part=streams):
            for s in part:
                x = self.m["x"][:, d, s * S:s * S + S]
                gate = self.m["mod"][:, layer, slot * DC + d, s:s + 1]
                p = ps[:, (s - part[0]) * S:(s - part[0] + 1) * S]
                done = self.dve.run(lambda e, x=x, g=gate, p=p: e.scalar_tensor_tensor(
                    x, p, g, x, ALU.mult, ALU.add), mark, self.x_ready[s * DC + d], self.mod_ready[layer])
                self.x_ready[s * DC + d] = done
            if last:
                self.feed_norm(d, part)
            return done
        return residual

    def norm_of(self, kind, streams=(0,), norming=None):
        self.norm = (kind, streams, norming)

    def feed_norm(self, d, streams=(0,)):
        m, act, dve = self.m, self.act, self.dve
        kind, all_streams, _ = self.norm
        t0, N = streams[0] * S, S * len(streams)
        tmp = m["tmp"][:, :].rearrange("p (d t) -> p d t", d=DC)
        ready = [self.x_ready[s * DC + d] for s in streams]
        x = m["x"][:, :, t0:t0 + N]
        added_before = [self.norm_added.get(s) for s in streams]
        if kind == "rms":
            total = tmp[:, 0, t0:t0 + N]
            free = [self.tmp_read, self.norm_chunk_read.get(d)]
            added = act.run(lambda e: e.activation(tmp[:, d, t0:t0 + N], x[:, d, :], ACT.Square), ready, free)
            if d:
                added = dve.run(lambda e: e.tensor_tensor(total, total, tmp[:, d, t0:t0 + N], ALU.add), added,
                                added_before)
        elif d:
            total = tmp[:, 0, S:2 * S]
            first = x[:, 0, :] if d == 1 else total
            added = dve.run(lambda e: e.tensor_tensor(total, first, x[:, d, :], ALU.add), ready,
                            self.tmp_read, added_before if d > 1 else self.x_ready[0])
        else:
            return
        for s in streams:
            self.norm_added[s] = added
        if d == DC - 1 and len(all_streams) == 1:
            self.mean_of(all_streams[0], total)

    def mean_of(self, stream, total):
        b, ps = self.bank()
        self.pe.wait(self.norm_added[stream], self.mean_ready)
        mark = self.mm(ps[:, 0:S], self.m["mean_w"][:, :], total, mark=True)
        self.norm_sum[stream] = (b, ps, mark)
        self.norm_chunk_read = {}

    def inv_root(self, b, ps, N, mark, factor, eps, silu_next=False, t0=0, meanwhile=None):
        m, act, dve = self.m, self.act, self.dve
        v, y, t = (m["stat"][:, i, t0:t0 + N] for i in range(3))
        var = dve.run(lambda e: e.tensor_scalar(v, ps[:, 0:N], factor, eps, ALU.mult, ALU.add),
                      mark, self.stat_read)
        self.bank_free[b] = var
        ln = act.run(lambda e: e.activation(y, v, ACT.Ln), var)
        ex = act.run(lambda e: e.activation(y, y, ACT.Exp, scale=-0.5), ln)
        if silu_next:
            act.quiet(lambda e: e.preload_act_table_set("silu_and_others"))
        if meanwhile:
            meanwhile()
        n1 = dve.run(lambda e: e.scalar_tensor_tensor(t, v, -0.5, y, ALU.mult, ALU.mult), ex)
        n2 = dve.run(lambda e: e.tensor_tensor(t, t, y, ALU.mult), n1)
        return y, dve.run(lambda e: e.scalar_tensor_tensor(y, t, 1.5, y, ALU.add, ALU.mult), n2)

    def layer_norm(self, index, permuted=False, split=True, meanwhile=None):
        m, act, dve, pe = self.m, self.act, self.dve, self.pe
        x = m["x"][:, :, 0:S]
        tmp = m["tmp"][:, :].rearrange("p (d t) -> p d t", d=DC)
        centred, square = tmp[:, :, 0:S], tmp[:, :, S:2 * S]
        b, ps, mark = self.norm_sum[0]
        b2, ps2 = self.bank()
        step = 2
        for r0 in range(0, DC, step):
            r = slice(r0, r0 + step)
            mean = ps[:, 0:S][:, None, :].broadcast_to([P, step, S])
            sub = dve.run(lambda e, r=r, mean=mean: e.tensor_tensor(
                centred[:, r, :], x[:, r, :], mean, ALU.subtract), mark, self.tmp_read)
            sq = act.run(lambda e, r=r: e.activation(square[:, r, :], centred[:, r, :], ACT.Square), sub)
            pe.wait(sq)
            for d in range(r0, r0 + step):
                var = self.mm(ps2[:, 0:S], m["mean_w"][:, :], square[:, d, :], d == 0, d == DC - 1,
                              mark=d == DC - 1)
        self.bank_free[b] = sub
        if meanwhile:
            meanwhile()
        y, root = self.inv_root(b2, ps2, S, var, 1.0, LN_EPS, silu_next=split and index % 3 != 0)
        if split:
            self.in_ready = []
        low_parts = []
        for d in range(DC):
            gain = m["cols"][:, self.col["ln_gain"] + index * DC + d:][:, 0:1]
            bias = m["cols"][:, self.col["ln_bias"] + index * DC + d:][:, 0:1]
            c, o = centred[:, d, :], x[:, d, :]
            hi, lo = m["in_hi"][:, d, 0:S], m["in_lo"][:, d, 0:S]
            if permuted:
                c_, o_ = (v.rearrange("p (c b a) -> p c b a", a=4, b=4) for v in (c, o))
                hi, lo = (v.rearrange("p (a b c) -> p c b a", a=4, b=4) for v in (hi, lo))
            else:
                c_, o_ = c, o
            normed = dve.run(lambda e, c=c: e.tensor_tensor(c, c, y, ALU.mult), root)
            high = None
            if split:
                high = act.run(lambda e, hi=hi, c=c_, g=gain, b=bias: e.activation(
                    hi, c, ACT.Identity, scale=g, bias=b), normed, self.in_read, self.cols_ready)
            if d % 2 == 0:
                full = dve.run(lambda e, o=o, c=c, g=gain, b=bias: e.tensor_scalar(
                    o, c, g, b, ALU.mult, ALU.add), normed, self.cols_ready)
            else:
                full = act.run(lambda e, o=o, c=c, g=gain, b=bias: e.activation(
                    o, c, ACT.Identity, scale=g, bias=b), normed, self.cols_ready)
            self.x_ready[d] = full
            self.norm_chunk_read[d] = [full, high, var]
            low_parts.append(lambda lo=lo, o=o_, hi=hi, full=full, high=high: self.in_ready.append(
                dve.run(lambda e: e.tensor_tensor(lo, o, hi.bitcast(F32), ALU.subtract),
                        full, high, self.in_read)))
            if split and d:
                low_parts[d - 1]()
            if not split and d > 1:
                self.feed_norm(d - 2)
        self.stat_read = [normed]
        self.tmp_read = [full, high, normed]
        if split:
            low_parts[d]()
        else:
            self.feed_norm(d - 1)
            self.feed_norm(d)

    def rms_gain(self, layer, i, scale):
        g0 = self.col["norm_g_2"] + (layer * 3 + i) * DC
        norm_g = self.m["cols"][:, g0:g0 + DC][:, :, None].broadcast_to([P, DC, 2])
        gain, scales = self.m["gain"], self.m["mod"][:, layer, scale * DC:scale * DC + DC, :]
        return self.dve.run(lambda e: e.scalar_tensor_tensor(
            gain[:, :, :], scales, 1.0, norm_g, ALU.add, ALU.mult),
            self.mod_ready[layer], self.cols_ready)

    def rms_chunks(self, layer, shift, s, chunks, ready, *marks):
        m, act, dve = self.m, self.act, self.dve
        tmp = m["tmp"][:, :].rearrange("p (d t) -> p d t", d=DC)
        tok = slice(s * S, s * S + S)
        y = m["stat"][:, 1, tok]
        high = {}

        def low_part(d):
            o, hi, lo = (v[:, d, tok] for v in (tmp, m["in_hi"], m["in_lo"]))
            sh = m["mod"][:, layer, shift * DC + d, s:s + 1]
            ready[d][s] = dve.run(lambda e: e.scalar_tensor_tensor(
                lo, o, sh, hi.bitcast(F32), ALU.add, ALU.subtract), high[d], self.in_read)

        for d in chunks:
            x, o, hi = (v[:, d, tok] for v in (m["x"], tmp, m["in_hi"]))
            g, sh = m["gain"][:, d, s:s + 1], m["mod"][:, layer, shift * DC + d, s:s + 1]
            scaled = dve.run(lambda e, o=o, x=x, g=g: e.scalar_tensor_tensor(
                o, x, g, y, ALU.mult, ALU.mult), *marks)
            high[d] = act.run(lambda e, hi=hi, o=o, sh=sh: e.activation(
                hi, o, ACT.Identity, bias=sh), scaled, self.in_read)
            if d - 1 in high:
                low_part(d - 1)
        low_part(d)
        return ready[d][s]

    def rms_both(self, layer, i, shift, scale):
        total = self.m["tmp"][:, 0:2 * S]
        silu_next = i != 1
        gained = self.rms_gain(layer, i, scale)
        ready = [{} for _ in range(DC)]
        self.mean_of(0, total[:, 0:S])
        b, ps, mark0 = self.norm_sum[0]
        y, root0 = self.inv_root(b, ps, S, mark0, 1.0, RMS_EPS)
        self.rms_chunks(layer, shift, 0, (0, 1), ready, root0, mark0, gained)
        yield
        self.in_ready = ready
        self.rms_chunks(layer, shift, 0, (2, 3), ready, root0, mark0, gained)
        yield
        self.mean_of(1, total[:, S:])
        b, ps, mark1 = self.norm_sum[1]
        y, root1 = self.inv_root(b, ps, S, mark1, 1.0, RMS_EPS, silu_next=silu_next, t0=S,
                                 meanwhile=lambda: self.rms_chunks(layer, shift, 0, (4, 5), ready, root0))
        self.rms_chunks(layer, shift, 0, (6, 7), ready, root0)
        done = self.rms_chunks(layer, shift, 1, range(DC), ready, root1, mark1)
        self.stat_read = self.tmp_read = [done]

    def rms_mod(self, layer, i, shift, scale, s=0, silu_next=True):
        gained = self.rms_gain(layer, i, scale)
        b, ps, mark = self.norm_sum[s]
        y, root = self.inv_root(b, ps, S, mark, 1.0, RMS_EPS, silu_next=silu_next, t0=s * S)
        if not isinstance(self.in_ready[0], dict):
            self.in_ready = [{} for _ in range(DC)]
        done = self.rms_chunks(layer, shift, s, range(DC), self.in_ready, root, mark, gained)
        self.stat_read = self.tmp_read = [done]

    def pool_mixer(self):
        m, act, dve, pe, a = self.m, self.act, self.dve, self.pe, self.a
        PAD, W = 8, S + 16
        padded = m["tmp"][:, 0:DC * W].rearrange("p (d t) -> p d t", d=DC)
        sums = m["tmp"][:, DC * W:DC * W + 4 * W].rearrange("p (i d t) -> p i d t", i=2, d=2)
        mean = m["work"][:, 0:0 + 2 * S]
        zero = dve.run(lambda e: e.memset(padded[:, :, 0:PAD], 0.0), self.tmp_read)
        zero = dve.run(lambda e: e.memset(padded[:, :, PAD + S:], 0.0))
        u_ready, mixed_ready = {}, {}
        h_hi, h_lo = (m[k][:, :].rearrange("p (f t) -> p f t", t=S) for k in ("h_hi", "h_lo"))
        inverse = m["const"][:, 0:4 * S].rearrange("p (g t) -> p g t", g=4)
        prev = [self.stat_read, self.stat_read]

        def window(g):
            stat = m["stat"][:, g % 2, :].rearrange("p (d t) -> p d t", d=2)
            src, half, n, step = padded[:, 2 * g:2 * g + 2, :], 1, W, zero
            for i in range(g + 1):
                n -= half
                dst = sums[:, i % 2, :, 0:n]
                step = dve.run(lambda e, d=dst, s=src, n=n, h=half: e.tensor_tensor(
                    d, s[:, :, 0:n], s[:, :, h:h + n], ALU.add), step, u_ready[2 * g + 1])
                src, half = sums[:, i % 2], half * 2
            first = PAD - half // 2
            inv = inverse[:, g, :][:, None, :].broadcast_to([P, 2, S])
            u = padded[:, 2 * g:2 * g + 2, PAD:PAD + S]
            step = dve.run(lambda e: e.tensor_tensor(stat, src[:, :, first:first + S], inv, ALU.mult),
                           step, self.const_tables, prev[g % 2])
            step = dve.run(lambda e: e.tensor_tensor(stat, stat, u, ALU.subtract), step)
            hi, lo = h_hi[:, 2 * g:2 * g + 2, :], h_lo[:, 2 * g:2 * g + 2, :]
            high = act.run(lambda e: e.activation(hi, stat, ACT.Copy), step, self.h_read)
            low = dve.run(lambda e: e.tensor_tensor(lo, stat, hi.bitcast(F32), ALU.subtract), high,
                          self.h_read)
            prev[g % 2] = [high, low]
            mixed_ready[g] = low
            return step

        def keep(d, b, ps, mark):
            u_ready[d] = act.run(lambda e: e.activation(padded[:, d, PAD:PAD + S], ps[:, 0:S], ACT.Copy),
                                 mark, self.tmp_read)
            self.bank_free[b] = u_ready[d]
            if d % 2:
                windowed.append(window(d // 2))

        windowed = []
        self.in_read = self.project(a["pool_w_in"][0], D, self.stage_in(0, S), S, keep, True)
        self.tmp_read = windowed[-1:]
        view = a["pool_w_group"][0].rearrange("g (c p) e -> p (g c) e", p=P)
        unit, whi, wlo = self.weights(view)
        y_ready = {}
        for e_ in reversed(range(DC)):
            g, j = e_ // 2, (e_ % 2) * P
            pe.wait(mixed_ready[g])
            b, ps = self.bank()
            for c in range(2):
                k = 2 * g + c
                mark = self.mm3(ps[:, 0:S], (whi[:, k, j:j + P], wlo[:, k, j:j + P]),
                                (h_hi[:, k, :], h_lo[:, k, :]), c == 0, c == 1, mark=c == 1)
            t = m["stat"][:, 2 + e_ % 2, 0:S]
            scale = m["cols"][:, self.col["pool_scale"] + e_:][:, 0:1]
            hi, lo = h_hi[:, DC + e_, :], h_lo[:, DC + e_, :]
            scaled = act.run(lambda e, t=t, ps=ps, s=scale: e.activation(t, ps[:, 0:S], ACT.Copy, scale=s),
                             mark, prev[0], y_ready.get(e_ + 2), self.cols_ready)
            self.bank_free[b] = scaled
            high = act.run(lambda e, hi=hi, t=t: e.activation(hi, t, ACT.Copy), scaled)
            y_ready[e_] = dve.run(lambda e, lo=lo, t=t, hi=hi: e.tensor_tensor(
                lo, t, hi.bitcast(F32), ALU.subtract), high)
        self.used[unit] = mark
        self.stat_read = [y_ready[0]]
        residual = self.add_scaled(0)

        def add(d, b, ps, mark):
            self.bank_free[b] = residual(d, ps, mark)

        def y(k):
            pe.wait(y_ready[k])
            return h_hi[:, DC + k, :], h_lo[:, DC + k, :]

        self.h_read = self.project(a["pool_w_out"][0], D, y, S, add, order=range(DC)[::-1])

    def attend(self, items):
        m, act, dve, pe = self.m, self.act, self.dve, self.pe
        buf = m["tmp"][:, 2048:4096].rearrange("p (i n) -> p i n", i=4)
        n_items = len(items)
        st = {}
        exps = [buf[:, 0, :], buf[:, 1, :], m["exp"][:, :]]
        for step in range(n_items + 3):
            if step < n_items:
                it = items[step]
                n, s = it["n"], st.setdefault(step, {})
                b, ps = self.bank()
                s["scores"] = it["scores"](ps)
                p = exps[step % 3][:, 0:n]
                peak, neg, total = (m["soft"][:, i, step % 4:step % 4 + 1] for i in range(3))
                slot_free = st[step - 3]["turned"] if step > 2 else self.tmp_read
                if it["bias"]:
                    ready = it["bias"](p, ps, [s["scores"], slot_free])
                    self.bank_free[b] = ready
                    src = p
                else:
                    ready, src = s["scores"], ps[:, 0:n]
                mx = dve.run(lambda e, o=peak, i=src: e.tensor_reduce(o, i, AX_X, ALU.max), ready)
                ng = dve.run(lambda e, o=neg, i=peak, c=-it["scale"]: e.tensor_scalar(
                    o, i, c, None, ALU.mult), mx)
                s["exp"] = act.run(lambda e, o=p, i=src, ng=neg, t=total, c=it["scale"]: e.activation(
                    o, i, ACT.Exp, bias=ng, scale=c, accum_out=t), ng, slot_free)
                if not it["bias"]:
                    self.bank_free[b] = s["exp"]
            i = step - 2
            if 0 <= i < n_items:
                it, s = items[i], st[i]
                n = it["n"]
                p, turned = exps[i % 3][:, 0:n], buf[:, 2 + i % 2, 0:n]
                b, ps = self.bank()
                pe.wait(s["exp"])
                for k in range(n // P):
                    s["turned"] = self.transpose(ps[:, k * P:(k + 1) * P], p[:, k * P:(k + 1) * P],
                                                 mark=k == n // P - 1)
                free = st[i - 2]["summed"] if i > 1 else self.tmp_read
                s["back"] = act.run(lambda e, o=turned, i=ps, n=n: e.activation(o, i[:, 0:n], ACT.Copy),
                                    s["turned"], free)
                self.bank_free[b] = s["back"]
            i = step - 3
            if i >= 0:
                it, s = items[i], st[i]
                n = it["n"]
                turned = buf[:, 2 + i % 2, 0:n]
                total, inv = (m["soft"][:, k, i % 4:i % 4 + 1] for k in (2, 3))
                b, ps = self.bank()
                pe.wait(s["back"], it.get("ready"))
                last = n // P - 1
                for k in range(last + 1):
                    s["summed"] = self.mm(ps[:, 0:it["width"]], turned[:, k * P:(k + 1) * P],
                                          it["values"][k], k == 0, k == last, mark=k == last)
                rec = dve.run(lambda e, o=inv, i=total: e.reciprocal(o, i), s["exp"])
                done = dve.run(lambda e, o=it["o"], ps=ps, w=it["width"], inv=inv: e.tensor_scalar(
                    o, ps[:, 0:w], inv, None, ALU.mult), s["summed"], rec, self.tmp_read)
                self.bank_free[b] = done
        return done, s["summed"]

    def turn_rows(self, rows, n_tiles, chunk0, n_chunks, ready):
        m, act, dve, pe = self.m, self.act, self.dve, self.pe
        N = n_tiles * P
        pe.wait(ready)
        marks = []
        for c in range(n_chunks):
            b, ps = self.bank()
            for t in range(n_tiles):
                mark = self.transpose(ps[:, t * P:(t + 1) * P], rows(t)[:, c * P:(c + 1) * P],
                                      mark=t == n_tiles - 1)
            hi, lo = (m[k][:, chunk0 + c, 0:N] for k in ("in_hi", "in_lo"))
            high = act.run(lambda e, hi=hi, ps=ps: e.activation(hi, ps[:, 0:N], ACT.Copy), mark,
                           self.in_read)
            low = dve.run(lambda e, lo=lo, ps=ps, hi=hi: e.tensor_tensor(
                lo, ps[:, 0:N], hi.bitcast(F32), ALU.subtract), high, self.in_read)
            self.bank_free[b] = low
            marks.append(low)
        self.tmp_read = [mark]
        return marks

    def value_rows(self, w_dram, x, n_tiles, dst):
        m, act = self.m, self.act
        K, n = w_dram.shape[0] // P, w_dram.shape[1]
        view = w_dram.rearrange("(k p) n -> p k n", p=P)
        width = min(UNIT // K, 512, n)
        done = []
        for c0 in range(0, n, width):
            unit, hi, lo = self.weights(view[:, :, c0:c0 + width])
            for t in range(n_tiles):
                b, ps = self.bank()
                for k in range(K):
                    xh, xl = x(k)
                    tok = slice(t * P, (t + 1) * P)
                    self.mm(ps[:, 0:width], xh[:, tok], hi[:, k, :], k == 0, False)
                    self.mm(ps[:, 0:width], xh[:, tok], lo[:, k, :], False, False)
                    mark = self.mm(ps[:, 0:width], xl[:, tok], hi[:, k, :], False, k == K - 1,
                                   mark=k == K - 1)
                o = dst(t)[:, c0:c0 + width]
                copied = act.run(lambda e, o=o, ps=ps: e.activation(o, ps[:, 0:width], ACT.Copy), mark,
                                 self.h_read)
                self.bank_free[b] = copied
            self.used[unit] = mark
        return copied, mark

    def dilated_mixer(self):
        m, act, dve, pe, a = self.m, self.act, self.dve, self.pe, self.a
        w_qkv = a["attn_w_qkv"][0]
        quad = 4 * HEAD
        size = DIL_GROUPS * 2 * S
        slopes = (2.0 ** (-8.0 * np.arange(1, 49) / 48)).reshape(3, 16).astype(np.float32)
        dist = m["const"][:, 4 * S:].rearrange("p (t n) -> p t n", t=2)
        rows = m["tmp"][:, 0:2048].rearrange("p (t n) -> p t n", t=2)
        x = self.stage_in(0, S)
        summed = [self.h_read, self.h_read]
        start_free = self.h_read
        for hq in range(HEADS // 4):
            buf = m["work"][:, (hq % 2) * 3 * size:(hq % 2 + 1) * 3 * size]
            qT, kT = (buf[:, i * size:(i + 1) * size].rearrange("p (g c t) -> p g c t", g=3, c=2)
                      for i in range(2))
            v = buf[:, 2 * size:3 * size].rearrange("p (t g n) -> p t g n", t=2, g=3)
            self.h_read = summed[hq % 2]
            ready = []
            for g in range(DIL_GROUPS):
                for which, dst, factor in ((0, qT, HEAD ** -0.5), (1, kT, 1.0)):
                    def keep(c, b, ps, mark, g=g, dst=dst, factor=factor):
                        done = act.run(lambda e: e.activation(dst[:, g, c, :], ps[:, 0:S], ACT.Copy,
                                                              scale=factor), mark, self.h_read)
                        self.bank_free[b] = done
                        ready.append(done)
                    c0 = (g * 3 + which) * D + hq * quad
                    self.project(w_qkv[:, c0:c0 + quad], quad, x, S, keep)
                c0 = (g * 3 + 2) * D + hq * quad
                copied, self.in_read = self.value_rows(
                    w_qkv[:, c0:c0 + quad], x, 2, lambda t, g=g: v[:, t, g, :])
                ready.append(copied)
            items = []
            pe.wait(*ready)
            for h in range(4):
                for t in range(2):
                    c, r = h // 2, (h % 2) * HEAD
                    q0 = t * P

                    def scores(ps, c=c, r=r, q0=q0):
                        for g, k0, n, col in ((0, 0, S, 0), (1, q0, P, S), (2, q0, P, S + P)):
                            mark = self.mm(ps[:, col:col + n], qT[r:r + HEAD, g, c, q0:q0 + P],
                                           kT[r:r + HEAD, g, c, k0:k0 + n], mark=g == 2)
                        return mark

                    def bias(o, ps, marks, head=hq * 4 + h, t=t):
                        for g, col, n in ((0, 0, S), (1, S, P), (2, S + P, P)):
                            mark = dve.run(lambda e, s=-float(slopes[g, head]), col=col, n=n:
                                           e.scalar_tensor_tensor(o[:, col:col + n], dist[:, t, col:col + n],
                                                                  s, ps[:, col:col + n], ALU.mult, ALU.add),
                                           *marks, self.const_tables)
                        return mark

                    e0 = h * HEAD
                    items.append(dict(
                        n=512, scores=scores, bias=bias, scale=1.0, width=HEAD,
                        values=[v[:, 0, 0, e0:e0 + HEAD], v[:, 1, 0, e0:e0 + HEAD],
                                v[:, t, 1, e0:e0 + HEAD], v[:, t, 2, e0:e0 + HEAD]],
                        o=rows[:, t, (hq * 4 + h) * HEAD:(hq * 4 + h + 1) * HEAD]))
            done, summed[hq % 2] = self.attend(items)
            self.tmp_read = [summed[hq % 2]]
        self.h_read = summed[(HEADS // 4 - 1) % 2]
        turned = self.turn_rows(lambda t: rows[:, t, :], 2, 0, DC, done)
        residual = self.add_scaled(0)
        tmp = m["stat"]

        def add(d, b, ps, mark):
            t = tmp[:, d % 2, 0:S]
            natural = ps[:, 0:S].rearrange("p (a b c) -> p c b a", a=4, b=4)
            copied = act.run(lambda e: e.activation(t.rearrange("p (c b a) -> p c b a", a=4, b=4), natural,
                                                    ACT.Copy), mark, self.x_ready[max(d - 2, 0)],
                             self.stat_read)
            self.bank_free[b] = copied
            residual(d, t, copied)

        self.in_ready = turned
        self.in_read = self.project(a["attn_w_out"][0], D, self.stage_in(0, S), S, add)
        self.stat_read = [self.x_ready[DC - 1]]

    def load_rpb(self):
        pad = self.m["rpb"]
        src = self.a["ab_rpb_2"][0].rearrange("h r c -> (h r) c")
        first = GRID_W - 1 - (RPB_W // 2)
        got = self.sync.dma(pad[:, first:first + RPB_W], src, self.slot["rpb"], self.rpb_zero)
        copies = pad[:, None, :].broadcast_to([NA_HEADS * RPB_H, GRID_W, P])
        self.rpb_stored = self.sync.dma(self.a["scratch"], copies, self.slot["rpb"], got)

    def load_mixer_tables(self):
        self.const_tables = self.sync.dma(self.m["const"][:, 0:1792], self.a["k_mixer"],
                                          self.slot["table"], self.const_read)

    def na_bias_loads(self):
        bias = self.m["work"][:, 8192:8192 + 4096].rearrange("p (h t n) -> p h t n", h=NA_HEADS, t=2)
        self.na_bias, scratch, free = bias, self.a["scratch"], self.h_read
        batches, self.na_bias_ready = [], {}
        self.sync.wait(self.rpb_stored)
        for h in range(NA_HEADS):
            for qr in range(GRID_H):
                row = h * RPB_H + RPB_H // 2 - qr
                src = bass.AP(scratch.tensor, row * GRID_W * P + GRID_W - 1,
                              [[P - 1, GRID_W], [GRID_W * P, GRID_H], [1, GRID_W]])
                p0 = (qr % 2) * GRID_W
                dst = bias[p0:p0 + GRID_W, h, qr // 2, :].rearrange("p (r c) -> p r c", r=GRID_H)
                landed = self.sync.dma(dst, src, self.slot[f"bias{h // 2}"], free)
            if h % 2:
                batches.append((h - 1, landed))
                if h > 1:
                    self.mask_na_bias(*batches[-2])
                if h < NA_HEADS - 1:
                    yield
        yield
        self.mask_na_bias(*batches[-1])

    def mask_na_bias(self, h0, landed):
        mask = self.m["const"][:, 1280:1792].rearrange("p (t n) -> p t n", t=2)
        for h in (h0, h0 + 1):
            bias = self.na_bias[:, h, :, :]
            self.na_bias_ready[h] = self.dve.run(lambda e, bias=bias: e.tensor_tensor(
                bias, bias, mask, ALU.add), landed, self.const_tables)

    def fourier_na_mixer(self, layer):
        m, act, dve, pe, a = self.m, self.act, self.dve, self.pe, self.a
        w_in = a["ab_w_in_2"][0]
        N = 2 * S
        x = self.stage_in(0, N)
        bias_loads = self.na_bias_loads()
        uT, qT, kT, v = (m["work"][:, i * 2048:(i + 1) * 2048].rearrange("p (c t) -> p c t", c=4)
                         for i in range(4))
        ready = {}

        def keeper(name, dst, factor=1.0):
            def keep(c, b, ps, mark):
                ready[name] = act.run(lambda e: e.activation(dst[:, c, :], ps[:, 0:N], ACT.Copy,
                                                             scale=factor), mark, self.h_read)
                self.bank_free[b] = ready[name]
            return keep

        self.project(w_in[:, 0:512], 512, x, N, keeper("u", uT))
        dft_d = m["const"][:, 0:256]
        dft_n = m["const"][:, 256:1280].rearrange("p (k f n) -> p k f n", k=2, f=2)
        spec = m["tmp"][:, :].rearrange("p (t g n) -> p t g n", t=4, g=4)
        pe.wait(ready["u"], self.const_tables)
        for g in range(4):
            for t in range(4):
                b, ps = self.bank()
                mark = self.mm(ps[:, 0:256], uT[:, g, t * P:(t + 1) * P], dft_d, mark=True)
                spec_ready = dve.run(lambda e, ps=ps, t=t, g=g: e.tensor_copy(spec[:, t, g, :], ps[:, 0:256]),
                                     mark, self.tmp_read)
                self.bank_free[b] = spec_ready
        next(bias_loads)
        for c0, name, dst, factor in ((512, "q", qT, HEAD ** -0.5), (1024, "k", kT, 1.0)):
            self.project(w_in[:, c0:c0 + 512], 512, x, N, keeper(name, dst, factor))
            next(bias_loads)
        v_done, self.in_read = self.value_rows(w_in[:, 1536:2048], x, 4, lambda t: v[:, t, :])
        next(bias_loads)
        turned = []
        pe.wait(spec_ready)
        for g in range(4):
            b, ps = self.bank()
            for s in range(2):
                for i, (k, f) in enumerate(((0, 0), (1, 0), (0, 1), (1, 1))):
                    mark = self.mm(ps[:, s * S:(s + 1) * S], spec[:, 2 * s + k, g, f * P:(f + 1) * P],
                                   dft_n[:, k, f, :], i == 0, i == 3, mark=s == 1 and i == 3)
            hi, lo = (m[k][:, g, 0:N] for k in ("in_hi", "in_lo"))
            high = act.run(lambda e, hi=hi, ps=ps: e.activation(hi, ps[:, 0:N], ACT.Copy), mark, self.in_read)
            low = dve.run(lambda e, lo=lo, ps=ps, hi=hi: e.tensor_tensor(
                lo, ps[:, 0:N], hi.bitcast(F32), ALU.subtract), high)
            self.bank_free[b] = low
            turned.append(low)
        self.tmp_read = [mark]
        next(bias_loads, None)
        rows = m["tmp"][:, 0:2048].rearrange("p (t n) -> p t n", t=4)
        pe.wait(ready["q"], ready["k"], v_done)
        items = []
        for t in range(4):
            for h in range(NA_HEADS):
                c, r = h // 2, (h % 2) * HEAD
                k0, n = (0, N) if t < 2 else (S, S)

                def scores(ps, c=c, r=r, t=t, k0=k0, n=n):
                    return self.mm(ps[:, 0:n], qT[r:r + HEAD, c, t * P:(t + 1) * P],
                                   kT[r:r + HEAD, c, k0:k0 + n], mark=True)

                def bias(o, ps, marks, h=h, t=t):
                    dve.run(lambda e: e.tensor_tensor(o[:, 0:S], self.na_bias[:, h, t, :], ps[:, 0:S],
                                                      ALU.add), *marks, self.na_bias_ready[h])
                    return dve.run(lambda e: e.tensor_copy(o[:, S:N], ps[:, S:N]))

                items.append(dict(
                    n=n, scores=scores, bias=bias if t < 2 else None, scale=1.0, width=HEAD,
                    values=[v[:, k, h * HEAD:(h + 1) * HEAD] for k in range(k0 // P, (k0 + n) // P)],
                    o=rows[:, t, h * HEAD:(h + 1) * HEAD]))
        done, summed = self.attend(items)
        self.h_read = summed
        turned += self.turn_rows(lambda t: rows[:, t, :], 4, 4, 4, done)
        self.in_ready = turned
        self.project_gated(a["ab_w_out_2"][0], layer, 5)

    def mla_mixer(self, layer):
        m, act, dve, pe, a = self.m, self.act, self.dve, self.pe, self.a
        N = 2 * S
        tables = act.dma(m["const"][:, 0:896], a["k_rope"], self.slot["table"], self.const_read)
        cos, sin = m["const"][:, 0:S], m["const"][:, S:2 * S]
        rotate = m["const"][:, 512:640]
        dup, dup_rotate = m["const"][0:ROPE, 640:768], m["const"][0:ROPE, 768:896]
        tmp, work = m["tmp"], m["work"]
        cq = tmp[:, 0:768].rearrange("p (c t) -> p c t", c=3)
        ckv = tmp[:, 768:1280]
        lat = m["latent"]
        cq_hi, cq_lo = (lat[:, i * 768:(i + 1) * 768].rearrange("p (c t) -> p c t", c=3) for i in range(2))
        ckv_hi, ckv_lo = lat[:, 1536:2048], lat[:, 2048:2560]
        qn = work[:, 0:2048].rearrange("p (h t) -> p h t", h=8)
        qr = work[:, 2048:3072].rearrange("p (j t) -> p j t", j=4)
        kn = work[:, 3072:7168].rearrange("p (h t) -> p h t", h=8)
        kr = work[:, 7168:7680]
        v = work[:, 7680:11776].rearrange("p (t n) -> p t n", t=4)
        spare = work[:, 11776:12288]
        w_in = a["mla_w_in_2"][0]
        xq, xk = self.stage_in(0, S), self.stage_in(0, N)
        h_free, t_free = self.h_read, self.tmp_read
        ready = {}

        def keep_q(c, b, ps, mark):
            ready[c] = act.run(lambda e: e.activation(cq[:, c, :], ps[:, 0:S], ACT.Copy), mark, t_free)
            self.bank_free[b] = ready[c]

        def keep_kv(c, b, ps, mark):
            ready["kv"] = act.run(lambda e: e.activation(ckv, ps[:, 0:N], ACT.Copy), mark, t_free)
            self.bank_free[b] = ready["kv"]

        def keep_kr(c, b, ps, mark):
            ready["kr"] = act.run(lambda e: e.activation(kr[0:ROPE, :], ps[0:ROPE, 0:N], ACT.Copy), mark,
                                  h_free)
            self.bank_free[b] = ready["kr"]

        def latent_squares(chunks, at, n, marks):
            squares = [work[:, at + d * n:at + (d + 1) * n] for d in range(len(chunks))]
            return squares, [act.run(lambda e, q=q, c=c: e.activation(q, c, ACT.Square), mark, h_free)
                             for q, c, mark in zip(squares, chunks, marks)]

        def latent_sum(squares, marks, n):
            b, ps = self.bank()
            for d, (q, landed) in enumerate(zip(squares, marks)):
                pe.wait(landed)
                mark = self.mm(ps[:, 0:n], m["mean_w"][:, :], q, d == 0, d == len(squares) - 1,
                               mark=d == len(squares) - 1)
            return b, ps, mark

        def latent_norm(summed, chunks, n, width, gain, his, los):
            b, ps, mark = summed
            y, root = self.inv_root(b, ps, n, mark, D / width, RMS_EPS)
            for d, c in enumerate(chunks):
                g = m["cols"][:, gain + d:gain + d + 1]
                scaled = dve.run(lambda e, c=c, g=g: e.scalar_tensor_tensor(c, c, g, y, ALU.mult, ALU.mult),
                                 root, mark)
                high = act.run(lambda e, c=c, hi=his[d]: e.activation(hi, c, ACT.Copy), scaled, t_free)
                low = dve.run(lambda e, c=c, hi=his[d], lo=los[d]: e.tensor_tensor(
                    lo, c, hi.bitcast(F32), ALU.subtract), high, t_free)
            self.stat_read = [low]
            return low

        self.project(w_in[:, 0:256], 256, xq, S, keep_q)
        self.project(w_in[:, 256:384], 128, xq, S, lambda c, b, ps, mark: keep_q(2, b, ps, mark))
        q_chunks = [cq[:, c, :] for c in range(3)]
        q_squares = latent_squares(q_chunks, 7680, S, [ready[c] for c in range(3)])
        self.project(w_in[:, 384:512], 128, xk, N, keep_kv)
        kv_squares = latent_squares([ckv], 7680 + 3 * S, N, [ready["kv"]])
        q_ready = latent_norm(latent_sum(*q_squares, S), q_chunks, S, Q_RANK, self.col["mla_g_q_2"],
                              [cq_hi[:, c, :] for c in range(3)], [cq_lo[:, c, :] for c in range(3)])
        self.in_read = self.project(w_in[:, 512:576], 64, xk, N, keep_kr)
        kv_sum = latent_sum(*kv_squares, N)
        kv_ready = latent_norm(kv_sum, [ckv], N, P, self.col["mla_g_kv_2"], [ckv_hi], [ckv_lo])
        self.h_read = h_free = [h_free, kv_sum[2]]

        pe.wait(ready["kr"], tables)
        b1, both = self.bank()
        m1 = self.mm(both[:, 0:N], dup, kr[0:ROPE, :], mark=True)
        b2, other = self.bank()
        m2 = self.mm(other[:, 0:S], dup_rotate, kr[0:ROPE, 0:S], mark=True)
        r0 = dve.run(lambda e: e.tensor_tensor(spare[:, 0:S], other[:, 0:S], sin, ALU.mult), m2, h_free, tables)
        self.bank_free[b2] = r0
        r1 = dve.run(lambda e: e.tensor_copy(kr[:, S:N], both[:, S:N]), m1, m2)
        r2 = dve.run(lambda e: e.tensor_tensor(kr[:, 0:S], both[:, 0:S], cos, ALU.mult))
        self.bank_free[b1] = r2
        kr_done = dve.run(lambda e: e.tensor_tensor(kr[:, 0:S], kr[:, 0:S], spare[:, 0:S], ALU.add), r0, r2)

        w_uq = a["mla_w_uq_2"][0].rearrange("(k p) n -> p k n", p=P)
        pe.wait(q_ready)
        for j in range(MLA_HEADS // 2):
            cols = w_uq[:, :, j * 384:(j + 1) * 384]
            heads = [cols[:, k, :].rearrange("p (h c) -> p h c", h=2) for k in range(3)]
            unit, hi, lo = self.weights(cols, [(k * 384 + first, heads[k][:, :, c0:c1]) for k in range(3)
                                               for first, c0, c1 in ((0, 0, NOPE), (2 * NOPE, NOPE, 192))])
            for part in range(3):
                b, ps = self.bank()
                for k in range(3):
                    w = [t[:, k, part * P:(part + 1) * P] for t in (hi, lo)]
                    mark = self.mm3(ps[:, 0:S], w, (cq_hi[:, k, :], cq_lo[:, k, :]), k == 0, k == 2,
                                    mark=k == 2)
                if part < 2:
                    q_done = act.run(lambda e, o=qn[:, 2 * j + part, :], ps=ps: e.activation(
                        o, ps[:, 0:S], ACT.Copy), mark, h_free)
                    self.bank_free[b] = q_done
                else:
                    raw = spare[:, 0:S]
                    c1 = act.run(lambda e, ps=ps: e.activation(raw, ps[:, 0:S], ACT.Copy), mark, kr_done)
                    self.bank_free[b] = c1
                    pe.wait(c1)
                    b2, ps2 = self.bank()
                    rot = self.mm(ps2[:, 0:S], rotate, raw, mark=True)
                    o, t = qr[:, j, :], spare[:, S:2 * S]
                    d1 = dve.run(lambda e, t=t, ps2=ps2: e.tensor_tensor(t, ps2[:, 0:S], sin, ALU.mult), rot)
                    self.bank_free[b2] = d1
                    d2 = dve.run(lambda e, o=o: e.tensor_tensor(o, raw, cos, ALU.mult), c1)
                    kr_done = dve.run(lambda e, o=o, t=t: e.tensor_tensor(o, o, t, ALU.add), d1, d2)
            self.used[unit] = mark
        unit, hi, lo = self.weights(a["mla_w_uk_2"][0].rearrange("(k p) n -> p k n", p=P))
        pe.wait(kv_ready)
        for h in range(MLA_HEADS):
            b, ps = self.bank()
            w = [t[:, 0, h * P:(h + 1) * P] for t in (hi, lo)]
            mark = self.mm3(ps[:, 0:N], w, (ckv_hi, ckv_lo), True, True, mark=True)
            kn_done = act.run(lambda e, ps=ps, h=h: e.activation(kn[:, h, :], ps[:, 0:N], ACT.Copy), mark)
            self.bank_free[b] = kn_done
        self.used[unit] = mark
        v_done, mark = self.value_rows(a["mla_w_uv_2"][0], lambda k: (ckv_hi, ckv_lo), 4,
                                       lambda t: v[:, t, :])
        self.tmp_read = [mark, kv_ready, q_ready]
        rows = m["tmp"][:, 0:2048].rearrange("p (t n) -> p t n", t=2)
        pe.wait(q_done, kn_done, v_done, kr_done)
        items = []
        for t in range(2):
            for h in range(MLA_HEADS):
                r = (h % 2) * ROPE

                def scores(ps, h=h, r=r, t=t):
                    self.mm(ps[:, 0:N], qn[:, h, t * P:(t + 1) * P], kn[:, h, :], True, False)
                    return self.mm(ps[:, 0:N], qr[r:r + ROPE, h // 2, t * P:(t + 1) * P],
                                   kr[r:r + ROPE, :], False, True, mark=True)

                items.append(dict(
                    n=N, scores=scores, bias=None, scale=float((NOPE + ROPE) ** -0.5), width=P,
                    values=[v[:, k, h * P:(h + 1) * P] for k in range(4)],
                    o=rows[:, t, h * P:(h + 1) * P]))
        done, summed = self.attend(items)
        self.h_read = summed
        turned = self.turn_rows(lambda t: rows[:, t, :], 2, 0, DC, done)
        residual = self.add_gated(layer, 5, (0,))

        def add(d, b, ps, mark):
            self.bank_free[b] = residual(d, ps, mark)

        self.in_ready = turned
        self.in_read = self.project(a["mla_w_o_2"][0], D, self.stage_in(0, S), S, add)

    def finish(self):
        m, dve, act, pe = self.m, self.dve, self.act, self.pe
        b, ps, mark = self.norm_sum[0]
        y, root = self.inv_root(b, ps, S, mark, 1.0, RMS_EPS)
        g0 = self.col["final_g_2"]
        rows = m["work"][:, 0:2048].rearrange("p (t n) -> p t n", t=2)
        out = self.out.rearrange("b (t p) d -> p (b t) d", p=P)
        for d in range(DC):
            x, g = m["x"][:, d, 0:S], m["cols"][:, g0 + d:g0 + d + 1]
            n = dve.run(lambda e, x=x, g=g: e.scalar_tensor_tensor(x, x, g, y, ALU.mult, ALU.mult), root)
            pe.wait(n)
            b, ps = self.bank()
            for t in range(2):
                mark = self.transpose(ps[:, t * P:(t + 1) * P], x[:, t * P:(t + 1) * P], mark=t == 1)
            o = rows[:, :, d * P:(d + 1) * P]
            done = act.run(lambda e, o=o, ps=ps: e.activation(
                o, ps[:, 0:S].rearrange("p (t n) -> p t n", t=2), ACT.Copy), mark, self.h_read)
            self.bank_free[b] = done
        self.sync.wait(self.sync.dma(out, rows, self.slot["out"], done))

    def emit(self):
        a = self.a
        self.setup()
        both = (0, 1)
        for i in range(DEPTH):
            w = [a[f"ffn1_w_{k}"][i] for k in ("gate", "up", "down")]
            extra = None
            if i == 0:
                tok = self.m["tmp"][:, 2048:4096].rearrange("p (t d) -> p t d", t=2)
                extra = lambda: self.transpose_in(tok, self.context_landed, 1)
            self.norm_of("ln")
            self.ffn(*w, S, self.add_scaled(0), extra=extra, start=self.first_gate if i == 0 else None)
            self.layer_norm(i * 3, permuted=i == 1)
            if i == 0:
                self.pool_mixer()
            else:
                self.load_rpb()
                self.dilated_mixer()
                self.const_read = self.dve_mark()
            self.layer_norm(i * 3 + 1)
            w = [a[f"ffn2_w_{k}"][i] for k in ("gate", "up", "down")]
            self.ffn(*w, S, self.add_scaled(0),
                     in_down=self.first_context_norm() if i == DEPTH - 1 else None)
            if i < DEPTH - 1:
                self.layer_norm(i * 3 + 2)
        self.ada_period = 2
        for layer in range(DEPTH):
            last = layer == DEPTH - 1
            w = [a[f"ffn_w_{k}_2"][layer, 0] for k in ("gate", "up", "down")]
            self.norm_of("rms", both, self.rms_both(layer, 1, 3, 4))
            self.ffn(*w, 2 * S, self.add_gated(layer, 2, both),
                     start=self.first_products if layer == 0 else None)
            if last:
                self.norm_of("rms")
                self.mla_mixer(layer)
                self.rms_mod(layer, 2, 6, 7)
                self.norm_of("rms")
            else:
                self.norm_of("rms", both, self.rms_both(layer, 2, 6, 7))
                self.fourier_na_mixer(layer)
                self.const_read = [self.h_read, self.dve_mark()]
                self.norm_of("rms", both, self.rms_both(layer + 1, 0, 0, 1))
            streams = (0,) if last else both
            w = [a[f"ffn_w_{k}_2"][layer, 1] for k in ("gate", "up", "down")]
            self.ffn(*w, S * len(streams), self.add_gated(layer, 8, streams))
        self.finish()

    def first_context_norm(self):
        assert self.ada_halves[0] >= (0, 4, 0)
        norm, self.norm = self.norm, ("rms", (0, 1), None)
        for d in range(DC):
            self.feed_norm(d, (1,))
        self.norm = norm
        yield
        yield
        self.mean_of(1, self.m["tmp"][:, S:2 * S])
        self.rms_mod(0, 0, 0, 1, s=1, silu_next=False)

    def first_products(self, gate, up):
        norm = self.norm
        latents, context = self.stage_in(0, S), self.stage_in(S, S)
        units, banks, products = [], [], []

        def context_product(w, ahead):
            units.append(self.weights(w, ahead=ahead))
            banks.append(self.open_banks(2 * P))
            self.accumulate(*units[-1][1:], banks[-1], DC, context, S, S)

        context_product(gate, 2)
        self.load_mixer_tables()
        self.norm_of("rms")
        self.layer_norm(DEPTH * 3 - 1, split=False, meanwhile=lambda: context_product(up, 1))
        self.rms_mod(0, 0, 0, 1)
        self.split_until(self.taken + 1)
        for (unit, hi, lo), taken in zip(units, banks):
            marks = self.accumulate(hi, lo, taken, DC, latents, 0, S)
            self.used[unit] = marks[-1]
            self.split_until(self.taken + 1 + len(products))
            products.append([(t[2], t[3], mark) for t, mark in zip(taken, marks)])
        self.norm = norm
        return products

    def dve_mark(self):
        return (self.dve.sem, self.dve.count)


def tables():
    f32 = np.float32
    t = np.arange(S)
    inverse = []
    for w in (2, 4, 8, 16):
        lo, hi = np.clip(t - w // 2, 0, S), np.clip(t + w // 2, 0, S)
        inverse.append(1.0 / (hi - lo))
    inverse = np.broadcast_to(np.concatenate(inverse)[None], (P, 4 * S))
    order = np.array([c * 16 + b * 4 + a for a in range(4) for b in range(4) for c in range(16)])
    dist = np.abs(order[:, None] - order[None, :]).astype(np.float64)
    same = lambda n: order[:, None] % n == order[None, :] % n
    d0 = np.where(dist <= 64, dist, FAR)
    d1, d2 = (np.where(same(n), dist, FAR) for n in (4, 16))
    tiles = []
    for i in range(2):
        r = slice(i * P, (i + 1) * P)
        tiles.append(np.concatenate([d0[r], d1[r, r], d2[r, r]], axis=1))
    block1 = np.concatenate([inverse] + tiles, axis=1).astype(f32)
    ang = 2 * np.pi * np.outer(np.arange(P), np.arange(P)) / P
    dft_d = np.concatenate([np.cos(ang), np.sin(ang)], axis=1) / np.sqrt(P)
    ang = 2 * np.pi * (np.outer(np.arange(S), np.arange(S)) % S) / S
    dft_n = np.stack([np.cos(ang), -np.sin(ang)], axis=1) / np.sqrt(S)
    dft_n = dft_n.reshape(2, P, 2, S).transpose(1, 0, 2, 3).reshape(P, 4 * S)
    col = t % GRID_W
    start = np.clip(col - 8, 0, GRID_W - 16)
    seen = (col[None, :] >= start[:, None]) & (col[None, :] < start[:, None] + 16)
    mask = np.where(seen, 0.0, -1e30).reshape(2, P, S).transpose(1, 0, 2).reshape(P, 2 * S)
    mixer = np.concatenate([dft_d, dft_n, mask], axis=1).astype(f32)
    inv = (10000.0 ** (-np.arange(0, 32, 2, dtype=f32) / f32(32))).astype(f32)
    row, colf = (t // GRID_W).astype(f32), (t % GRID_W).astype(f32)
    ar, ac = row[:, None] * inv[None], colf[:, None] * inv[None]
    angle = np.concatenate([ar, ar, ac, ac], axis=1)
    cos, sin = (np.concatenate([f(angle).T] * 2, axis=0) for f in (np.cos, np.sin))
    rot = np.zeros((ROPE, ROPE))
    for i in range(16):
        rot[16 + i, i] = rot[48 + i, 32 + i] = -1.0
        rot[i, 16 + i] = rot[32 + i, 48 + i] = 1.0
    rot2 = np.zeros((P, P))
    rot2[:ROPE, :ROPE] = rot2[ROPE:, ROPE:] = rot
    dup = np.zeros((P, 2 * P))
    dup[:ROPE] = np.concatenate([np.eye(ROPE), np.eye(ROPE), rot, rot], axis=1)
    rope = np.concatenate([cos, sin, rot2, dup], axis=1).astype(f32)
    return {"k_ident": np.eye(P, dtype=f32), "k_block1": block1, "k_mixer": mixer, "k_rope": rope}


NAMES = ["x", "ffn1_w_gate", "ffn1_w_up", "ffn1_w_down", "ffn2_w_gate", "ffn2_w_up", "ffn2_w_down",
         "ln_gain", "ln_bias", "pool_w_in", "pool_w_group", "pool_scale", "pool_w_out", "attn_w_qkv",
         "attn_w_out", "c_2", "ctx_2", "c_ctx_2", "ada_w_2", "ada_b_2", "norm_g_2", "ffn_w_gate_2",
         "ffn_w_up_2", "ffn_w_down_2", "ab_w_in_2", "ab_rpb_2", "ab_w_out_2", "mla_w_in_2", "mla_g_q_2",
         "mla_g_kv_2", "mla_w_uq_2", "mla_w_uk_2", "mla_w_uv_2", "mla_w_o_2", "final_g_2"]
IN_ROWS = ["ln_gain", "ln_bias", "norm_g_2", "pool_scale", "final_g_2", "mla_g_q_2", "mla_g_kv_2", "c_2",
           "c_ctx_2"]


def as_rows(ap):
    n = int(np.prod(ap.shape))
    return bass.AP(ap.tensor, 0, [[P, n // P], [1, P]])


def build(nc, shapes):
    a = {name: nc.dram_tensor(f"in_{name}", shape, F32, kind="ExternalInput").ap()
         for name, shape in shapes.items()}
    out = nc.dram_tensor("out_0", (1, S, D), F32, kind="ExternalOutput").ap()
    a["scratch"] = nc.dram_tensor("rpb_rows", (NA_HEADS * RPB_H, GRID_W, P), F32, kind="Internal").ap()
    for name in IN_ROWS:
        a[name] = as_rows(a[name])
    ada_b = as_rows(a["ada_b_2"])
    for layer in range(DEPTH):
        a[f"ada_b_2.{layer}"] = ada_b[layer * MODC:(layer + 1) * MODC, :]
    build_program(nc, a, out)
    return "out_0"


def kernel(**inputs):
    import concourse.bacc as bacc
    from concourse.bass_utils import run_bass_kernel_spmd

    nc = bacc.Bacc("TRN2", target_bir_lowering=False, num_devices=1,
                   dynamic_dma_scratch_size=1024)
    arrays = {name: np.ascontiguousarray(inputs[name]) for name in NAMES}
    arrays.update(tables())
    result = build(nc, {name: v.shape for name, v in arrays.items()})
    r = run_bass_kernel_spmd(nc, [{f"in_{n}": v for n, v in arrays.items()}], core_ids=[0])
    return r.results[0][result]
```
